# Optimizing a Trainium2 kernel written in Bass

```python
import jax, jax.numpy as jnp
from jax import lax
import numpy as np

D_MODEL = 1024
BATCH = 1
SEQ = 512
DEPTH = 1

HEAD_DIM = 64
D_MIX = D_MODEL
GDN_HEADS = (D_MIX // 2) // HEAD_DIM
GDN_WIDTH = GDN_HEADS * HEAD_DIM
SWA_Q_HEADS = (D_MIX - GDN_WIDTH) // HEAD_DIM
SWA_KV_HEADS = 2
SWA_GROUP = SWA_Q_HEADS // SWA_KV_HEADS
SWA_WIDTH = SWA_Q_HEADS * HEAD_DIM
SWA_KV_WIDTH = SWA_KV_HEADS * HEAD_DIM
WINDOW = 128
CONV_WIDTH = 4
CHUNK = 64
D_FF = ((8 * D_MODEL // 3 + 255) // 256) * 256
PROJ_WIDTH = 4 * GDN_WIDTH + 2 * GDN_HEADS + SWA_WIDTH + 2 * SWA_KV_WIDTH
EPS = 1e-6


def rms_norm(x, w):
    xf = x.astype(jnp.float32)
    y = xf * lax.rsqrt(jnp.mean(xf * xf, axis=-1, keepdims=True) + EPS)
    return (y * w.astype(jnp.float32)).astype(x.dtype)

def l2_norm(x):
    xf = x.astype(jnp.float32)
    return xf * lax.rsqrt(jnp.sum(xf * xf, axis=-1, keepdims=True) + EPS)

def causal_depthwise_conv(x, w):
    return lax.conv_general_dilated(
        x, w.astype(x.dtype), window_strides=(1,), padding=[(CONV_WIDTH - 1, 0)],
        dimension_numbers=('NWC', 'WIO', 'NWC'), feature_group_count=x.shape[-1])

def gated_delta_rule_chunked(q, k, v, g, beta):
    B, T, H, Dk = q.shape
    Dv = v.shape[-1]
    N = T // CHUNK

    def chunks(t):
        t = t.reshape((B, N, CHUNK, H) + t.shape[3:])
        return jnp.moveaxis(t, 3, 1)

    q = chunks(q) * (Dk ** -0.5)
    k, v, g, beta = chunks(k), chunks(v), chunks(g), chunks(beta)
    G = jnp.cumsum(g, axis=-1)
    idx = jnp.arange(CHUNK)
    causal = idx[:, None] >= idx[None, :]
    strict = idx[:, None] > idx[None, :]
    decay = jnp.exp(jnp.where(causal, G[..., :, None] - G[..., None, :], -jnp.inf))
    kb = k * beta[..., None]
    A = jnp.where(strict, jnp.einsum('bhncd,bhnsd->bhncs', kb, k) * decay, 0.0)
    L = A + jnp.eye(CHUNK, dtype=A.dtype)
    rhs = jnp.concatenate([v * beta[..., None], kb * jnp.exp(G)[..., None]], axis=-1)
    sol = lax.linalg.triangular_solve(L, rhs, left_side=True, lower=True, unit_diagonal=True)
    u, w = sol[..., :Dv], sol[..., Dv:]
    qk = jnp.where(causal, jnp.einsum('bhncd,bhnsd->bhncs', q, k) * decay, 0.0)
    q_dec = q * jnp.exp(G)[..., None]
    k_dec = k * jnp.exp(G[..., -1:] - G)[..., None]
    chunk_decay = jnp.exp(G[..., -1])

    xs = tuple(jnp.moveaxis(t, 2, 0) for t in (u, w, qk, q_dec, k_dec, chunk_decay))

    def step(S, inp):
        u_c, w_c, qk_c, qd_c, kd_c, dec_c = inp
        v_new = u_c - jnp.einsum('bhcd,bhde->bhce', w_c, S)
        o = jnp.einsum('bhcd,bhde->bhce', qd_c, S) + jnp.einsum('bhcs,bhse->bhce', qk_c, v_new)
        S = S * dec_c[..., None, None] + jnp.einsum('bhcd,bhce->bhde', kd_c, v_new)
        return S, o

    S0 = jnp.zeros((B, H, Dk, Dv), jnp.float32)
    _, o = lax.scan(step, S0, xs)
    return jnp.transpose(o, (1, 0, 3, 2, 4)).reshape(B, T, H, Dv)

def sliding_window_attention(q, k, v, sinks):
    B, T, Hq, D = q.shape
    NB = T // WINDOW
    qb = q.reshape(B, NB, WINDOW, SWA_KV_HEADS, SWA_GROUP, D)

    def banded(t):
        t = t.reshape(B, NB, WINDOW, SWA_KV_HEADS, D)
        prev = jnp.pad(t, ((0, 0), (1, 0), (0, 0), (0, 0), (0, 0)))[:, :-1]
        return jnp.concatenate([prev, t], axis=2)

    kw, vw = banded(k), banded(v)
    s = jnp.einsum('bnqhgd,bnkhd->bhgnqk', qb, kw).astype(jnp.float32) * (D ** -0.5)
    qi = jnp.arange(WINDOW)[:, None] + WINDOW
    ki = jnp.arange(2 * WINDOW)[None, :]
    dist = (qi - ki).astype(jnp.float32)
    in_window = (qi - ki >= 0) & (qi - ki < WINDOW)
    key_exists = (jnp.arange(NB)[:, None] * WINDOW + ki - WINDOW) >= 0
    mask = in_window[None] & key_exists[:, None, :]
    slopes = 2.0 ** (-8.0 * (jnp.arange(Hq, dtype=jnp.float32) + 1.0) / Hq)
    slopes = slopes.reshape(SWA_KV_HEADS, SWA_GROUP)
    s = s - slopes[:, :, None, None, None] * dist
    s = jnp.where(mask, s, -jnp.inf)
    sink = sinks.astype(jnp.float32).reshape(SWA_KV_HEADS, SWA_GROUP)[None, :, :, None, None, None]
    m = jnp.maximum(jnp.max(s, axis=-1, keepdims=True), sink)
    p = jnp.exp(s - m)
    p = p / (jnp.sum(p, axis=-1, keepdims=True) + jnp.exp(sink - m))
    o = jnp.einsum('bhgnqk,bnkhd->bnqhgd', p.astype(v.dtype), vw)
    return o.reshape(B, T, Hq * D)

def first_inputs(seed: int = 0) -> dict:
    key = jax.random.key(seed)
    ks = jax.random.split(key, 20)
    f32 = jnp.float32
    nrm = lambda k, shape, scale: jax.random.normal(k, shape, f32) * scale
    gain = lambda k, shape: 1.0 + 0.1 * jax.random.normal(k, shape, f32)
    a_init = jax.random.uniform(ks[6], (DEPTH, GDN_HEADS), f32, 1.0, 16.0)
    dt = jnp.exp(jax.random.uniform(ks[7], (DEPTH, GDN_HEADS), f32, np.log(1e-3), np.log(1e-1)))
    return {
        'x': nrm(ks[0], (BATCH, SEQ, D_MODEL), 1.0),
        'c': nrm(ks[1], (BATCH, D_MODEL), 1.0),
        'w_ada': nrm(ks[2], (DEPTH, D_MODEL, 6 * D_MODEL), D_MODEL ** -0.5),
        'b_ada': nrm(ks[3], (DEPTH, 6 * D_MODEL), 0.1),
        'norm1_w': gain(ks[4], (DEPTH, D_MODEL)),
        'w_in': nrm(ks[5], (DEPTH, D_MODEL, PROJ_WIDTH), D_MODEL ** -0.5),
        'conv_w': nrm(ks[8], (DEPTH, CONV_WIDTH, 1, 3 * GDN_WIDTH), CONV_WIDTH ** -0.5),
        'a_log': jnp.log(a_init),
        'dt_bias': dt + jnp.log(-jnp.expm1(-dt)),
        'gdn_norm_w': gain(ks[9], (DEPTH, HEAD_DIM)),
        'q_norm_w': gain(ks[10], (DEPTH, HEAD_DIM)),
        'k_norm_w': gain(ks[11], (DEPTH, HEAD_DIM)),
        'sinks': nrm(ks[12], (DEPTH, SWA_Q_HEADS), 1.0),
        'w_out': nrm(ks[13], (DEPTH, D_MIX, D_MODEL), D_MIX ** -0.5),
        'norm2_w': gain(ks[14], (DEPTH, D_MODEL)),
        'w_gate': nrm(ks[15], (DEPTH, D_MODEL, D_FF), D_MODEL ** -0.5),
        'w_up': nrm(ks[16], (DEPTH, D_MODEL, D_FF), D_MODEL ** -0.5),
        'w_down': nrm(ks[17], (DEPTH, D_FF, D_MODEL), D_FF ** -0.5),
    }

def first_block(x, c, w_ada, b_ada, norm1_w, w_in, conv_w, a_log, dt_bias, gdn_norm_w,
              q_norm_w, k_norm_w, sinks, w_out, norm2_w, w_gate, w_up, w_down):
    B, T, _ = x.shape
    split_sizes = (GDN_WIDTH,) * 4 + (GDN_HEADS,) * 2 + (SWA_WIDTH, SWA_KV_WIDTH, SWA_KV_WIDTH)
    split_points = []
    acc = 0
    for sz in split_sizes[:-1]:
        acc += sz
        split_points.append(acc)
    c_act = jax.nn.silu(c)
    for l in range(DEPTH):
        mod = (c_act @ w_ada[l] + b_ada[l])[:, None, :]
        shift1, scale1, gate1, shift2, scale2, gate2 = jnp.split(mod, 6, axis=-1)

        h = rms_norm(x, norm1_w[l]) * (1.0 + scale1) + shift1
        proj = h @ w_in[l]
        gq, gk, gv, gz, ga, gb, sq, sk, sv = jnp.split(proj, split_points, axis=-1)

        qkv = jax.nn.silu(causal_depthwise_conv(jnp.concatenate([gq, gk, gv], axis=-1), conv_w[l]))
        gq, gk, gv = jnp.split(qkv, 3, axis=-1)
        heads = lambda t: t.reshape(B, T, -1, HEAD_DIM)
        q_g = l2_norm(heads(gq))
        k_g = l2_norm(heads(gk))
        v_g = heads(gv).astype(jnp.float32)
        beta = jax.nn.sigmoid(gb.astype(jnp.float32))
        g = -jnp.exp(a_log[l].astype(jnp.float32)) * jax.nn.softplus(
            ga.astype(jnp.float32) + dt_bias[l].astype(jnp.float32))
        o_g = gated_delta_rule_chunked(q_g, k_g, v_g, g, beta).astype(x.dtype)
        o_g = rms_norm(o_g, gdn_norm_w[l]) * jax.nn.silu(heads(gz))
        o_g = o_g.reshape(B, T, GDN_WIDTH)

        q_s = rms_norm(heads(sq), q_norm_w[l])
        k_s = rms_norm(heads(sk), k_norm_w[l])
        v_s = heads(sv)
        o_s = sliding_window_attention(q_s, k_s, v_s, sinks[l])

        mixed = jnp.concatenate([o_g, o_s], axis=-1) @ w_out[l]
        x = x + gate1 * mixed

        h2 = rms_norm(x, norm2_w[l]) * (1.0 + scale2) + shift2
        ffn = (jax.nn.silu(h2 @ w_gate[l]) * (h2 @ w_up[l])) @ w_down[l]
        x = x + gate2 * ffn
    return x


N_META = 16
N_BRANCH = 4
POOL_WINDOWS = (2, 4, 8, 16)
POOL_GROUP = 64
POOL_W = POOL_GROUP * 4
MLA_HEADS = 8
QK_NOPE = 64
QK_ROPE = 32
V_DIM = 64
Q_RANK = 256
KV_RANK = 128
ROPE_THETA = 10000.0
MLA_W = MLA_HEADS * V_DIM
Q_BLOCK = 128
CONF_W = 256
CONF_K = 31
SC_W = 256
SC_K = 3

IN_SPLITS = (POOL_W, POOL_W,
             Q_RANK, KV_RANK, QK_ROPE, MLA_W,
             2 * CONF_W, CONF_W,
             3 * SC_W, SC_W,
             N_BRANCH * D_MODEL)
IN_W = sum(IN_SPLITS)


def rms_norm_2(x, g):
    xf = x.astype(jnp.float32)
    y = xf * lax.rsqrt(jnp.mean(xf * xf, axis=-1, keepdims=True) + EPS)
    return (y * g.astype(jnp.float32)).astype(x.dtype)

def layer_norm(x, g, b):
    xf = x.astype(jnp.float32)
    mu = jnp.mean(xf, axis=-1, keepdims=True)
    var = jnp.mean(jnp.square(xf - mu), axis=-1, keepdims=True)
    y = (xf - mu) * lax.rsqrt(var + EPS)
    return (y * g.astype(jnp.float32) + b.astype(jnp.float32)).astype(x.dtype)

def split_cols(z):
    idx = [int(i) for i in np.cumsum(IN_SPLITS)[:-1]]
    return jnp.split(z, idx, axis=-1)

def causal_dwconv(u, w):
    width, c = w.shape
    up = jnp.pad(u, ((0, 0), (width - 1, 0), (0, 0)))
    return lax.conv_general_dilated(up, w[:, None, :].astype(u.dtype), window_strides=(1,),
                                    padding='VALID', dimension_numbers=('NWC', 'WIO', 'NWC'),
                                    feature_group_count=c)

def rope_tables(n_pos, dim, dtype):
    inv = 1.0 / (ROPE_THETA ** (jnp.arange(0, dim, 2, dtype=jnp.float32) / dim))
    ang = jnp.arange(n_pos, dtype=jnp.float32)[:, None] * inv[None, :]
    return jnp.cos(ang).astype(dtype), jnp.sin(ang).astype(dtype)

def apply_rope(t, cos, sin):
    t1, t2 = jnp.split(t, 2, axis=-1)
    return jnp.concatenate([t1 * cos - t2 * sin, t1 * sin + t2 * cos], axis=-1)

def pool_mixer(v, w_group, scale):
    b_, l_, _ = v.shape
    vf = v.astype(jnp.float32)
    groups = jnp.split(vf, len(POOL_WINDOWS), axis=-1)
    pos = jnp.arange(l_)
    outs = []
    for g, w in zip(groups, POOL_WINDOWS):
        cs = jnp.cumsum(g, axis=1)
        lag = jnp.pad(cs, ((0, 0), (w, 0), (0, 0)))[:, :l_]
        cnt = jnp.minimum(pos + 1, w).astype(jnp.float32)[None, :, None]
        outs.append((cs - lag) / cnt - g)
    p = jnp.stack(outs, axis=2).astype(v.dtype)
    y = jnp.einsum('blgc,gcd->blgd', p, w_group).reshape(b_, l_, POOL_W)
    return y * scale

def mla_attention(c_q, c_kv, k_rope, q_norm_g, w_uq, kv_norm_g, w_ukv, cos, sin):
    b_, l_, _ = c_q.shape
    q = (rms_norm_2(c_q, q_norm_g) @ w_uq).reshape(b_, l_, MLA_HEADS, QK_NOPE + QK_ROPE)
    q_nope, q_rope = jnp.split(q, [QK_NOPE], axis=-1)
    q_rope = apply_rope(q_rope, cos[:, None, :], sin[:, None, :])
    kv = (rms_norm_2(c_kv, kv_norm_g) @ w_ukv).reshape(b_, l_, MLA_HEADS, QK_NOPE + V_DIM)
    k_nope, v = jnp.split(kv, [QK_NOPE], axis=-1)
    k_rope = apply_rope(k_rope, cos, sin)
    k = jnp.concatenate([k_nope, jnp.broadcast_to(k_rope[:, :, None, :], (b_, l_, MLA_HEADS, QK_ROPE))], axis=-1)
    qf = jnp.concatenate([q_nope, q_rope], axis=-1) * ((QK_NOPE + QK_ROPE) ** -0.5)
    n_blk = -(-l_ // Q_BLOCK)
    lp = n_blk * Q_BLOCK
    pad = ((0, 0), (0, lp - l_), (0, 0), (0, 0))
    qf, k, v = jnp.pad(qf, pad), jnp.pad(k, pad), jnp.pad(v, pad)
    k_pos = jnp.arange(lp)
    q_blocks = qf.reshape(b_, n_blk, Q_BLOCK, MLA_HEADS, QK_NOPE + QK_ROPE).transpose(1, 0, 2, 3, 4)

    def attend(args):
        qb, i = args
        s = jnp.einsum('bqhd,bkhd->bhqk', qb, k).astype(jnp.float32)
        q_pos = i * Q_BLOCK + jnp.arange(Q_BLOCK)
        s = jnp.where(k_pos[None, :] <= q_pos[:, None], s, -jnp.inf)
        p = jax.nn.softmax(s, axis=-1).astype(v.dtype)
        return jnp.einsum('bhqk,bkhd->bqhd', p, v)

    o = lax.map(attend, (q_blocks, jnp.arange(n_blk)))
    return o.transpose(1, 0, 2, 3, 4).reshape(b_, lp, MLA_W)[:, :l_]

def conformer_conv(u, w_dw, b_dw, ln_g, ln_b):
    a, gate = jnp.split(u, 2, axis=-1)
    z = a * jax.nn.sigmoid(gate)
    z = causal_dwconv(z, w_dw) + b_dw
    z = layer_norm(z, ln_g, ln_b)
    return jax.nn.silu(z)

def short_conv(bcx, w_dw):
    bg, cg, xv = jnp.split(bcx, 3, axis=-1)
    return bg * causal_dwconv(cg * xv, w_dw)

def second_inputs(seed: int = 0) -> dict:
    key = jax.random.key(seed)
    ks = jax.random.split(key, 24)
    f32 = jnp.float32

    def nrm(k, shape, fan_in):
        return jax.random.normal(k, shape, f32) * (fan_in ** -0.5)

    def gain(k, shape):
        return 1.0 + 0.05 * jax.random.normal(k, shape, f32)

    def bias(k, shape):
        return 0.02 * jax.random.normal(k, shape, f32)

    return {
        "x": jax.random.normal(ks[0], (BATCH, SEQ, D_MODEL), f32),
        "meta_tokens": jax.random.normal(ks[1], (N_META, D_MODEL), f32),
        "pre_norm_g": gain(ks[2], (DEPTH, D_MODEL)),
        "w_in": nrm(ks[3], (DEPTH, D_MODEL, IN_W), D_MODEL),
        "gate_bias": bias(ks[4], (DEPTH, N_BRANCH * D_MODEL)),
        "pool_w": nrm(ks[5], (DEPTH, 4, POOL_GROUP, POOL_GROUP), POOL_GROUP),
        "pool_scale": gain(ks[6], (DEPTH, POOL_W)),
        "w_out_pool": nrm(ks[7], (DEPTH, POOL_W, D_MODEL), POOL_W),
        "q_norm_g": gain(ks[8], (DEPTH, Q_RANK)),
        "w_uq": nrm(ks[9], (DEPTH, Q_RANK, MLA_HEADS * (QK_NOPE + QK_ROPE)), Q_RANK),
        "kv_norm_g": gain(ks[10], (DEPTH, KV_RANK)),
        "w_ukv": nrm(ks[11], (DEPTH, KV_RANK, MLA_HEADS * (QK_NOPE + V_DIM)), KV_RANK),
        "w_out_mla": nrm(ks[12], (DEPTH, MLA_W, D_MODEL), MLA_W),
        "conf_dw_w": nrm(ks[13], (DEPTH, CONF_K, CONF_W), CONF_K),
        "conf_dw_b": bias(ks[14], (DEPTH, CONF_W)),
        "conf_ln_g": gain(ks[15], (DEPTH, CONF_W)),
        "conf_ln_b": bias(ks[16], (DEPTH, CONF_W)),
        "w_out_conf": nrm(ks[17], (DEPTH, CONF_W, D_MODEL), CONF_W),
        "sc_dw_w": nrm(ks[18], (DEPTH, SC_K, SC_W), SC_K),
        "w_out_sc": nrm(ks[19], (DEPTH, SC_W, D_MODEL), SC_W),
        "w_o": nrm(ks[20], (DEPTH, D_MODEL, D_MODEL), D_MODEL),
        "post_norm_g": gain(ks[21], (DEPTH, D_MODEL)),
    }

def second_block(x, meta_tokens, pre_norm_g, w_in, gate_bias, pool_w, pool_scale, w_out_pool,
              q_norm_g, w_uq, kv_norm_g, w_ukv, w_out_mla, conf_dw_w, conf_dw_b, conf_ln_g,
              conf_ln_b, w_out_conf, sc_dw_w, w_out_sc, w_o, post_norm_g):
    b_ = x.shape[0]
    meta = jnp.broadcast_to(meta_tokens[None].astype(x.dtype), (b_, N_META, D_MODEL))
    h_res = jnp.concatenate([meta, x], axis=1)
    l_ = h_res.shape[1]
    cos, sin = rope_tables(l_, QK_ROPE, x.dtype)

    for i in range(DEPTH):
        h = rms_norm_2(h_res, pre_norm_g[i])
        z = h @ w_in[i]
        (pv, pg, cq, ckv, kr, mg, cu, cg, sbcx, sg, gl) = split_cols(z)

        y_a = (pool_mixer(pv, pool_w[i], pool_scale[i]) * jax.nn.silu(pg)) @ w_out_pool[i]
        y_b = (mla_attention(cq, ckv, kr, q_norm_g[i], w_uq[i], kv_norm_g[i], w_ukv[i], cos, sin)
               * jax.nn.silu(mg)) @ w_out_mla[i]
        y_c = (conformer_conv(cu, conf_dw_w[i], conf_dw_b[i], conf_ln_g[i], conf_ln_b[i])
               * jax.nn.silu(cg)) @ w_out_conf[i]
        y_d = (short_conv(sbcx, sc_dw_w[i]) * jax.nn.silu(sg)) @ w_out_sc[i]

        gts = jax.nn.sigmoid(gl + gate_bias[i]).reshape(b_, l_, N_BRANCH, D_MODEL)
        m = (gts[:, :, 0] * y_a + gts[:, :, 1] * y_b + gts[:, :, 2] * y_c + gts[:, :, 3] * y_d)
        h_res = h_res + rms_norm_2(m @ w_o[i], post_norm_g[i])

    return h_res[:, N_META:]


def setup_inputs(seed=0):
    out = dict(first_inputs(seed))
    for name, value in second_inputs(seed + 1).items():
        if name != "x":
            out[name + "_2"] = value
    return out


def reference(
    x, c, w_ada, b_ada, norm1_w, w_in, conv_w, a_log, dt_bias, gdn_norm_w, q_norm_w, k_norm_w,
    sinks, w_out, norm2_w, w_gate, w_up, w_down, meta_tokens_2, pre_norm_g_2, w_in_2,
    gate_bias_2, pool_w_2, pool_scale_2, w_out_pool_2, q_norm_g_2, w_uq_2, kv_norm_g_2, w_ukv_2,
    w_out_mla_2, conf_dw_w_2, conf_dw_b_2, conf_ln_g_2, conf_ln_b_2, w_out_conf_2, sc_dw_w_2,
    w_out_sc_2, w_o_2, post_norm_g_2,
):
    x = first_block(
        x, c, w_ada, b_ada, norm1_w, w_in, conv_w, a_log, dt_bias, gdn_norm_w, q_norm_w,
        k_norm_w, sinks, w_out, norm2_w, w_gate, w_up, w_down,
    )
    return second_block(
        x, meta_tokens_2, pre_norm_g_2, w_in_2, gate_bias_2, pool_w_2, pool_scale_2,
        w_out_pool_2, q_norm_g_2, w_uq_2, kv_norm_g_2, w_ukv_2, w_out_mla_2, conf_dw_w_2,
        conf_dw_b_2, conf_ln_g_2, conf_ln_b_2, w_out_conf_2, sc_dw_w_2, w_out_sc_2, w_o_2,
        post_norm_g_2,
    )


_drawn_inputs = setup_inputs


def setup_inputs(seed=0):
    import zlib

    import numpy as np

    out = dict(_drawn_inputs(seed))
    spreads = {}
    factors = {'q_norm_w': 3.929,
     'k_norm_w': 4.373,
     'gate_bias_2': 8.0,
     'pool_scale_2': 19.297,
     'q_norm_g_2': 8.0,
     'kv_norm_g_2': 8.0,
     'conf_dw_b_2': 6.435,
     'conf_ln_g_2': 23.499,
     'conf_ln_b_2': 50.204,
     'sinks': 4.001}
    for name, (base, spread) in spreads.items():
        noise = np.random.default_rng([zlib.crc32(name.encode()), seed]).standard_normal(out[name].shape)
        drawn = base * np.exp(spread * noise) if base else spread * noise
        out[name] = __import__('jax').numpy.asarray(drawn.astype(out[name].dtype))
    for name, factor in factors.items():
        out[name] = (out[name] * factor).astype(out[name].dtype)
    return out
```

```python
from contextlib import ExitStack

import numpy as np

import concourse.bass as bass
from concourse import mybir

F32 = mybir.dt.float32
ALU = mybir.AluOpType
ACT = mybir.ActivationFunctionType
AX = mybir.AxisListType

P = 128
D = 1024
KD = D // P
T = 512
META = 16
TM = T + META
HD = 64
GH = 8
NJ = GH // 2
CH = 64
NC = T // CH
WIN = 128
NB = T // WIN
FF = 2816
KF = FF // P
EPS = 1e-6
QK_NOPE, QK_ROPE, V_DIM = 64, 32, 64
QD = QK_NOPE + QK_ROPE
CONF_K = 31
SC_K = 3
NEG = -1e30

CONST_W = {}
_at = 0
for _name, _w in (("ident", 128), ("ones", 128), ("onesbd", 128), ("m16", 128), ("m16T", 128), ("m32", 128),
                  ("m64", 128), ("strictT", 64), ("inclT", 64), ("stack", 64), ("sel", 512), ("pick", 4 * 40 * 2),
                  ("two", 2), ("reset", 512), ("invw", 2), ("causal", 128)):
    CONST_W[_name] = (_at, _w)
    _at += _w
CONST_COLS = _at

V1_ROWS = {"b_ada": 0, "norm1": 48, "norm2": 56, "pre": 64, "gate_bias": 72, "conf_b": 104, "ln_g": 106,
           "ln_b": 108, "pool_scale": 110, "q_norm": 112, "kv_norm": 114, "gdn_norm": 115, "qn": 116, "kn": 117,
           "c": 118}
V1_N = 126
V2_ROWS = {"conv": 0, "conf": 48, "sc": 110}
V2_N = 116


def shape_constants():
    c = np.zeros((P, CONST_COLS), np.float32)

    def put(name, a):
        o, w = CONST_W[name]
        c[:a.shape[0], o:o + w] = a.reshape(a.shape[0], -1)

    r = np.arange(P)
    head, tok = r // 64, r % 64
    same = head[:, None] == head[None, :]
    lower = tok[:, None] > tok[None, :]
    b16 = tok[:, None] // 16 == tok[None, :] // 16
    b32 = tok[:, None] // 32 == tok[None, :] // 32
    put("ident", np.eye(P))
    put("ones", np.ones((P, P)))
    put("onesbd", same)
    put("m16", same & lower & b16)
    put("m16T", (same & lower & b16).T)
    put("m32", same & lower & b32 & ~b16)
    put("m64", same & lower & ~b32)
    t = np.arange(64)
    put("strictT", t[None, :] > tok[:, None])
    put("inclT", t[None, :] >= tok[:, None])
    put("stack", t[None, :] == tok[:, None])
    sel = np.zeros((40, NJ, P))
    pick = np.zeros((P, 2, NJ, 40))
    for j in range(NJ):
        for h in (0, 1):
            sel[2 * j + h, j, 64 * h:64 * h + 64] = 1
            sel[32 + 2 * j + h, j, 64 * h:64 * h + 64] = 1
            pick[64 * h:64 * h + 64, 0, j, 2 * j + h] = 1
            pick[64 * h:64 * h + 64, 1, j, 32 + 2 * j + h] = 1
    put("sel", sel)
    put("pick", pick)
    two = np.zeros((P, 2))
    two[:64, 0] = 1
    two[64:, 1] = 1
    put("two", two)
    reset = np.ones((P, T))
    reset[:, ::CH] = 0
    put("reset", reset)
    w = np.zeros((P, 2))
    w[:64, 0], w[64:, 0], w[:64, 1], w[64:, 1] = 1 / 2, 1 / 4, 1 / 8, 1 / 16
    put("invw", w)
    put("causal", np.where(r[None, :] <= r[:, None], 0.0, NEG))

    slopes = 2.0 ** (-8.0 * (np.arange(8, dtype=np.float32) + 1.0) / 8)
    dist = (r[:, None] + WIN - np.arange(2 * WIN)[None, :]).astype(np.float32)
    inside = (dist >= 0) & (dist < WIN)
    alibi = np.where(inside[:, None, :], -slopes[None, :, None] * dist[:, None, :], NEG)
    inv = (1.0 / (np.float32(10000.0) ** (np.arange(0, QK_ROPE, 2, dtype=np.float32) / QK_ROPE))).astype(np.float32)
    ang = inv[:, None] * np.arange(TM, dtype=np.float32)[None, :]
    rope = np.zeros((QK_ROPE, 2, TM), np.float32)
    rope[:16, 0] = rope[16:, 0] = np.cos(ang)
    rope[:16, 1], rope[16:, 1] = -np.sin(ang), np.sin(ang)
    return c, alibi.astype(np.float32).reshape(P, 8 * 2 * WIN), rope.reshape(QK_ROPE, 2 * TM)


def program(nc, a, out, known):
    ctx = ExitStack()
    counted, reached = {}, {}
    with ctx:
        sems = {}

        def sem(name):
            if name not in sems:
                sems[name] = ctx.enter_context(nc.semaphore(name))
            return sems[name]

        def signal(stage, *index):
            reached[stage] = reached.get(stage, 0) + 1
            counted[(stage,) + index] = reached[stage]
            return sem(stage), 1

        def done(stage, *index):
            return sem(stage), (known[(stage,) + index] if known else 1)

        def sb(name, width, rows=P):
            return ctx.enter_context(nc.sbuf_tensor(name, [rows, width], F32))

        banks = [ctx.enter_context(nc.psum_tensor(f"bank{i}", [P, 512], F32)) for i in range(8)]

        xT = sb("xT", KD * T)[:, :].rearrange("p (k t) -> p k t", k=KD)
        hbuf = sb("hbuf", KD * TM)
        hT = hbuf[:, :].rearrange("p (k t) -> p k t", k=KD)
        NS = 3
        PANEL = 4096
        ring = [sb(f"ring{i}", PANEL) for i in range(NS)]
        consts = sb("consts", CONST_COLS)
        V1 = sb("V1", V1_N)
        V2 = sb("V2", V2_N)
        post = sb("post", D)
        poolw = sb("poolw", 2 * P)
        small = sb("small", 672)
        arena = sb("arena", 26700)

        def cst(name, rows=P):
            o, w = CONST_W[name]
            return consts[0:rows, o:o + w]

        ident, ones, onesbd = cst("ident"), cst("ones"), cst("onesbd")

        class Cut:
            def __init__(self, buf, at=0, end=None):
                self.buf, self.at = buf, at
                self.end = end or buf.shape[1]

            def take(self, width, rows=P, lo=0):
                r = self.buf[lo:lo + rows, self.at:self.at + width]
                self.at += width
                assert self.at <= self.end, (self.at, self.end)
                return r

        s_ = Cut(small)
        modT, modA1, modA2, cs = s_.take(48), s_.take(8), s_.take(8), s_.take(8)
        sinks, nega, dtb = s_.take(8), s_.take(1), s_.take(1)
        ssum, sroot, srstd = s_.take(4), s_.take(4), s_.take(4)
        hmeta = s_.take(8 * META)
        eglast, cA, cB = (s_.take(NC) for _ in range(3))
        rq = s_.take(NB * GH)
        smax, snmax, ssumx, sden, sesk = s_.take(16), s_.take(16), s_.take(16), s_.take(16), s_.take(16)
        rqm = s_.take(NB)
        wqk, fss, frs = s_.take(1), s_.take(8), s_.take(8)
        msum = s_.take(2)
        epsc, eps64, eps96 = s_.take(1), s_.take(1), s_.take(1)
        cols = s_.take(128)

        A1 = Cut(arena)
        qkv = A1.take(12 * T).rearrange("p (m t) -> p m t", m=12)
        gz = A1.take(NJ * T).rearrange("p (m t) -> p m t", m=NJ)
        sq = A1.take(4 * T).rearrange("p (m t) -> p m t", m=4)
        gates = A1.take(2 * T)
        glog, grow_ = gates[:, 0:T], gates[:, T:2 * T]
        hsq = [A1.take(T) for _ in range(2)]
        hrs = [A1.take(T) for _ in range(2)]
        base1 = A1.at
        B1 = Cut(arena, base1)
        sk, sv, vs = B1.take(T), B1.take(T), B1.take(T).rearrange("p (b d) -> p b d", b=NB)
        kpad = B1.take(4 * T).rearrange("p (g h t) -> p g h t", g=2, h=2)
        raw = [B1.take(T + 3) for _ in range(3)]
        alibi = B1.take(8 * 2 * WIN)
        sc = [B1.take(2 * 2 * WIN) for _ in range(2)]
        pr = [B1.take(2 * 2 * WIN) for _ in range(2)]
        prT = [B1.take(4 * WIN) for _ in range(2)]
        gt = [B1.take(T) for _ in range(4)]
        C1 = Cut(arena, 0)
        xin = C1.take(4 * D).rearrange("p (b f) -> p b f", b=4)
        rows1, rows2 = C1.take(P), C1.take(P)
        min_ = C1.take(D)
        C1b = Cut(arena, base1)
        nsq = C1b.take(KD * T).rearrange("p (k t) -> p k t", k=KD)
        rbc = C1b.take(T)
        diag = C1b.take(4 * P).rearrange("p (b t) -> p b t", b=4)
        msq = C1b.take(8 * META)
        adaacc = [post[:, 0:512], post[:, 512:1024]]
        G1 = Cut(arena, base1)
        blk = [G1.take(NC * P).rearrange("p (n c) -> p n c", n=NC) for _ in range(10)]
        qkw = G1.take(NC * CH).rearrange("p (n c) -> p n c", n=NC)
        state = G1.take(P)
        vnew = [G1.take(P) for _ in range(2)]
        G2 = Cut(hbuf)
        g_row, b_row, e_, w1, w2, qe, gx = (G2.take(T).rearrange("p (n c) -> p n c", n=NC) for _ in range(7))

        Fa = Cut(arena)
        aT = Fa.take(KF * T).rearrange("p (k t) -> p k t", k=KF)
        silug = [Fa.take(T) for _ in range(2)]
        Fa.at = max(Fa.at, 0)
        fsq = Fa.take(KD * T).rearrange("p (k t) -> p k t", k=KD)
        frbc = Fa.take(T)
        fdiag = Fa.take(4 * P).rearrange("p (b t) -> p b t", b=4)

        E2 = Cut(arena)
        ybr = E2.take(10 * T).rearrange("p (k t) -> p k t", k=10)
        base2 = E2.at
        M2 = Cut(arena, base2)
        qh = M2.take(8 * T).rearrange("p (h t) -> p h t", h=8)
        kh = M2.take(8 * TM).rearrange("p (h t) -> p h t", h=8)
        vv = M2.take(5 * T).rearrange("p (b d) -> p b d", b=5)
        msc = [M2.take(TM) for _ in range(2)]
        mpr = [M2.take(TM) for _ in range(2)]
        mpT = [M2.take(4 * WIN) for _ in range(2)]
        mpR = [M2.take(WIN) for _ in range(2)]
        rest2 = M2.at
        cq = M2.take(2 * T).rearrange("p (k t) -> p k t", k=2)
        ckv, kr = M2.take(TM), M2.take(TM)
        krs, ksq = M2.take(TM), M2.take(TM)
        krb = M2.take(TM)
        rope = M2.take(2 * TM).rearrange("p (s t) -> p s t", s=2)
        qsw = M2.take(2 * T).rearrange("p (h t) -> p h t", h=2)
        N2 = Cut(arena, base2)
        pv = [N2.take(TM) for _ in range(2)]
        pw = [N2.take(TM) for _ in range(3)]
        pg = N2.take(2 * T).rearrange("p (k t) -> p k t", k=2)
        zc = [N2.take(30 + TM) for _ in range(2)]
        ga_ = N2.take(TM)
        cacc = N2.take(2 * T).rearrange("p (k t) -> p k t", k=2)
        csq = N2.take(2 * T).rearrange("p (k t) -> p k t", k=2)
        cmr = N2.take(2 * T).rearrange("p (k t) -> p k t", k=2)
        bg = N2.take(2 * T).rearrange("p (k t) -> p k t", k=2)
        cgx = [N2.take(TM) for _ in range(2)]
        uu = [N2.take(2 + TM) for _ in range(2)]
        O2 = Cut(arena, base2)
        mT = O2.take(KD * T).rearrange("p (k t) -> p k t", k=KD)
        sg = [O2.take(T) for _ in range(2)]
        prod = [O2.take(T) for _ in range(2)]
        xtok = O2.take(4 * D).rearrange("p (b f) -> p b f", b=4)
        fin = [O2.take(D) for _ in range(4)]
        fjunk = O2.take(D)

        panels, index_of = [], {}

        def w_cols(w, c0, n, k0=0, kn=None):
            kn = kn or w.shape[0] // P - k0
            return w[k0 * P:(k0 + kn) * P, c0:c0 + n].rearrange("(k p) n -> p k n", p=P)

        def panel(name, kn, width, parts):
            index_of[name] = len(panels)
            panels.append((name, kn, width, parts))

        w_in, w_ada, w_out = a["w_in"][0], a["w_ada"][0], a["w_out"][0]
        w_gate, w_up, w_down = a["w_gate"][0], a["w_up"][0], a["w_down"][0]
        w_in2 = a["w_in_2"][0]

        def ada_panel(i):
            panel(f"ada{i}", KD, 512, [(0, 512, w_cols(w_ada, 512 * i, 512))])

        for i in range(4):
            ada_panel(i)
        for i in range(3):
            panel(f"qkv{i}", KD, 512, [(0, 512, w_cols(w_in, 512 * i, 512))])
            ada_panel(4 + i)
        panel("absk", KD, 296, [(0, 32, w_cols(w_in, 2048, 32)), (32, 8, w_cols(w_in, 2056, 8)),
                                (40, 256, w_cols(w_in, 2576, 256))])
        ada_panel(7)
        panel("sq", KD, 512, [(0, 512, w_cols(w_in, 2064, 512))])
        ada_panel(8)
        panel("gz", KD, 512, [(0, 512, w_cols(w_in, 1536, 512))])
        for i in range(9, 12):
            ada_panel(i)
        for i in range(2):
            panel(f"out{i}", KD, 512, [(0, 512, w_cols(w_out, 512 * i, 512))])
        for i in range(11):
            panel(f"gu{i}", KD, 512, [(0, 256, w_cols(w_gate, 256 * i, 256)), (256, 256, w_cols(w_up, 256 * i, 256))])
        for i in range(4):
            for h in range(2):
                panel(f"down{i}{h}", KF // 2, 256, [(0, 256, w_cols(w_down, 256 * i, 256, 11 * h, 11))])
        seg = {"pvpg": (0, 512), "cu": (1440, 512), "cgbg": (1952, 512), "cx": (2464, 512), "sg": (2976, 256),
               "cqkv": (512, 416), "mg": (928, 512)}
        for name, (c0, n) in seg.items():
            panel(name, KD, n, [(0, n, w_cols(w_in2, c0, n))])
        panel("uq", 2, 768, [(0, 768, w_cols(a["w_uq_2"][0], 0, 768))])
        panel("ukv", 1, 1024, [(0, 1024, w_cols(a["w_ukv_2"][0], 0, 1024))])
        GL0 = 3232
        branch_w = [("w_out_pool_2", 2), ("w_out_mla_2", 4), ("w_out_conf_2", 2), ("w_out_sc_2", 2)]
        for m in range(KD):
            if m % 2 == 0:
                panels.append((f"yw{m // 2}", 10, 256, None))
                index_of[f"yw{m // 2}"] = len(panels) - 1
            panel(f"gl{m}", KD, 512, [(128 * b, 128, w_cols(w_in2, GL0 + 1024 * b + 128 * m, 128)) for b in range(4)])
        for i in range(2):
            panel(f"wo{i}", KD, 512, [(0, 512, w_cols(a["w_o_2"][0], 512 * i, 512))])

        loads_of_slot = [0] * NS
        loaded_at = {}
        for i, (name, kn, width, parts) in enumerate(panels):
            n_dma = 4 if parts is None else len(parts)
            loads_of_slot[i % NS] += 16 * n_dma
            loaded_at[name] = loads_of_slot[i % NS]

        def W(name):
            i = index_of[name]
            _, kn, width, _ = panels[i]
            return ring[i % NS][:, 0:kn * width].rearrange("p (k n) -> p k n", k=kn)

        def loaded(name):
            return sem(f"loaded{index_of[name] % NS}"), loaded_at[name]

        place, tiles, uses, held, turn = {}, [], [0] * 8, set(), [0]

        def open_tile(pe, *key, hold=False):
            while turn[0] % 8 in held:
                turn[0] += 1
            b = turn[0] % 8
            turn[0] += 1
            place[key] = b, uses[b] + 1
            uses[b] += 1
            tiles.append((key, place[key]))
            if hold:
                held.add(b)
            if uses[b] > 1:
                pe.wait_ge(sem(f"bank{b}_read"), uses[b] - 1)
            return banks[b]

        def let_go(*key):
            held.discard(place[key][0])

        def fill(*key):
            return sem(f"bank{place[key][0]}_filled"), 1

        def filled(*key):
            return sem(f"bank{place[key][0]}_filled"), place[key][1]

        def read(*key):
            return sem(f"bank{place[key][0]}_read"), 1

        def copied(*key):
            return sem(f"bank{place[key][0]}_read"), place[key][1]

        def bank(*key):
            return banks[place[key][0]]

        def arrived(name, n=1):
            return sem("ld_" + name), 16 * n

        SWU = [(b, hp) for b in range(NB) for hp in range(4)]
        MLU = [(i, h) for i in range(NB) for h in range(8)]
        keys_of = [META + WIN * (i + 1) for i in range(NB)]

        block = ctx.enter_context(nc.Block())
        last_tile_of = {}

        @block.tensor
        def _(pe):
            mm, tr = nc.tensor.matmul, nc.tensor.transpose

            def project(key, name, c0, m, rhs, n, release=False, out0=0):
                o = open_tile(pe, *key)
                pe.wait_ge(*loaded(name))
                w = W(name)
                for k in range(w.shape[1]):
                    last = mm(o[0:m, 0:n], w[:, k, c0:c0 + m], rhs(k), start=k == 0, stop=k == w.shape[1] - 1)
                last.then_inc(*fill(*key))
                if release:
                    last_tile_of[name] = key

            def norm_stats(tag, sq_of, ready, n_chunks=KD):
                o = open_tile(pe, "sum" + tag)
                for b in range(4):
                    for k in range(n_chunks):
                        if b == 0:
                            pe.wait_ge(*ready(k))
                        last = mm(o[:, b:b + 1], sq_of(k)[:, b * P:(b + 1) * P], ones[:, 0:1],
                                  start=k == 0, stop=k == n_chunks - 1)
                last.then_inc(*fill("sum" + tag))

            def norm_spread(tag, dg):
                o = open_tile(pe, "spread" + tag)
                pe.wait_ge(*done("diag" + tag))
                for b in range(4):
                    last = mm(o[:, b * P:(b + 1) * P], ones, dg[:, b, :], start=True, stop=True)
                last.then_inc(*fill("spread" + tag))

            def ada(i):
                o = open_tile(pe, "ada", i)
                pe.wait_ge(*done("adaacc", i))
                for c in range(4):
                    last = mm(o[:, c:c + 1], adaacc[i % 2][:, c * P:(c + 1) * P], ones[:, 0:1], start=True, stop=True)
                last.then_inc(*fill("ada", i))

            pe.wait_ge(*arrived("const"))
            pe.wait_ge(*arrived("rows", 21))
            o = open_tile(pe, "vec")
            tr(o[:, 0:V1_N], rows1[0:V1_N, :], ident[0:V1_N, 0:V1_N])
            tr(o[:, P:P + V2_N], rows2[0:V2_N, :], ident[0:V2_N, 0:V2_N]).then_inc(*fill("vec"))
            pe.wait_ge(*arrived("x", 2))
            for k in range(KD):
                o = open_tile(pe, "x", k)
                for b in range(4):
                    last = tr(o[:, b * P:(b + 1) * P], xin[:, b, k * P:(k + 1) * P], ident)
                last.then_inc(*fill("x", k))
            o = open_tile(pe, "meta")
            for k in range(KD):
                last = tr(o[:, k * META:(k + 1) * META], min_[0:META, k * P:(k + 1) * P], ident[0:META, 0:META])
            last.then_inc(*fill("meta"))
            norm_stats("1", lambda k: nsq[:, k, :], lambda k: done("nsq", k))
            o = open_tile(pe, "summeta")
            pe.wait_ge(*done("msq"))
            for k in range(KD):
                last = mm(o[0:META, 0:1], msq[:, k * META:(k + 1) * META], ones[:, 0:1], start=k == 0, stop=k == KD - 1)
            last.then_inc(*fill("summeta"))
            norm_spread("1", diag)
            o = open_tile(pe, "spreadmeta")
            pe.wait_ge(*done("diagmeta"))
            mm(o[:, 0:META], ones[0:META, :], rbc[0:META, 0:META], start=True, stop=True).then_inc(*fill("spreadmeta"))
            for i in range(4):
                ada(i)

            hx = lambda k: hT[:, k, 0:T]
            hs_tile = None
            for k in range(KD):
                pe.wait_ge(*done("h1", k))
            for i in range(3):
                for m in range(4 * i, 4 * i + 4):
                    project(("pj", m), f"qkv{i}", P * (m % 4), P, hx, T, release=m % 4 == 3)
                ada(4 + i)
            project(("ab",), "absk", 0, 40, hx, T)
            project(("sk",), "absk", 40, P, hx, T)
            project(("sv",), "absk", 40 + P, P, hx, T, release=True)
            ada(7)
            for m in range(4):
                project(("sq", m), "sq", P * m, P, hx, T, release=m == 3)
            ada(8)
            for m in range(4):
                project(("gz", m), "gz", P * m, P, hx, T, release=m == 3)
            for i in range(9, 12):
                ada(i)

            o = open_tile(pe, "hsum")
            pick = cst("pick").rearrange("p (w j c) -> p w j c", w=2, j=NJ)
            for m in range(8):
                pe.wait_ge(*done("hsq", m))
                last = mm(o[0:40, :], pick[:, m // 4, m % 4, :], hsq[m % 2], start=m == 0, stop=m == 7)
                last.then_inc(*(fill("hsum") if m == 7 else signal("hsum_step", m)))
            o = open_tile(pe, "sksum")
            pe.wait_ge(*done("hsq", 8))
            mm(o[:, :], onesbd, hsq[0], start=True, stop=True).then_inc(*fill("sksum"))
            o = open_tile(pe, "sqsum")
            for m in range(4):
                pe.wait_ge(*done("hsq", 9 + m))
                for b in range(NB):
                    c = (b * 4 + m) * 2
                    last = mm(o[:, c:c + 2], hsq[(9 + m) % 2][:, b * P:(b + 1) * P], cst("two"), start=True, stop=True)
                last.then_inc(*(fill("sqsum") if m == 3 else signal("sqsum_step", m)))
            o = open_tile(pe, "vs")
            pe.wait_ge(*copied("sv"))
            for b in range(NB):
                last = tr(o[:, b * P:(b + 1) * P], sv[:, b * P:(b + 1) * P], ident)
            last.then_inc(*fill("vs"))

            o = open_tile(pe, "cols")
            pe.wait_ge(*done("grows"))
            for n in range(NC):
                for s, (r0, src) in enumerate(((0, glog), (32, glog), (32, grow_), (64, grow_))):
                    for h in range(2):
                        last = mm(o[h * HD:(h + 1) * HD, n * 32 + 8 * s:n * 32 + 8 * s + 8],
                                  src[0:72, n * CH:(n + 1) * CH], ident[0:72, r0:r0 + 8],
                                  start=True, stop=True)
            last.then_inc(*fill("cols"))

            pe.wait_ge(*done("kpad"))

            def sw_scores(u):
                b, hp = SWU[u]
                k0, wk = (0, WIN) if b == 0 else ((b - 1) * WIN, 2 * WIN)
                o = open_tile(pe, "ss", u)
                for p in range(2):
                    last = mm(o[:, p * wk:(p + 1) * wk], sq[:, hp, b * WIN:(b + 1) * WIN],
                              kpad[:, hp // 2, p, k0:k0 + wk], start=True, stop=True)
                last.then_inc(*fill("ss", u))

            def sw_turn(u):
                b, hp = SWU[u]
                nk = 1 if b == 0 else 2
                o = open_tile(pe, "st", u)
                pe.wait_ge(*done("sprob", u))
                for c in range(2 * nk):
                    last = tr(o[:, c * WIN:(c + 1) * WIN], pr[u % 2][:, c * WIN:(c + 1) * WIN], ident)
                last.then_inc(*fill("st", u))

            def sw_values(u):
                b, hp = SWU[u]
                nk = 1 if b == 0 else 2
                if hp == 0:
                    sw_out[0] = open_tile(pe, "so", b, hold=True)
                o = sw_out[0]
                pe.wait_ge(*copied("st", u))
                g = hp // 2
                for p in range(2):
                    for kb in range(nk):
                        last = mm(o[p * HD:(p + 1) * HD, hp * WIN:(hp + 1) * WIN],
                                  vs[:, b - nk + 1 + kb, g * HD:(g + 1) * HD],
                                  prT[u % 2][:, (p * nk + kb) * WIN:(p * nk + kb + 1) * WIN],
                                  start=kb == 0, stop=kb == nk - 1)
                if hp == 3:
                    last.then_inc(*fill("so", b))
                    let_go("so", b)
                else:
                    last.then_inc(*signal("so_step", u))

            sw_out = [None]
            for u in range(len(SWU) + 2):
                if u < len(SWU):
                    sw_scores(u)
                if u >= 2:
                    sw_turn(u - 2)
                    sw_values(u - 2)

            for j in range(NJ):
                for s, (r0, src) in enumerate(((0, glog), (32, glog), (0, grow_))):
                    o = open_tile(pe, "rows", j, s)
                    selj = cst("sel", 40)[r0:r0 + 8, j * P:(j + 1) * P]
                    mm(o[:, :], selj, src[r0:r0 + 8, :], start=True, stop=True).then_inc(*fill("rows", j, s))

                def squares(name, left, right, waits=()):
                    for half in range(2):
                        o = open_tile(pe, name, j, half)
                        if half == 0:
                            for w in waits:
                                pe.wait_ge(*w)
                        for n in range(4):
                            nn = 4 * half + n
                            last = mm(o[:, n * P:(n + 1) * P], left[:, nn, :], right[:, nn, :], start=True, stop=True)
                        last.then_inc(*fill(name, j, half))

                def turns(name, src, waits=()):
                    for half in range(2):
                        o = open_tile(pe, name, j, half)
                        if half == 0:
                            for w in waits:
                                pe.wait_ge(*w)
                        for n in range(4):
                            last = tr(o[:, n * P:(n + 1) * P], src[:, 4 * half + n, :], ident)
                        last.then_inc(*fill(name, j, half))

                squares("kk", blk[0], blk[0], [done("kbd", j)])
                o = open_tile(pe, "kq", j)
                for n in range(NC):
                    last = mm(o[:, n * CH:(n + 1) * CH], blk[0][:, n, :],
                              qkv[:, j, n * CH:(n + 1) * CH], start=True, stop=True)
                last.then_inc(*fill("kq", j))
                turns("tA", blk[2], [copied("kk", j, 1)])
                squares("d2", blk[3], blk[5], [done("dT", j), copied("tA", j, 1)])
                squares("d2T", blk[5], blk[3])
                squares("d4", blk[9], blk[8], [copied("d2", j, 1), copied("d2T", j, 1)])
                squares("d4T", blk[8], blk[9])
                squares("p1", blk[8], blk[4], [done("p0", j)])
                turns("kt", blk[0])
                turns("vt", blk[1])
                squares("d8", blk[3], blk[2], [copied("d4", j, 1), copied("d4T", j, 1)])
                squares("p2", blk[2], blk[4], [copied("p1", j, 1)])
                squares("p3", blk[5], blk[4], [copied("d8", j, 1), copied("p2", j, 1)])
                turns("t16", blk[4], [copied("p3", j, 1)])
                squares("z1", blk[6], blk[4])
                squares("i32", blk[2], blk[3], [copied("t16", j, 1), copied("z1", j, 1)])
                turns("t32", blk[4], [copied("i32", j, 1)])
                squares("z2", blk[7], blk[4])
                squares("i64", blk[5], blk[3], [copied("t32", j, 1), copied("z2", j, 1)])
                squares("wT", blk[8], blk[4], [copied("kt", j, 1), copied("i64", j, 1)])
                oo = open_tile(pe, "go", j, hold=True)
                for n in range(NC):
                    o = open_tile(pe, "vn", j, n)
                    if n == 0:
                        pe.wait_ge(*copied("wT", j, 1))
                        pe.wait_ge(*copied("vt", j, 1))
                        pe.wait_ge(*done("qe", j))
                        pe.wait_ge(*copied("kq", j))
                    last = mm(o[:, 0:P], blk[4][:, n, :], blk[1][:, n, :], start=True, stop=n == 0)
                    if n > 0:
                        pe.wait_ge(*copied("su", j, n - 1))
                        last = mm(o[:, 0:P], blk[6][:, n, :], state, start=False, stop=True)
                    last.then_inc(*fill("vn", j, n))
                    if n > 0:
                        mm(oo[:, n * CH:(n + 1) * CH], state, qe[:, n, :], start=True, stop=False)
                    pe.wait_ge(*copied("vn", j, n))
                    if n < NC - 1:
                        o = open_tile(pe, "su", j, n)
                        mm(o[:, 0:P], blk[0][:, n, :], vnew[n % 2], start=True, stop=True).then_inc(*fill("su", j, n))
                    last = mm(oo[:, n * CH:(n + 1) * CH], vnew[n % 2], qkw[:, n, :], start=n == 0, stop=True)
                    last.then_inc(*(fill("go", j) if n == NC - 1 else signal("go_step", j, n)))
                let_go("go", j)

            o = open_tile(pe, "osum")
            for j in range(NJ):
                pe.wait_ge(*done("osq", j))
                last = mm(o[0:40, :], pick[:, 0, j, :], hsq[j % 2], start=j == 0, stop=j == NJ - 1)
                last.then_inc(*(fill("osum") if j == NJ - 1 else signal("osum_step", j)))
            for j in range(NJ):
                o = open_tile(pe, "ospread", j)
                if j == 0:
                    pe.wait_ge(*done("orow"))
                mm(o[:, :], cst("sel", 40)[0:8, j * P:(j + 1) * P], hrs[1][0:8, :], start=True, stop=True)\
                    .then_inc(*fill("ospread", j))

            for j in range(NJ):
                pe.wait_ge(*done("mixg", j))
            pe.wait_ge(*copied("so", NB - 1))
            mix = lambda k: qkv[:, k, :] if k < 4 else sq[:, k - 4, :]
            for m in range(KD):
                project(("mo", m), f"out{m // 4}", P * (m % 4), P, mix, T, release=m % 4 == 3)
            norm_stats("2", lambda k: fsq[:, k, :], lambda k: done("fsq", k))
            norm_spread("2", fdiag)
            for k in range(KD):
                pe.wait_ge(*done("h2", k))
            for i in range(11):
                for c in range(2):
                    project(("fg", 2 * i + c), f"gu{i}", P * c, P, hx, T)
                    project(("fu", 2 * i + c), f"gu{i}", 256 + P * c, P, hx, T, release=c == 1)
            for m in range(KD):
                o = open_tile(pe, "fd", m)
                for half in range(2):
                    name = f"down{m // 2}{half}"
                    pe.wait_ge(*loaded(name))
                    for k in range(11):
                        kk = 11 * half + k
                        if m == 0:
                            pe.wait_ge(*copied("fu", kk))
                        last = mm(o[:, :], W(name)[:, k, P * (m % 2):P * (m % 2) + P], aT[:, kk, :],
                                  start=kk == 0, stop=kk == KF - 1)
                    last.then_inc(*(fill("fd", m) if half else signal("fd_half", m)))
                last_tile_of[f"down{m // 2}0"] = last_tile_of[f"down{m // 2}1"] = ("fd", m)
            norm_stats("3", lambda k: fsq[:, k, :], lambda k: done("gsq", k))
            norm_spread("3", fdiag)

            pe.wait_ge(*done("h3meta"))
            for k in range(KD):
                pe.wait_ge(*done("h3", k))
            hall = [lambda k: hT[:, k, 0:TM // 2], lambda k: hT[:, k, TM // 2:TM]]
            hreal = lambda k: hT[:, k, META:TM]

            def project_all(key, name, c0, m, release=False):
                for half in range(2):
                    project(key + (half,), name, c0, m, hall[half], TM // 2, release and half == 1)

            for m in range(2):
                project_all(("pv", m), "pvpg", P * m, P)
            for m in range(2):
                project(("pg", m), "pvpg", 256 + P * m, P, hreal, T, release=m == 1)
            for m in range(2):
                project_all(("cgate", m), "cu", 256 + P * m, P)
                project_all(("cu", m), "cu", P * m, P, release=m == 1)
            for m in range(2):
                o = open_tile(pe, "py", m)
                pe.wait_ge(*done("pool", m))
                mm(o[:, :], poolw[:, P * m:P * m + P], pw[m][:, META:TM], start=True, stop=True).then_inc(*fill("py", m))
            for m in range(2):
                project(("cg", m), "cgbg", P * m, P, hreal, T)
            for m in range(2):
                project(("bg", m), "cgbg", 256 + P * m, P, hreal, T, release=m == 1)
            for m in range(2):
                project_all(("cgx", m), "cx", P * m, P)
                project_all(("xv", m), "cx", 256 + P * m, P, release=m == 1)
            for m in range(2):
                project(("sg", m), "sg", P * m, P, hreal, T, release=m == 1)
            for tag, src in (("cmean", cacc), ("cvar", csq)):
                o = open_tile(pe, tag)
                for m in range(2):
                    pe.wait_ge(*done(tag + "_in", m))
                    last = mm(o[:, :], ones, src[:, m, :], start=m == 0, stop=m == 1)
                last.then_inc(*fill(tag))
            for m in range(2):
                project(("cq", m), "cqkv", P * m, P, hreal, T)
            project_all(("ckv",), "cqkv", 256, P)
            project_all(("kr",), "cqkv", 320, 96, release=True)
            for m in range(4):
                project(("mg", m), "mg", P * m, P, hreal, T, release=m == 3)

            o = open_tile(pe, "cqsum")
            for b in range(4):
                for k in range(2):
                    if b == 0:
                        pe.wait_ge(*done("cqsq", k))
                    last = mm(o[:, b:b + 1], qsw[:, k, b * P:(b + 1) * P], ones[:, 0:1], start=k == 0, stop=k == 1)
            last.then_inc(*fill("cqsum"))
            for half in range(2):
                o = open_tile(pe, "kvsum", half)
                pe.wait_ge(*done("ckvsq"))
                mm(o[:, 0:TM // 2], ones, ksq[:, half * (TM // 2):(half + 1) * (TM // 2)], start=True, stop=True)\
                    .then_inc(*fill("kvsum", half))
            pe.wait_ge(*loaded("uq"))
            pe.wait_ge(*done("cqg", 1))
            for h in range(8):
                o = open_tile(pe, "q", h)
                for k in range(2):
                    last = mm(o[0:QD, :], W("uq")[:, k, h * QD:(h + 1) * QD], cq[:, k, :], start=k == 0, stop=k == 1)
                last.then_inc(*fill("q", h))
            last_tile_of["uq"] = ("q", 7)
            pe.wait_ge(*loaded("ukv"))
            pe.wait_ge(*done("ckvn"))
            wkv = W("ukv")[:, 0, :].rearrange("p (h d) -> p h d", h=8)
            for h in range(8):
                for half in range(2):
                    o = open_tile(pe, "k", h, half)
                    mm(o[0:HD, 0:TM // 2], wkv[:, h, 0:HD], ckv[:, half * (TM // 2):(half + 1) * (TM // 2)],
                       start=True, stop=True).then_inc(*fill("k", h, half))
            for b in range(5):
                n = P if b < 4 else META
                o = open_tile(pe, "v", b)
                mm(o[0:n, :], ckv[:, b * P:b * P + n], wkv[:, :, HD:2 * HD], start=True, stop=True)\
                    .then_inc(*fill("v", b))
            last_tile_of["ukv"] = ("v", 4)

            def ml_scores(u):
                i, h = MLU[u]
                n = keys_of[i]
                o = open_tile(pe, "ms", u)
                m0 = min(n, 512)
                mm(o[:, 0:m0], qh[0:QD, h, i * WIN:(i + 1) * WIN], kh[0:QD, h, 0:m0], start=True, stop=True)\
                    .then_inc(*fill("ms", u))
                if n > 512:
                    o = open_tile(pe, "ms2", u)
                    mm(o[:, 0:n - 512], qh[0:QD, h, i * WIN:(i + 1) * WIN], kh[0:QD, h, 512:n],
                       start=True, stop=True).then_inc(*fill("ms2", u))

            def ml_turn(u):
                i, h = MLU[u]
                o = open_tile(pe, "mt", u)
                pe.wait_ge(*done("mprob", u))
                for c in range(i + 1):
                    last = tr(o[:, c * WIN:(c + 1) * WIN], mpr[u % 2][:, c * WIN:(c + 1) * WIN], ident)
                last.then_inc(*fill("mt", u))
                o = open_tile(pe, "mr", u)
                tr(o[0:META, 0:WIN], mpr[u % 2][:, (i + 1) * WIN:(i + 1) * WIN + META], ident)\
                    .then_inc(*fill("mr", u))

            ml_out = [None]

            def ml_values(u):
                i, h = MLU[u]
                if h == 0:
                    ml_out[0] = open_tile(pe, "mo2", i, hold=True)
                o = ml_out[0]
                p, pair = h % 2, h // 2
                pe.wait_ge(*copied("mt", u))
                for c in range(i + 1):
                    mm(o[p * HD:(p + 1) * HD, pair * WIN:(pair + 1) * WIN], vv[:, c, h * HD:(h + 1) * HD],
                       mpT[u % 2][:, c * WIN:(c + 1) * WIN], start=c == 0, stop=False)
                pe.wait_ge(*copied("mr", u))
                last = mm(o[p * HD:(p + 1) * HD, pair * WIN:(pair + 1) * WIN], vv[:, i + 1, h * HD:(h + 1) * HD],
                          mpR[u % 2], start=False, stop=True)
                last.then_inc(*(fill("mo2", i) if h == 7 else signal("mo_step", u)))
                if h == 7:
                    let_go("mo2", i)

            pe.wait_ge(*done("qrope", 3))
            pe.wait_ge(*done("krope"))
            pe.wait_ge(*copied("k", 7, 1))
            pe.wait_ge(*copied("v", 4))
            pe.wait_ge(*done("vpad"))
            for u in range(len(MLU) + 2):
                if u < len(MLU):
                    ml_scores(u)
                if u >= 2:
                    ml_turn(u - 2)
                    ml_values(u - 2)

            for b in range(NB):
                pe.wait_ge(*copied("mo2", b))
            for k in range(2):
                pe.wait_ge(*copied("py", k))
                pe.wait_ge(*done("yc", k))
                pe.wait_ge(*done("yd", k))
            for m in range(KD):
                k0 = 0
                yw = f"yw{m // 2}"
                for b in range(4):
                    project(("gl", m, b), f"gl{m}", P * b, P, hreal, T, release=b == 3)
                    o = open_tile(pe, "y", m, b)
                    pe.wait_ge(*loaded(yw))
                    nk = branch_w[b][1]
                    for k in range(nk):
                        last = mm(o[:, :], W(yw)[:, k0 + k, P * (m % 2):P * (m % 2) + P], ybr[:, k0 + k, :],
                                  start=k == 0, stop=k == nk - 1)
                    last.then_inc(*fill("y", m, b))
                    k0 += nk
                last_tile_of[yw] = ("y", m, 3)
            for b in range(4):
                for half in range(2):
                    o = open_tile(pe, "xt", b, half)
                    for c in range(4):
                        last = tr(o[:, c * P:(c + 1) * P], xT[:, 4 * half + c, b * P:(b + 1) * P], ident)
                    last.then_inc(*fill("xt", b, half))
            for k in range(KD):
                pe.wait_ge(*done("mT", k))
            for half in range(2):
                pe.wait_ge(*loaded(f"wo{half}"))
            for b in range(4):
                for half in range(2):
                    o = open_tile(pe, "fo", b, half)
                    for k in range(KD):
                        last = mm(o[:, :], mT[:, k, b * P:(b + 1) * P], W(f"wo{half}")[:, k, :],
                                  start=k == 0, stop=k == KD - 1)
                    last.then_inc(*fill("fo", b, half))

        @block.sync
        def _(sp):
            sp.dma_start(consts[:, :], a["consts"]).then_inc(sem("ld_const"), 16)
            sp.dma_start(xin, a["x"][0].rearrange("(b p) f -> p b f", p=P)).then_inc(sem("ld_x"), 16)
            sp.dma_start(min_[0:META, :], a["meta_tokens_2"]).then_inc(sem("ld_x"), 16)
            for i, (name, kn, width, parts) in enumerate(panels):
                if i >= NS:
                    before = panels[i - NS][0]
                    sp.wait_ge(*(done("adaacc", int(before[3:])) if before.startswith("ada")
                                 else filled(*last_tile_of[before])))
                dst = W(name)
                if parts is None:
                    m2 = int(name[2:])
                    k0 = 0
                    for wname, nk in branch_w:
                        sp.dma_start(dst[:, k0:k0 + nk, :], w_cols(a[wname][0], 256 * m2, 256))\
                            .then_inc(sem(f"loaded{i % NS}"), 16)
                        k0 += nk
                else:
                    for c0, n, src in parts:
                        sp.dma_start(dst[:, :, c0:c0 + n], src).then_inc(sem(f"loaded{i % NS}"), 16)
            sp.wait_ge(sem("stored"), 16 * 4)

        @block.gpsimd
        def _(pool):
            vec = [("b_ada", a["b_ada"][0], 48), ("norm1", a["norm1_w"][0], 8), ("norm2", a["norm2_w"][0], 8),
                   ("pre", a["pre_norm_g_2"][0], 8), ("gate_bias", a["gate_bias_2"][0], 32),
                   ("conf_b", a["conf_dw_b_2"][0], 2), ("ln_g", a["conf_ln_g_2"][0], 2),
                   ("ln_b", a["conf_ln_b_2"][0], 2), ("pool_scale", a["pool_scale_2"][0], 2),
                   ("q_norm", a["q_norm_g_2"][0], 2), ("kv_norm", a["kv_norm_g_2"][0], 1), ("c", a["c"][0], 8)]
            for name, src, n in vec:
                r = V1_ROWS[name]
                pool.dma_start(rows1[r:r + n, :], src.rearrange("(r p) -> r p", p=P)).then_inc(sem("ld_rows"), 16)
            for name, src in (("gdn_norm", a["gdn_norm_w"]), ("qn", a["q_norm_w"]), ("kn", a["k_norm_w"])):
                r = V1_ROWS[name]
                for h in range(2):
                    pool.dma_start(rows1[r:r + 1, h * HD:(h + 1) * HD], src).then_inc(sem("ld_rows"), 16)
            pool.dma_start(rows2[0:48, :], a["conv_w"][0, :, 0, :].rearrange("k (m p) -> (k m) p", p=P))\
                .then_inc(sem("ld_rows"), 16)
            pool.dma_start(rows2[48:110, :], a["conf_dw_w_2"][0].rearrange("k (m p) -> (k m) p", p=P))\
                .then_inc(sem("ld_rows"), 16)
            pool.dma_start(rows2[110:116, :], a["sc_dw_w_2"][0].rearrange("k (m p) -> (k m) p", p=P))\
                .then_inc(sem("ld_rows"), 16)
            pool.dma_start(nega[0:8, :], a["a_log"][0].rearrange("(h o) -> h o", o=1)).then_inc(sem("ld_gate"), 16)
            pool.dma_start(dtb[0:8, :], a["dt_bias"][0].rearrange("(h o) -> h o", o=1)).then_inc(sem("ld_gate"), 16)
            pool.dma_start(sinks, a["sinks"].broadcast_to([P, 8])).then_inc(sem("ld_gate"), 16)
            nc.gpsimd.memset(poolw[:, :], 0.0).then_inc(*signal("poolw0"))
            pool.wait_ge(*done("poolw0"))
            for g in range(4):
                r, c = (g % 2) * HD, (g // 2) * P + (g % 2) * HD
                pool.dma_start(poolw[r:r + HD, c:c + HD], a["pool_w_2"][0, g]).then_inc(sem("ld_poolw"), 16)
            pool.wait_ge(*done("xn1", KD - 1))
            pool.wait_ge(*copied("spreadmeta"))
            pool.dma_start(alibi, a["alibi"]).then_inc(sem("ld_alibi"), 16)
            nc.gpsimd.memset(kpad, 0.0).then_inc(*signal("kpad0"))
            for u, (b, hp) in enumerate(SWU):
                wk = WIN if b == 0 else 2 * WIN
                pool.wait_ge(*done("srec", u))
                v = pr[u % 2][:, 0:2 * wk].rearrange("p (h k) -> p h k", h=2)
                nc.gpsimd.tensor_tensor(v, v, sden[:, 2 * (u % 8):2 * (u % 8) + 2].unsqueeze(2).broadcast_to([P, 2, wk]),
                                        ALU.mult).then_inc(*signal("sprob", u))
            eye8 = ident.unsqueeze(1).broadcast_to([P, NC, P])
            m16T = cst("m16T").unsqueeze(1).broadcast_to([P, NC, P])
            for j in range(NJ):
                pool.wait_ge(*copied("kk", j, 0))
                pool.wait_ge(*copied("kk", j, 1))
                nc.gpsimd.tensor_tensor(blk[3], blk[2], m16T, ALU.mult).then_inc(*signal("dT", j))
                pool.wait_ge(*done("dT", j))
                nc.gpsimd.tensor_tensor(blk[4], eye8, blk[3], ALU.subtract).then_inc(*signal("p0", j))
            pool.wait_ge(*filled("ada", 11))
            pool.dma_start(post[:, :], a["post_norm_g_2"].broadcast_to([P, D])).then_inc(sem("ld_post"), 16)
            pool.wait_ge(*filled("fd", 7))
            pool.dma_start(rope[HD:QD, :, :], a["rope"].rearrange("r (s t) -> r s t", s=2)).then_inc(sem("ld_rope"), 16)
            half = QK_ROPE // 2
            pool.wait_ge(*copied("kr", 0))
            pool.wait_ge(*copied("kr", 1))
            for d0, s0 in ((HD, HD + half), (HD + half, HD)):
                pool.dma_start(krs[d0:d0 + half, :], kr[s0:s0 + half, :]).then_inc(sem("ld_krs"), 16)
            for g in range(4):
                for h in (2 * g, 2 * g + 1):
                    pool.wait_ge(*copied("q", h))
                if g:
                    pool.wait_ge(*done("qrope", g - 1))
                for d0, s0 in ((HD, HD + half), (HD + half, HD)):
                    pool.dma_start(qsw[d0:d0 + half, :, :], qh[s0:s0 + half, 2 * g:2 * g + 2, :])\
                        .then_inc(sem("ld_qsw"), 16)
            for u, (i, h) in enumerate(MLU):
                n = keys_of[i]
                pool.wait_ge(*done("mrec", u))
                v = mpr[u % 2][:, 0:n]
                nc.gpsimd.tensor_tensor(v, v, sden[:, u % 16:u % 16 + 1].broadcast_to([P, n]), ALU.mult)\
                    .then_inc(*signal("mprob", u))

        @block.scalar
        def _(act):
            A = nc.scalar.activation
            act.wait_ge(*filled("vec"))
            A(V1[:, :], bank("vec")[:, 0:V1_N], ACT.Copy).then_inc(*signal("v1"))
            A(V2[:, :], bank("vec")[:, P:P + V2_N], ACT.Copy).then_inc(*read("vec"))
            act.wait_ge(*done("v1"))
            A(cs, V1[:, V1_ROWS["c"]:V1_ROWS["c"] + 8], ACT.Silu).then_inc(*signal("cs"))
            for k in range(KD):
                act.wait_ge(*filled("x", k))
                A(xT[:, k, :], bank("x", k)[:, :], ACT.Copy).then_inc(*read("x", k))
            act.wait_ge(*filled("meta"))
            A(hmeta, bank("meta")[:, 0:8 * META], ACT.Copy).then_inc(*read("meta"))

            def root(tag, out, key, scale, bias):
                act.wait_ge(*filled(*key))
                A(out, bank(*key)[0:out.shape[0], 0:out.shape[1]], ACT.Sqrt, bias=bias, scale=scale).then_inc(*read(*key))

            root("1", sroot, ("sum1",), 1.0 / D, epsc)
            root("meta", msum[0:META, 0:1], ("summeta",), 1.0 / D, epsc[0:META, :])
            act.wait_ge(*done("modA1"))
            for k in range(KD):
                act.wait_ge(*done("xn1", k))
                A(hT[:, k, 0:T], hT[:, k, 0:T], ACT.Identity, scale=modA1[:, k:k + 1], bias=modT[:, k:k + 1])\
                    .then_inc(*signal("h1", k))
            def conv_in(m):
                act.wait_ge(*filled("pj", m))
                if m >= 3:
                    act.wait_ge(*done("conv", m - 3, 3))
                A(raw[m % 3][:, 3:], bank("pj", m)[:, :], ACT.Copy).then_inc(*read("pj", m))

            def conv_out(m):
                act.wait_ge(*done("conv", m, 3))
                A(qkv[:, m, :], qkv[:, m, :], ACT.Silu).then_inc(*signal("silu", m))

            act.wait_ge(*done("rawpad"))
            for m in range(14):
                if m < 12:
                    conv_in(m)
                if m >= 2:
                    conv_out(m - 2)
            act.wait_ge(*filled("ab"))
            A(gt[3][0:40, :], bank("ab")[0:40, :], ACT.Copy).then_inc(*read("ab"))
            act.wait_ge(*filled("sk"))
            A(sk, bank("sk")[:, :], ACT.Copy).then_inc(*read("sk"))
            act.wait_ge(*filled("sv"))
            A(sv, bank("sv")[:, :], ACT.Copy).then_inc(*read("sv"))
            for m in range(4):
                act.wait_ge(*filled("sq", m))
                A(sq[:, m, :], bank("sq", m)[:, :], ACT.Copy).then_inc(*read("sq", m))
            for m in range(4):
                act.wait_ge(*filled("gz", m))
                A(gz[:, m, :], bank("gz", m)[:, :], ACT.Silu).then_inc(*read("gz", m))
            for m in range(8):
                act.wait_ge(*done("silu", m))
                if m >= 2:
                    act.wait_ge(*done("hsum_step", m - 2))
                A(hsq[m % 2], qkv[:, m, :], ACT.Square).then_inc(*signal("hsq", m))
            act.wait_ge(*done("hsum_step", 6))
            act.wait_ge(*copied("sk"))
            A(hsq[0], sk, ACT.Square).then_inc(*signal("hsq", 8))
            act.wait_ge(*filled("hsum"))
            for m in range(4):
                act.wait_ge(*copied("sq", m))
                if m == 1:
                    act.wait_ge(*filled("sksum"))
                if m >= 2:
                    act.wait_ge(*done("sqsum_step", m - 2))
                A(hsq[(9 + m) % 2], sq[:, m, :], ACT.Square).then_inc(*signal("hsq", 9 + m))
            act.wait_ge(*filled("hsum"))
            A(hrs[0][0:40, :], bank("hsum")[0:40, :], ACT.Sqrt, bias=epsc[0:40, :]).then_inc(*read("hsum"))
            act.wait_ge(*filled("sksum"))
            A(hrs[1], bank("sksum")[:, :], ACT.Sqrt, bias=epsc, scale=1.0 / HD).then_inc(*read("sksum"))
            act.wait_ge(*filled("sqsum"))
            A(rq, bank("sqsum")[:, 0:32], ACT.Sqrt, bias=eps64).then_inc(*read("sqsum"))
            act.wait_ge(*filled("vs"))
            A(vs, bank("vs")[:, :].rearrange("p (b d) -> p b d", b=NB), ACT.Copy).then_inc(*read("vs"))
            act.wait_ge(*copied("ab"))
            A(gt[0][32:40, :], gt[3][32:40, :], ACT.Exp, scale=-1.0).then_inc(*signal("egb"))
            act.wait_ge(*arrived("gate", 3))
            A(nega[0:8, :], nega[0:8, :], ACT.Exp).then_inc(*signal("ealog"))
            act.wait_ge(*done("nabs"))
            A(gt[2][0:8, :], gt[2][0:8, :], ACT.Exp).then_inc(*signal("eabs"))
            act.wait_ge(*done("eabs"))
            A(gt[2][0:8, :], gt[2][0:8, :], ACT.Ln, bias=1.0).then_inc(*signal("lnabs"))
            act.wait_ge(*done("skn"))
            act.wait_ge(*done("kpad0"))
            for g in range(2):
                for p in range(2):
                    last = A(kpad[p * HD:(p + 1) * HD, g, p, :], sk[g * HD:(g + 1) * HD, :], ACT.Copy)
                    last.then_inc(*(signal("kpad") if g and p else signal("kpad_part")))
            act.wait_ge(*filled("cols"))
            cps = bank("cols")[:, 0:256].rearrange("p (n s j h) -> p h n s j", n=NC, s=4, j=NJ)
            colv = cols.rearrange("p (n s j) -> p n s j", n=NC, s=4)
            for h in range(2):
                rows = slice(h * HD, (h + 1) * HD)
                A(colv[rows].rearrange("p n s j -> p n (s j)"), cps[rows, h].rearrange("p n s j -> p n (s j)"), ACT.Copy)\
                    .then_inc(*(read("cols") if h else signal("cols_low")))

            def sw_exp(u):
                b, hp = SWU[u]
                wk = WIN if b == 0 else 2 * WIN
                act.wait_ge(*done("snmax", u))
                if u >= 2:
                    act.wait_ge(*filled("st", u - 2))
                s2 = 2 * (u % 8)
                for p in range(2):
                    A(pr[u % 2][:, p * wk:(p + 1) * wk], sc[u % 2][:, p * wk:(p + 1) * wk], ACT.Exp,
                      bias=snmax[:, s2 + p:s2 + p + 1], accum_out=ssumx[:, s2 + p:s2 + p + 1])\
                        .then_inc(*signal("sexp", u, p))
                A(sesk[:, s2:s2 + 2], sesk[:, s2:s2 + 2], ACT.Exp).then_inc(*signal("sesk", u))

            def sw_copy(u):
                b, hp = SWU[u]
                n = 2 * WIN if b == 0 else 4 * WIN
                act.wait_ge(*filled("st", u))
                if u >= 2:
                    b2, hp2 = SWU[u - 2]
                    act.wait_ge(*(filled("so", b2) if hp2 == 3 else done("so_step", u - 2)))
                A(prT[u % 2][:, 0:n], bank("st", u)[:, 0:n], ACT.Copy).then_inc(*read("st", u))
                if hp == 3:
                    act.wait_ge(*filled("so", b))
                    A(sq[:, :, b * WIN:(b + 1) * WIN], bank("so", b)[:, :].rearrange("p (h t) -> p h t", h=4),
                      ACT.Copy).then_inc(*read("so", b))

            for u in range(len(SWU) + 2):
                if u < len(SWU):
                    sw_exp(u)
                if u >= 2:
                    sw_copy(u - 2)

            v4 = lambda t: t.rearrange("p (n c) -> p n c", n=4)
            for j in range(NJ):
                if j == 0:
                    act.wait_ge(*done("bdzero"))
                else:
                    act.wait_ge(*filled("go", j - 1))
                for half, (dst, m) in enumerate(((blk[0], 4 + j), (blk[1], 8 + j))):
                    for h in range(2):
                        rows = slice(h * HD, (h + 1) * HD)
                        A(dst[rows, :, h * HD:(h + 1) * HD],
                          qkv[rows, m, :].rearrange("p (n c) -> p n c", n=NC), ACT.Copy)\
                            .then_inc(*(signal("kbd", j) if half and h else signal("bd_part", j, half, h)))
                act.wait_ge(*filled("rows", j, 0))
                A(g_row, bank("rows", j, 0)[:, :].rearrange("p (n c) -> p n c", n=NC), ACT.Copy).then_inc(*read("rows", j, 0))
                act.wait_ge(*done("emin", j))
                A(e_, e_, ACT.Exp).then_inc(*signal("e", j))
                act.wait_ge(*copied("rows", j, 0))
                A(gx, g_row, ACT.Exp).then_inc(*signal("gx", j))
                A(cA, colv[:, :, 0, j], ACT.Exp).then_inc(*signal("cAexp", j))
                A(eglast, g_row[:, :, CH - 1], ACT.Exp).then_inc(*signal("eglast", j))
                act.wait_ge(*done("cBarg", j))
                A(cB, cB, ACT.Exp).then_inc(*signal("cBexp", j))

                def move(name, dst, scale=1.0, waits=()):
                    for w in waits:
                        act.wait_ge(*w)
                    for half in range(2):
                        act.wait_ge(*filled(name, j, half))
                        A(dst[:, 4 * half:4 * half + 4, :], v4(bank(name, j, half)[:, :]), ACT.Copy, scale=scale)\
                            .then_inc(*read(name, j, half))

                move("d2", blk[8])
                move("d2T", blk[9])
                move("d4", blk[2], waits=[done("p0", j)])
                move("d4T", blk[3])
                move("d8", blk[5])
                move("t16", blk[2])
                move("z1", blk[3])
                move("t32", blk[5])
                move("z2", blk[3])
                move("wT", blk[6], scale=-1.0)
                for n in range(NC):
                    act.wait_ge(*filled("vn", j, n))
                    A(vnew[n % 2], bank("vn", j, n)[:, 0:P], ACT.Copy).then_inc(*read("vn", j, n))
                act.wait_ge(*filled("go", j))
                A(qkv[:, j, :], bank("go", j)[:, :], ACT.Copy).then_inc(*read("go", j))
            for j in range(NJ):
                act.wait_ge(*copied("go", j))
                if j >= 2:
                    act.wait_ge(*done("osum_step", j - 2))
                A(hsq[j % 2], qkv[:, j, :], ACT.Square).then_inc(*signal("osq", j))
            act.wait_ge(*filled("osum"))
            A(hrs[1][0:40, :], bank("osum")[0:40, :], ACT.Sqrt, bias=epsc[0:40, :], scale=1.0 / HD).then_inc(*read("osum"))

            for m in range(KD):
                act.wait_ge(*copied("mo", m))
                A(fsq[:, m, :], xT[:, m, :], ACT.Square).then_inc(*signal("fsq", m))
            root("2", sroot, ("sum2",), 1.0 / D, epsc)
            act.wait_ge(*done("modA2"))
            for k in range(KD):
                act.wait_ge(*done("xn2", k))
                A(hT[:, k, 0:T], hT[:, k, 0:T], ACT.Identity, scale=modA2[:, k:k + 1], bias=modT[:, 24 + k:25 + k])\
                    .then_inc(*signal("h2", k))
            for k in range(KF):
                act.wait_ge(*filled("fg", k))
                if k >= 2:
                    act.wait_ge(*copied("fu", k - 2))
                A(silug[k % 2], bank("fg", k)[:, :], ACT.Silu).then_inc(*read("fg", k))
            for m in range(KD):
                act.wait_ge(*copied("fd", m))
                A(fsq[:, m, :], xT[:, m, :], ACT.Square).then_inc(*signal("gsq", m))
            root("3", sroot, ("sum3",), 1.0 / D, epsc)
            act.wait_ge(*filled("fu", KF - 1))
            A(hT[:, :, 0:META], hmeta.rearrange("p (k t) -> p k t", k=KD), ACT.Copy).then_inc(*signal("h3meta"))

            H2 = TM // 2

            def both(key, dst, func=ACT.Copy):
                for half in range(2):
                    act.wait_ge(*filled(*key, half))
                    A(dst[:, half * H2:(half + 1) * H2], bank(*key, half)[:, 0:H2], func).then_inc(*read(*key, half))

            for m in range(2):
                both(("pv", m), pv[m])
            for m in range(2):
                act.wait_ge(*filled("pg", m))
                A(pg[:, m, :], bank("pg", m)[:, :], ACT.Silu).then_inc(*read("pg", m))
            for m in range(2):
                if m:
                    act.wait_ge(*copied("cu", 0, 1))
                both(("cgate", m), ga_, ACT.Sigmoid)
            for m in range(2):
                act.wait_ge(*filled("cg", m))
                A(ybr[:, 6 + m, :], bank("cg", m)[:, :], ACT.Silu).then_inc(*read("cg", m))
            for m in range(2):
                act.wait_ge(*filled("bg", m))
                A(bg[:, m, :], bank("bg", m)[:, :], ACT.Copy).then_inc(*read("bg", m))
            for m in range(2):
                both(("cgx", m), cgx[m])
            for m in range(2):
                act.wait_ge(*filled("sg", m))
                A(ybr[:, 8 + m, :], bank("sg", m)[:, :], ACT.Silu).then_inc(*read("sg", m))
            act.wait_ge(*filled("cmean"))
            A(cmr[:, 0, :], bank("cmean")[:, :], ACT.Copy, scale=1.0 / 256).then_inc(*read("cmean"))
            for m in range(2):
                act.wait_ge(*done("ccen", m))
                if m == 0:
                    act.wait_ge(*filled("cmean"))
                A(csq[:, m, :], cacc[:, m, :], ACT.Square).then_inc(*signal("cvar_in", m))
            act.wait_ge(*filled("cvar"))
            A(cmr[:, 1, :], bank("cvar")[:, :], ACT.Sqrt, scale=1.0 / 256, bias=epsc).then_inc(*read("cvar"))
            for m in range(2):
                act.wait_ge(*filled("cq", m))
                A(cq[:, m, :], bank("cq", m)[:, :], ACT.Copy).then_inc(*read("cq", m))
            both(("ckv",), ckv)
            for half in range(2):
                act.wait_ge(*filled("kr", half))
                A(kr[HD:QD, half * H2:(half + 1) * H2], bank("kr", half)[HD:QD, 0:H2], ACT.Copy).then_inc(*read("kr", half))
            for m in range(4):
                act.wait_ge(*filled("mg", m))
                A(ybr[:, 2 + m, :], bank("mg", m)[:, :], ACT.Silu).then_inc(*read("mg", m))
            for m in range(2):
                act.wait_ge(*done("cnorm", m))
                A(cacc[:, m, :], cacc[:, m, :], ACT.Silu, scale=V1[:, V1_ROWS["ln_g"] + m:V1_ROWS["ln_g"] + m + 1],
                  bias=V1[:, V1_ROWS["ln_b"] + m:V1_ROWS["ln_b"] + m + 1]).then_inc(*signal("csilu", m))
            for k in range(2):
                act.wait_ge(*copied("cq", k))
                A(qsw[:, k, :], cq[:, k, :], ACT.Square).then_inc(*signal("cqsq", k))
            act.wait_ge(*copied("ckv", 1))
            A(ksq, ckv, ACT.Square).then_inc(*signal("ckvsq"))
            act.wait_ge(*filled("cqsum"))
            A(rqm, bank("cqsum")[:, 0:4], ACT.Sqrt, scale=float(QD) / 256, bias=eps96).then_inc(*read("cqsum"))
            for half in range(2):
                act.wait_ge(*filled("kvsum", half))
                A(krb[:, half * H2:(half + 1) * H2], bank("kvsum", half)[:, 0:H2], ACT.Sqrt, scale=1.0 / P, bias=epsc)\
                    .then_inc(*read("kvsum", half))
            for k in range(2):
                act.wait_ge(*copied("py", k))
                act.wait_ge(*done("yc", k))
                act.wait_ge(*done("yd", k))
            for h in range(8):
                act.wait_ge(*filled("q", h))
                A(qh[0:QD, h, :], bank("q", h)[0:QD, :], ACT.Copy).then_inc(*read("q", h))
            for h in range(8):
                for half in range(2):
                    act.wait_ge(*filled("k", h, half))
                    A(kh[0:HD, h, half * H2:(half + 1) * H2], bank("k", h, half)[0:HD, 0:H2], ACT.Copy)\
                        .then_inc(*read("k", h, half))
            for b in range(5):
                n = P if b < 4 else META
                act.wait_ge(*filled("v", b))
                if b == 4:
                    act.wait_ge(*done("vpad"))
                A(vv[0:n, b, :], bank("v", b)[0:n, :], ACT.Copy).then_inc(*read("v", b))

            act.wait_ge(*done("rqm"))

            def ml_in(u):
                i, h = MLU[u]
                n = keys_of[i]
                m0 = min(n, 512)
                if u >= 2:
                    act.wait_ge(*done("mexp", u - 2))
                act.wait_ge(*filled("ms", u))
                A(msc[u % 2][:, 0:m0], bank("ms", u)[:, 0:m0], ACT.Copy, scale=rqm[:, i:i + 1]).then_inc(*read("ms", u))
                if n > 512:
                    act.wait_ge(*filled("ms2", u))
                    A(msc[u % 2][:, 512:n], bank("ms2", u)[:, 0:n - 512], ACT.Copy, scale=rqm[:, i:i + 1])\
                        .then_inc(*read("ms2", u))

            def ml_exp(u):
                i, h = MLU[u]
                n = keys_of[i]
                act.wait_ge(*done("mmax", u))
                if u >= 2:
                    act.wait_ge(*filled("mr", u - 2))
                c = u % 16
                A(mpr[u % 2][:, 0:n], msc[u % 2][:, 0:n], ACT.Exp, bias=snmax[:, c:c + 1], accum_out=ssumx[:, c:c + 1])\
                    .then_inc(*signal("mexp", u))

            def ml_copy(u):
                i, h = MLU[u]
                act.wait_ge(*filled("mt", u))
                if u >= 2:
                    i2, h2 = MLU[u - 2]
                    act.wait_ge(*(filled("mo2", i2) if h2 == 7 else done("mo_step", u - 2)))
                A(mpT[u % 2][:, 0:(i + 1) * WIN], bank("mt", u)[:, 0:(i + 1) * WIN], ACT.Copy).then_inc(*read("mt", u))
                act.wait_ge(*filled("mr", u))
                if u < 2:
                    act.wait_ge(*done("vpad"))
                A(mpR[u % 2][0:META, :], bank("mr", u)[0:META, 0:WIN], ACT.Copy).then_inc(*read("mr", u))

            for u in range(len(MLU) + 2):
                if u < len(MLU):
                    ml_in(u)
                if 1 <= u <= len(MLU):
                    ml_exp(u - 1)
                if u >= 2:
                    ml_copy(u - 2)

            for m in range(KD):
                for b in range(4):
                    x = 4 * m + b
                    if x >= 2:
                        act.wait_ge(*copied("y", (x - 2) // 4, (x - 2) % 4))
                    act.wait_ge(*filled("gl", m, b))
                    c = V1_ROWS["gate_bias"] + 8 * b + m
                    A(sg[x % 2], bank("gl", m, b)[:, :], ACT.Sigmoid, bias=V1[:, c:c + 1]).then_inc(*read("gl", m, b))
            for b in range(4):
                for half in range(2):
                    act.wait_ge(*filled("xt", b, half))
                    A(xtok[:, b, half * 512:(half + 1) * 512], bank("xt", b, half)[:, :], ACT.Copy)\
                        .then_inc(*read("xt", b, half))
            for b in range(4):
                for half in range(2):
                    if b or half:
                        act.wait_ge(*done("fss", b - 1 if half == 0 else b, 1 - half))
                    act.wait_ge(*filled("fo", b, half))
                    A(fjunk[:, 0:512], bank("fo", b, half)[:, :], ACT.Square, accum_out=fss[:, 2 * b + half:2 * b + half + 1])\
                        .then_inc(*signal("fss", b, half))
                act.wait_ge(*done("ftot", b))
                A(frs[:, b:b + 1], fss[:, 2 * b:2 * b + 1], ACT.Sqrt, scale=1.0 / D, bias=epsc).then_inc(*signal("froot", b))
                act.wait_ge(*done("fin", b))
                act.dma_start(out[0].rearrange("(b p) f -> b p f", p=P)[b], fin[b]).then_inc(sem("stored"), 16)

        @block.vector
        def _(dve):
            v = nc.vector
            chain = [0]

            def link(ins):
                chain[0] += 1
                ins.then_inc(sem("dve_chain"), 1)
                dve.wait_ge(sem("dve_chain"), chain[0])

            def col(name, i=0, n=1):
                r = V1_ROWS[name] + i
                return V1[:, r:r + n]

            tt, ts, stt = v.tensor_tensor, v.tensor_scalar, v.scalar_tensor_tensor

            link(v.memset(gates, 0.0))
            v.memset(epsc, EPS)
            v.memset(eps64, EPS * HD)
            v.memset(eps96, EPS * QD).then_inc(*signal("eps"))
            for k in range(KD):
                dve.wait_ge(*copied("x", k))
                tt(nsq[:, k, :], xT[:, k, :], xT[:, k, :], ALU.mult).then_inc(*signal("nsq", k))
            dve.wait_ge(*copied("meta"))
            tt(msq, hmeta, hmeta, ALU.mult).then_inc(*signal("msq"))

            def spread(tag, dg):
                dve.wait_ge(*copied("sum" + tag))
                link(v.reciprocal(srstd, sroot))
                for b in range(4):
                    last = ts(dg[:, b, :], ident, srstd[:, b:b + 1], None, ALU.mult)
                    last.then_inc(*(signal("diag" + tag) if b == 3 else signal("diag_part" + tag)))

            spread("1", diag)
            dve.wait_ge(*copied("summeta"))
            link(v.reciprocal(msum[0:META, 1:2], msum[0:META, 0:1]))
            ts(rbc[0:META, 0:META], ident[0:META, 0:META], msum[0:META, 1:2], None, ALU.mult)\
                .then_inc(*signal("diagmeta"))
            hm = hmeta.rearrange("p (k t) -> p k t", k=KD)
            dve.wait_ge(*filled("spreadmeta"))
            for k in range(KD):
                last = stt(out=hm[:, k, :], in0=hm[:, k, :], scalar=col("pre", k), in1=bank("spreadmeta")[:, 0:META],
                           op0=ALU.mult, op1=ALU.mult)
                last.then_inc(*(read("spreadmeta") if k == KD - 1 else signal("hmeta", k)))

            dve.wait_ge(*done("cs"))

            def ada_sum(i):
                dve.wait_ge(*loaded(f"ada{i}"))
                if i >= 2:
                    dve.wait_ge(*filled("ada", i - 2))
                acc, w = adaacc[i % 2], W(f"ada{i}")
                link(ts(acc, w[:, 0, :], cs[:, 0:1], None, ALU.mult))
                for k in range(1, KD):
                    last = stt(out=acc, in0=w[:, k, :], scalar=cs[:, k:k + 1], in1=acc, op0=ALU.mult, op1=ALU.add)
                    if k < KD - 1:
                        link(last)
                last.then_inc(*signal("adaacc", i))

            def ada_mod(i):
                dve.wait_ge(*filled("ada", i))
                tt(modT[:, 4 * i:4 * i + 4], bank("ada", i)[:, 0:4], col("b_ada", 4 * i, 4), ALU.add)\
                    .then_inc(*read("ada", i))

            for i in range(4):
                ada_sum(i)
                if i:
                    ada_mod(i - 1)
            ada_mod(3)
            dve.wait_ge(*copied("ada", 3))
            stt(out=modA1, in0=modT[:, 8:16], scalar=1.0, in1=col("norm1", 0, 8), op0=ALU.add, op1=ALU.mult)\
                .then_inc(*signal("modA1"))

            def normed(tag, stage):
                dve.wait_ge(*filled("spread" + tag))
                for k in range(KD):
                    ins = tt(hT[:, k, 0:T], xT[:, k, :], bank("spread" + tag)[:, :], ALU.mult)
                    ins.then_inc(*signal(stage, k))
                dve.wait_ge(*done(stage, KD - 1))
                v.engine_nop().then_inc(*read("spread" + tag))

            normed("1", "xn1")
            dve.wait_ge(*copied("spreadmeta"))
            for i in range(2):
                v.memset(raw[i][:, 0:3], 0.0)
            v.memset(raw[2][:, 0:3], 0.0).then_inc(*signal("rawpad"))

            def conv4(m):
                dve.wait_ge(*copied("pj", m))
                tap = lambda k: V2[:, 12 * k + m:12 * k + m + 1]
                ts(qkv[:, m, :], raw[m % 3][:, 0:T], tap(0), None, ALU.mult).then_inc(*signal("conv", m, 0))
                for k in range(1, 4):
                    dve.wait_ge(*done("conv", m, k - 1))
                    stt(out=qkv[:, m, :], in0=raw[m % 3][:, k:k + T], scalar=tap(k), in1=qkv[:, m, :],
                        op0=ALU.mult, op1=ALU.add).then_inc(*signal("conv", m, k))

            for i in range(3):
                for m in range(4 * i, 4 * i + 4):
                    conv4(m)
                ada_sum(4 + i)
                ada_mod(4 + i)
            dve.wait_ge(*copied("ab"))
            dve.wait_ge(*arrived("gate", 3))
            link(ts(gt[1][0:8, :], gt[3][0:8, :], dtb[0:8, :], None, ALU.add))
            stt(out=gt[2][0:8, :], in0=gt[1][0:8, :], scalar=-1.0, in1=gt[1][0:8, :], op0=ALU.mult, op1=ALU.min)\
                .then_inc(*signal("nabs"))
            for i in range(7, 12):
                ada_sum(i)
                ada_mod(i)
            dve.wait_ge(*copied("ada", 11))
            stt(out=modA2, in0=modT[:, 32:40], scalar=1.0, in1=col("norm2", 0, 8), op0=ALU.add, op1=ALU.mult)\
                .then_inc(*signal("modA2"))
            dve.wait_ge(*copied("hsum"))
            link(v.reciprocal(grow_[0:40, :], hrs[0][0:40, :]))
            link(ts(grow_[0:8, :], grow_[0:8, :], float(HD) ** -0.5, None, ALU.mult))
            dve.wait_ge(*copied("sksum"))
            link(v.reciprocal(hrs[1], hrs[1]))
            link(tt(wqk, col("qn"), col("kn"), ALU.mult))
            dve.wait_ge(*copied("sk"))
            stt(out=sk, in0=sk, scalar=wqk, in1=hrs[1], op0=ALU.mult, op1=ALU.mult).then_inc(*signal("skn"))
            dve.wait_ge(*copied("sqsum"))
            link(v.reciprocal(rq, rq))
            dve.wait_ge(*done("egb"))
            link(ts(gt[0][32:40, :], gt[0][32:40, :], 1.0, None, ALU.add))
            link(v.reciprocal(gt[0][32:40, :], gt[0][32:40, :]))
            link(v.tensor_copy(grow_[64:72, :], gt[0][32:40, :]))
            link(tt(glog[32:40, :], gt[0][32:40, :], grow_[32:40, :], ALU.mult))
            dve.wait_ge(*done("lnabs"))
            dve.wait_ge(*done("ealog"))
            link(ts(gt[1][0:8, :], gt[1][0:8, :], 0.0, None, ALU.max))
            link(tt(gt[1][0:8, :], gt[1][0:8, :], gt[2][0:8, :], ALU.add))
            link(ts(gt[1][0:8, :], gt[1][0:8, :], nega[0:8, :], -1.0, ALU.mult, ALU.mult))
            v.tensor_tensor_scan(glog[0:8, :], cst("reset", 8), gt[1][0:8, :], 0.0, ALU.mult, ALU.add)\
                .then_inc(*signal("grows"))

            dve.wait_ge(*arrived("alibi"))

            def sw_bias(u):
                b, hp = SWU[u]
                wk = WIN if b == 0 else 2 * WIN
                dve.wait_ge(*filled("ss", u))
                if u >= 2:
                    dve.wait_ge(*done("sexp", u - 2, 1))
                for p in range(2):
                    h = 2 * hp + p
                    al = alibi[:, h * 2 * WIN + (2 * WIN - wk):(h + 1) * 2 * WIN]
                    ins = stt(out=sc[u % 2][:, p * wk:(p + 1) * wk], in0=bank("ss", u)[:, p * wk:(p + 1) * wk],
                              scalar=rq[:, b * 8 + h:b * 8 + h + 1], in1=al, op0=ALU.mult, op1=ALU.add)
                    ins.then_inc(*(read("ss", u) if p else signal("sbias", u)))
                dve.wait_ge(*copied("ss", u))
                s2 = 2 * (u % 8)
                link(v.reduce_max(smax[:, s2:s2 + 2], sc[u % 2][:, 0:2 * wk].rearrange("p (h k) -> p h k", h=2), AX.X))
                link(tt(smax[:, s2:s2 + 2], smax[:, s2:s2 + 2], sinks[:, 2 * hp:2 * hp + 2], ALU.max))
                link(ts(snmax[:, s2:s2 + 2], smax[:, s2:s2 + 2], -1.0, None, ALU.mult))
                tt(sesk[:, s2:s2 + 2], sinks[:, 2 * hp:2 * hp + 2], snmax[:, s2:s2 + 2], ALU.add)\
                    .then_inc(*signal("snmax", u))

            def sw_sum(u):
                s2 = 2 * (u % 8)
                dve.wait_ge(*done("sexp", u, 1))
                dve.wait_ge(*done("sesk", u))
                link(tt(sden[:, s2:s2 + 2], ssumx[:, s2:s2 + 2], sesk[:, s2:s2 + 2], ALU.add))
                v.reciprocal(sden[:, s2:s2 + 2], sden[:, s2:s2 + 2]).then_inc(*signal("srec", u))

            for u in range(len(SWU) + 1):
                if u < len(SWU):
                    sw_bias(u)
                if u:
                    sw_sum(u - 1)

            v4 = lambda t: t.rearrange("p (n c) -> p n c", n=4)
            v8 = lambda t: t.rearrange("p (n c) -> p n c", n=NC)
            over_c = lambda c: c.unsqueeze(2).broadcast_to([P, NC, CH])
            colv = cols.rearrange("p (n s j) -> p n s j", n=NC, s=4)
            mask64 = lambda name: cst(name).unsqueeze(1).broadcast_to([P, NC, CH])
            mask4 = lambda name: cst(name).unsqueeze(1).broadcast_to([P, 4, P])
            dve.wait_ge(*filled("so", NB - 1))
            link(v.memset(blk[0], 0.0))
            v.memset(blk[1], 0.0).then_inc(*signal("bdzero"))
            dve.wait_ge(*copied("cols"))
            for j in range(NJ):
                gcolj, brkj, rkj, betaj = (colv[:, :, s, j] for s in range(4))
                dve.wait_ge(*copied("rows", j, 0))
                link(tt(e_, g_row, over_c(gcolj), ALU.subtract))
                ts(e_, e_, 0.0, None, ALU.min).then_inc(*signal("emin", j))
                tt(cB, g_row[:, :, CH - 1], gcolj, ALU.subtract).then_inc(*signal("cBarg", j))
                dve.wait_ge(*done("e", j))
                link(tt(e_, e_, over_c(rkj), ALU.mult))
                dve.wait_ge(*filled("rows", j, 1))
                tt(w1, e_, v8(bank("rows", j, 1)[:, :]), ALU.mult).then_inc(*read("rows", j, 1))
                dve.wait_ge(*copied("rows", j, 1))
                link(tt(w1, w1, mask64("strictT"), ALU.mult))
                dve.wait_ge(*filled("rows", j, 2))
                link(tt(w2, e_, v8(bank("rows", j, 2)[:, :]), ALU.mult))
                link(tt(w2, w2, mask64("inclT"), ALU.mult))
                dve.wait_ge(*done("gx", j))
                tt(qe, gx, v8(bank("rows", j, 2)[:, :]), ALU.mult).then_inc(*read("rows", j, 2))
                dve.wait_ge(*copied("rows", j, 2))
                tt(qe, qe, v8(qkv[:, j, :]), ALU.mult).then_inc(*signal("qe", j))
                for half in range(2):
                    dve.wait_ge(*filled("kk", j, half))
                    w = w1[:, 4 * half:4 * half + 4, :].unsqueeze(2).broadcast_to([P, 4, 2, CH])
                    tt(blk[2][:, 4 * half:4 * half + 4, :].rearrange("p n (h c) -> p n h c", h=2),
                       bank("kk", j, half)[:, :].rearrange("p (n h c) -> p n h c", n=4, h=2), w, ALU.mult)\
                        .then_inc(*read("kk", j, half))
                dve.wait_ge(*filled("kq", j))
                tt(qkw, v8(bank("kq", j)[:, :]), w2, ALU.mult).then_inc(*read("kq", j))
                for half in range(2):
                    dve.wait_ge(*filled("tA", j, half))
                    src = v4(bank("tA", j, half)[:, :])
                    for i, (dst, name) in enumerate(((blk[5], "m16"), (blk[6], "m32"), (blk[7], "m64"))):
                        ins = tt(dst[:, 4 * half:4 * half + 4, :], src, mask4(name), ALU.mult)
                        ins.then_inc(*(read("tA", j, half) if i == 2 else signal("tA_part", j, half, i)))

                def add(name, op=ALU.add):
                    for half in range(2):
                        dve.wait_ge(*filled(name, j, half))
                        d = blk[4][:, 4 * half:4 * half + 4, :]
                        tt(d, d, v4(bank(name, j, half)[:, :]), op).then_inc(*read(name, j, half))

                def scaled(name, parts):
                    for half in range(2):
                        dve.wait_ge(*filled(name, j, half))
                        src = v4(bank(name, j, half)[:, :])
                        for i, (dst, c) in enumerate(parts):
                            ins = tt(dst[:, 4 * half:4 * half + 4, :], src,
                                     c[:, 4 * half:4 * half + 4].unsqueeze(2).broadcast_to([P, 4, P]), ALU.mult)
                            ins.then_inc(*(read(name, j, half) if i == len(parts) - 1 else signal(name + "_part", j, half)))

                dve.wait_ge(*done("p0", j))
                add("p1")
                dve.wait_ge(*done("cBexp", j))
                link(tt(cA, cA, brkj, ALU.mult))
                link(tt(cB, cB, rkj, ALU.mult))
                scaled("kt", ((blk[8], cA), (blk[0], cB)))
                scaled("vt", ((blk[1], betaj),))
                add("p2")
                add("p3")
                add("i32", ALU.subtract)
                add("i64", ALU.subtract)
                dve.wait_ge(*done("eglast", j))
                for n in range(NC - 1):
                    dve.wait_ge(*filled("su", j, n))
                    ps = bank("su", j, n)[:, 0:P]
                    if n == 0:
                        v.tensor_copy(state, ps).then_inc(*read("su", j, n))
                    else:
                        dve.wait_ge(*copied("su", j, n - 1))
                        stt(out=state, in0=state, scalar=eglast[:, n:n + 1], in1=ps, op0=ALU.mult, op1=ALU.add)\
                            .then_inc(*read("su", j, n))
            dve.wait_ge(*copied("osum"))
            v.reciprocal(hrs[1][0:40, :], hrs[1][0:40, :]).then_inc(*signal("orow"))
            for j in range(NJ):
                dve.wait_ge(*filled("ospread", j))
                stt(out=qkv[:, j, :], in0=qkv[:, j, :], scalar=col("gdn_norm"), in1=bank("ospread", j)[:, :],
                    op0=ALU.mult, op1=ALU.mult).then_inc(*read("ospread", j))
                dve.wait_ge(*copied("ospread", j))
                tt(qkv[:, j, :], qkv[:, j, :], gz[:, j, :], ALU.mult).then_inc(*signal("mixg", j))

            def residual(key, m, gate):
                dve.wait_ge(*filled(key, m))
                stt(out=xT[:, m, :], in0=bank(key, m)[:, :], scalar=modT[:, gate + m:gate + m + 1], in1=xT[:, m, :],
                    op0=ALU.mult, op1=ALU.add).then_inc(*read(key, m))

            for m in range(KD):
                residual("mo", m, 16)
            spread("2", fdiag)
            normed("2", "xn2")
            for k in range(KF):
                dve.wait_ge(*copied("fg", k))
                dve.wait_ge(*filled("fu", k))
                tt(aT[:, k, :], bank("fu", k)[:, :], silug[k % 2], ALU.mult).then_inc(*read("fu", k))
            for m in range(KD):
                residual("fd", m, 40)
            spread("3", fdiag)
            dve.wait_ge(*filled("spread3"))
            dve.wait_ge(*filled("fu", KF - 1))
            for k in range(KD):
                stt(out=hT[:, k, META:TM], in0=xT[:, k, :], scalar=col("pre", k), in1=bank("spread3")[:, :],
                    op0=ALU.mult, op1=ALU.mult).then_inc(*signal("h3", k))
            dve.wait_ge(*done("h3", KD - 1))
            v.engine_nop().then_inc(*read("spread3"))

            H2 = TM // 2
            v.memset(zc[0][:, 0:30], 0.0)
            v.memset(zc[1][:, 0:30], 0.0)
            v.memset(uu[0][:, 0:2], 0.0)
            link(v.memset(uu[1][:, 0:2], 0.0))
            lo, hi = slice(0, HD), slice(HD, P)

            def shifted(dst, src, by, first, rows=slice(0, P)):
                link(tt(dst[rows, first:TM], src[rows, first:TM], src[rows, first - by:TM - by], ALU.add))

            def pooled(m, rows, src):
                return stt(out=pw[m][rows, META:TM], in0=src[rows, META:TM],
                           scalar=cst("invw")[rows, m:m + 1], in1=pv[m][rows, META:TM], op0=ALU.mult, op1=ALU.subtract)

            for m in range(2):
                dve.wait_ge(*copied("pv", m, 1))
                shifted(pw[m], pv[m], 1, 1)
                if m == 0:
                    shifted(pw[2], pw[0], 2, 3, hi)
                else:
                    shifted(pw[2], pw[1], 2, 3)
                    shifted(pw[1], pw[2], 4, 7)
                    shifted(pw[2], pw[1], 8, 15, hi)
                link(pooled(m, lo, pw[m]))
                pooled(m, hi, pw[2]).then_inc(*signal("pool", m))
                dve.wait_ge(*done("pool", m))
            for m in range(2):
                for half in range(2):
                    dve.wait_ge(*copied("cgate", m, half))
                    dve.wait_ge(*filled("cu", m, half))
                    tt(zc[m][:, 30 + half * H2:30 + (half + 1) * H2], bank("cu", m, half)[:, 0:H2],
                       ga_[:, half * H2:(half + 1) * H2], ALU.mult).then_inc(*read("cu", m, half))
            for m in range(2):
                dve.wait_ge(*filled("py", m))
                dve.wait_ge(*copied("pg", m))
                stt(out=ybr[:, m, :], in0=bank("py", m)[:, :], scalar=col("pool_scale", m), in1=pg[:, m, :],
                    op0=ALU.mult, op1=ALU.mult).then_inc(*read("py", m))

            for m in range(2):
                for half in range(2):
                    dve.wait_ge(*copied("cgx", m, half))
                    dve.wait_ge(*filled("xv", m, half))
                    tt(uu[m][:, 2 + half * H2:2 + (half + 1) * H2], bank("xv", m, half)[:, 0:H2],
                       cgx[m][:, half * H2:(half + 1) * H2], ALU.mult).then_inc(*read("xv", m, half))
            for m in range(2):
                dve.wait_ge(*copied("xv", m, 1))
                acc = cgx[m][:, 0:T]
                for k in range(SC_K):
                    tap = V2[:, V2_ROWS["sc"] + 2 * k + m:V2_ROWS["sc"] + 2 * k + m + 1]
                    src = uu[m][:, META + k:META + k + T]
                    link(ts(acc, src, tap, None, ALU.mult) if k == 0 else
                         stt(out=acc, in0=src, scalar=tap, in1=acc, op0=ALU.mult, op1=ALU.add))
                dve.wait_ge(*copied("bg", m))
                link(tt(acc, acc, bg[:, m, :], ALU.mult))
                dve.wait_ge(*copied("sg", m))
                tt(ybr[:, 8 + m, :], ybr[:, 8 + m, :], acc, ALU.mult).then_inc(*signal("yd", m))
            for k in range(CONF_K):
                for m in range(2):
                    if k == 0:
                        dve.wait_ge(*copied("cu", m, 1))
                    else:
                        dve.wait_ge(*done("cmean_in" if k == CONF_K else "cconv", k - 1, m))
                    tap = V2[:, V2_ROWS["conf"] + 2 * k + m:V2_ROWS["conf"] + 2 * k + m + 1]
                    src = zc[m][:, META + k:META + k + T]
                    ins = (ts(cacc[:, m, :], src, tap, col("conf_b", m), ALU.mult, ALU.add) if k == 0 else
                           stt(out=cacc[:, m, :], in0=src, scalar=tap, in1=cacc[:, m, :], op0=ALU.mult, op1=ALU.add))
                    ins.then_inc(*(signal("cmean_in", m) if k == CONF_K - 1 else signal("cconv", k, m)))
            dve.wait_ge(*copied("cmean"))
            for m in range(2):
                tt(cacc[:, m, :], cacc[:, m, :], cmr[:, 0, :], ALU.subtract).then_inc(*signal("ccen", m))
            dve.wait_ge(*copied("cvar"))
            link(v.reciprocal(cmr[:, 1, :], cmr[:, 1, :]))
            for m in range(2):
                dve.wait_ge(*done("cvar_in", m))
                tt(cacc[:, m, :], cacc[:, m, :], cmr[:, 1, :], ALU.mult).then_inc(*signal("cnorm", m))
            for m in range(2):
                dve.wait_ge(*done("csilu", m))
                tt(ybr[:, 6 + m, :], ybr[:, 6 + m, :], cacc[:, m, :], ALU.mult).then_inc(*signal("yc", m))
            for k in range(2):
                dve.wait_ge(*done("cqsq", k))
                ts(cq[:, k, :], cq[:, k, :], col("q_norm", k), None, ALU.mult).then_inc(*signal("cqg", k))
            dve.wait_ge(*done("ckvsq"))
            for half in range(2):
                dve.wait_ge(*copied("kvsum", half))
            link(v.reciprocal(krb, krb))
            stt(out=ckv, in0=ckv, scalar=col("kv_norm"), in1=krb, op0=ALU.mult, op1=ALU.mult).then_inc(*signal("ckvn"))
            dve.wait_ge(*copied("cqsum"))
            v.reciprocal(rqm, rqm).then_inc(*signal("rqm"))
            for k in range(2):
                dve.wait_ge(*done("yc", k))
            v.memset(mpR[0], 0.0)
            v.memset(mpR[1], 0.0)
            v.memset(vv[:, 4, :], 0.0).then_inc(*signal("vpad"))
            r3 = slice(HD, QD)
            dve.wait_ge(*arrived("rope"))
            dve.wait_ge(*arrived("krs", 2))
            link(tt(kr[r3, :], kr[r3, :], rope[r3, 0, :], ALU.mult))
            link(tt(krs[r3, :], krs[r3, :], rope[r3, 1, :], ALU.mult))
            tt(kh[r3, :, :], kr[r3, :].unsqueeze(1).broadcast_to([QK_ROPE, 8, TM]),
               krs[r3, :].unsqueeze(1).broadcast_to([QK_ROPE, 8, TM]), ALU.add).then_inc(*signal("krope"))
            for g in range(4):
                q2 = qh[r3, 2 * g:2 * g + 2, :]
                dve.wait_ge(*arrived("qsw", 2 * (g + 1)))
                cs2 = [rope[r3, s, META:TM].unsqueeze(1).broadcast_to([QK_ROPE, 2, T]) for s in range(2)]
                link(tt(q2, q2, cs2[0], ALU.mult))
                link(tt(qsw[r3, :, :], qsw[r3, :, :], cs2[1], ALU.mult))
                tt(q2, q2, qsw[r3, :, :], ALU.add).then_inc(*signal("qrope", g))
                dve.wait_ge(*done("qrope", g))

            def ml_max(u):
                i, h = MLU[u]
                n = keys_of[i]
                dve.wait_ge(*copied("ms2" if n > 512 else "ms", u))
                s, c = msc[u % 2], u % 16
                link(tt(s[:, n - WIN:n], s[:, n - WIN:n], cst("causal"), ALU.add))
                link(v.reduce_max(smax[:, c:c + 1], s[:, 0:n], AX.X))
                ts(snmax[:, c:c + 1], smax[:, c:c + 1], -1.0, None, ALU.mult).then_inc(*signal("mmax", u))

            def ml_rec(u):
                i, h = MLU[u]
                c = u % 16
                dve.wait_ge(*done("mexp", u))
                v.reciprocal(sden[:, c:c + 1], ssumx[:, c:c + 1]).then_inc(*signal("mrec", u))

            for u in range(len(MLU) + 3):
                if u >= 3 and MLU[u - 3][1] == 7:
                    i = MLU[u - 3][0]
                    dve.wait_ge(*filled("mo2", i))
                    for pair in range(4):
                        dve.wait_ge(*copied("mg", pair))
                    y = ybr[:, 2:6, i * WIN:(i + 1) * WIN]
                    tt(y, bank("mo2", i)[:, :].rearrange("p (h t) -> p h t", h=4), y, ALU.mult)\
                        .then_inc(*read("mo2", i))
                if u < len(MLU):
                    ml_max(u)
                if 1 <= u <= len(MLU):
                    ml_rec(u - 1)
            for m in range(KD):
                for b in range(4):
                    x = 4 * m + b
                    dve.wait_ge(*copied("gl", m, b))
                    dve.wait_ge(*filled("y", m, b))
                    dst = mT[:, m, :] if b == 0 else prod[b % 2]
                    tt(dst, bank("y", m, b)[:, :], sg[x % 2], ALU.mult).then_inc(*read("y", m, b))
                    dve.wait_ge(*copied("y", m, b))
                    if b:
                        ins = tt(mT[:, m, :], mT[:, m, :], prod[b % 2], ALU.add)
                        if b < 3:
                            link(ins)
                        else:
                            ins.then_inc(*signal("mT", m))
            dve.wait_ge(*arrived("post"))
            for b in range(4):
                for half in range(2):
                    dve.wait_ge(*copied("xt", b, half))
                dve.wait_ge(*done("fss", b, 1))
                tt(fss[:, 2 * b:2 * b + 1], fss[:, 2 * b:2 * b + 1], fss[:, 2 * b + 1:2 * b + 2], ALU.add)\
                    .then_inc(*signal("ftot", b))
                dve.wait_ge(*done("froot", b))
                link(v.reciprocal(frs[:, 4 + b:5 + b], frs[:, b:b + 1]))
                for half in range(2):
                    c = slice(512 * half, 512 * half + 512)
                    f = fin[b][:, c]
                    stt(out=f, in0=bank("fo", b, half)[:, :], scalar=frs[:, 4 + b:5 + b], in1=post[:, c],
                        op0=ALU.mult, op1=ALU.mult).then_inc(*read("fo", b, half))
                    dve.wait_ge(*copied("fo", b, half))
                    tt(f, f, xtok[:, b, c], ALU.add).then_inc(*(signal("fin", b) if half else signal("fin_half", b)))

    counted["tiles"] = tiles
    return counted


_INS = ["x", "c", "w_ada", "b_ada", "norm1_w", "w_in", "conv_w", "a_log", "dt_bias", "gdn_norm_w", "q_norm_w",
        "k_norm_w", "sinks", "w_out", "norm2_w", "w_gate", "w_up", "w_down", "meta_tokens_2", "pre_norm_g_2",
        "w_in_2", "gate_bias_2", "pool_w_2", "pool_scale_2", "w_out_pool_2", "q_norm_g_2", "w_uq_2", "kv_norm_g_2",
        "w_ukv_2", "w_out_mla_2", "conf_dw_w_2", "conf_dw_b_2", "conf_ln_g_2", "conf_ln_b_2", "w_out_conf_2",
        "sc_dw_w_2", "w_out_sc_2", "w_o_2", "post_norm_g_2"]


def kernel(**inputs):
    import concourse.bacc as _bacc
    from concourse.bass_utils import run_bass_kernel_spmd as _run

    consts, alibi, rope = shape_constants()
    arrays = {f"in_{name}_dram": np.ascontiguousarray(inputs[name]) for name in _INS}
    arrays |= {"in_consts_dram": consts, "in_alibi_dram": alibi, "in_rope_dram": rope}

    def build(known):
        nc = _bacc.Bacc("TRN2", target_bir_lowering=False, num_devices=1)
        aps = {n[3:-5]: nc.dram_tensor(n, v.shape, mybir.dt.from_np(v.dtype), kind="ExternalInput").ap()
               for n, v in arrays.items()}
        o = nc.dram_tensor("out_0_dram", (1, T, D), F32, kind="ExternalOutput").ap()
        return nc, program(nc, aps, o, known)

    nc, _ = build(build(None)[1])
    return _run(nc, [arrays], core_ids=[0]).results[0]["out_0_dram"]
```

```python
from contextlib import ExitStack

import numpy as np

import concourse.bass as bass
from concourse import mybir

F32 = mybir.dt.float32
F32R = mybir.dt.float32r
ALU = mybir.AluOpType
ACT = mybir.ActivationFunctionType
AX = mybir.AxisListType

P = 128
D = 1024
KD = D // P
T = 512
META = 16
TM = T + META
HD = 64
GH = 8
NJ = GH // 2
CH = 64
NC = T // CH
WIN = 128
NB = T // WIN
FF = 2816
KF = FF // P
FFN_PARTS = ((0, 12), (12, 10))
EPS = 1e-6
QK_NOPE, QK_ROPE, V_DIM = 64, 32, 64
QD = QK_NOPE + QK_ROPE
CONF_K = 31
SC_K = 3
NEG = -1e30

CONST_W = {}
_at = 0
for _name, _w in (("ident", 128), ("ones", 128), ("onesbd", 128), ("m16", 128), ("m16T", 128), ("m32", 128),
                  ("m64", 128), ("strictT", 64), ("inclT", 64), ("stack", 64), ("sel", 512), ("pick", 4 * 40 * 2),
                  ("two", 2), ("reset", 512), ("invw", 2), ("causal", 128)):
    CONST_W[_name] = (_at, _w)
    _at += _w
CONST_COLS = _at

V1_ROWS = {"b_ada": 0, "norm1": 48, "norm2": 56, "pre": 64, "gate_bias": 72, "conf_b": 104, "ln_g": 106,
           "ln_b": 108, "pool_scale": 110, "q_norm": 112, "kv_norm": 114, "gdn_norm": 115, "qn": 116, "kn": 117,
           "c": 118}
V1_N = 126
V2_ROWS = {"conv": 0, "conf": 48, "sc": 110}
V2_N = 116


def shape_constants():
    c = np.zeros((P, CONST_COLS), np.float32)

    def put(name, a):
        o, w = CONST_W[name]
        c[:a.shape[0], o:o + w] = a.reshape(a.shape[0], -1)

    r = np.arange(P)
    head, tok = r // 64, r % 64
    same = head[:, None] == head[None, :]
    lower = tok[:, None] > tok[None, :]
    b16 = tok[:, None] // 16 == tok[None, :] // 16
    b32 = tok[:, None] // 32 == tok[None, :] // 32
    put("ident", np.eye(P))
    put("ones", np.ones((P, P)))
    put("onesbd", same)
    put("m16", same & lower & b16)
    put("m16T", (same & lower & b16).T)
    put("m32", same & lower & b32 & ~b16)
    put("m64", same & lower & ~b32)
    t = np.arange(64)
    put("strictT", t[None, :] > tok[:, None])
    put("inclT", t[None, :] >= tok[:, None])
    put("stack", t[None, :] == tok[:, None])
    sel = np.zeros((40, NJ, P))
    pick = np.zeros((P, 2, NJ, 40))
    for j in range(NJ):
        for h in (0, 1):
            sel[2 * j + h, j, 64 * h:64 * h + 64] = 1
            sel[32 + 2 * j + h, j, 64 * h:64 * h + 64] = 1
            pick[64 * h:64 * h + 64, 0, j, 2 * j + h] = 1
            pick[64 * h:64 * h + 64, 1, j, 32 + 2 * j + h] = 1
    put("sel", sel)
    put("pick", pick)
    two = np.zeros((P, 2))
    two[:64, 0] = 1
    two[64:, 1] = 1
    put("two", two)
    reset = np.ones((P, T))
    reset[:, ::CH] = 0
    put("reset", reset)
    w = np.zeros((P, 2))
    w[:64, 0], w[64:, 0], w[:64, 1], w[64:, 1] = 1 / 2, 1 / 4, 1 / 8, 1 / 16
    put("invw", w)
    put("causal", np.where(r[None, :] <= r[:, None], 0.0, NEG))

    slopes = 2.0 ** (-8.0 * (np.arange(8, dtype=np.float32) + 1.0) / 8)
    dist = (r[:, None] + WIN - np.arange(2 * WIN)[None, :]).astype(np.float32)
    inside = (dist >= 0) & (dist < WIN)
    alibi = np.where(inside[:, None, :], -slopes[None, :, None] * dist[:, None, :], NEG)
    inv = (1.0 / (np.float32(10000.0) ** (np.arange(0, QK_ROPE, 2, dtype=np.float32) / QK_ROPE))).astype(np.float32)
    ang = inv[:, None] * np.arange(TM, dtype=np.float32)[None, :]
    rope = np.zeros((QK_ROPE, 2, TM), np.float32)
    rope[:16, 0] = rope[16:, 0] = np.cos(ang)
    rope[:16, 1], rope[16:, 1] = -np.sin(ang), np.sin(ang)
    return c, alibi.astype(np.float32).reshape(P, 8 * 2 * WIN), rope.reshape(QK_ROPE, 2 * TM)


def program(nc, a, out, known):
    ctx = ExitStack()
    counted, reached = {}, {}
    with ctx:
        sems = {}

        def sem(name):
            if name not in sems:
                sems[name] = ctx.enter_context(nc.semaphore(name))
            return sems[name]

        def signal(stage, *index):
            reached[stage] = reached.get(stage, 0) + 1
            counted[(stage,) + index] = reached[stage]
            return sem(stage), 1

        def done(stage, *index):
            return sem(stage), (known[(stage,) + index] if known else 1)

        def sb(name, width, rows=P):
            return ctx.enter_context(nc.sbuf_tensor(name, [rows, width], F32))

        banks = [ctx.enter_context(nc.psum_tensor(f"bank{i}", [P, 512], F32)) for i in range(8)]

        xT = sb("xT", KD * T)[:, :].rearrange("p (k t) -> p k t", k=KD)
        NS = 3
        PANEL = 2048
        ring = [sb(f"ring{i}", PANEL) for i in range(NS)]
        consts = sb("consts", CONST_COLS)
        V1 = sb("V1", V1_N)
        V2 = sb("V2", V2_N)
        post = sb("post", D)
        poolw = sb("poolw", 2 * P)
        small = sb("small", 672)
        acc_buf = sb("acc", TM)
        tball = sb("tb", 2 * TM)
        tb = [tball[:, i * TM:(i + 1) * TM] for i in range(2)]
        with ExitStack() as over:
            wscratch = over.enter_context(nc.sbuf_tensor("wscratch", [P, 4 * PANEL], F32))
        whi = [ctx.enter_context(nc.sbuf_tensor(f"whi{i}", [P, PANEL], F32R)) for i in range(2)]
        wlo = [ctx.enter_context(nc.sbuf_tensor(f"wlo{i}", [P, PANEL], F32R)) for i in range(2)]
        with ExitStack() as over:
            hscratch = over.enter_context(nc.sbuf_tensor("hscratch", [P, 2 * KD * TM], F32))
        hsplit = ctx.enter_context(nc.sbuf_tensor("hsplit", [P, 2 * KD * TM], F32R))
        hs = hsplit[:, :].rearrange("p (s k t) -> p s k t", s=2, k=KD)
        ARENA = 19960
        with ExitStack() as over:
            arena = over.enter_context(nc.sbuf_tensor("arena", [P, ARENA], F32))
        KA = FFN_PARTS[0][1]
        with ExitStack() as over:
            a_buf = over.enter_context(nc.sbuf_tensor("a_split", [P, 2 * KA * T], F32R))
        a_s = a_buf[:, :].rearrange("p (s k t) -> p s k t", s=2, k=KA)
        ctx.enter_context(nc.sbuf_tensor("ybr_place", [P, 10 * T], F32))
        m_buf = ctx.enter_context(nc.sbuf_tensor("m_split", [P, 2 * KD * T], F32R))
        ms_ = m_buf[:, :].rearrange("p (s k t) -> p s k t", s=2, k=KD)
        real = slice(META, TM)

        def cst(name, rows=P):
            o, w = CONST_W[name]
            return consts[0:rows, o:o + w]

        ident, ones, onesbd = cst("ident"), cst("ones"), cst("onesbd")

        class Cut:
            def __init__(self, buf, at=0, end=None):
                self.buf, self.at = buf, at
                self.end = end or buf.shape[1]

            def take(self, width, rows=P, lo=0):
                r = self.buf[lo:lo + rows, self.at:self.at + width]
                self.at += width
                assert self.at <= self.end, (self.at, self.end)
                return r

        s_ = Cut(small)
        modT, modA1, modA2, cs = s_.take(48), s_.take(8), s_.take(8), s_.take(8)
        sinks, nega, dtb = s_.take(8), s_.take(1), s_.take(1)
        ssum, sroot, srstd = s_.take(4), s_.take(4), s_.take(4)
        hmeta = s_.take(8 * META)
        eglast, cA, cB = (s_.take(NC) for _ in range(3))
        rq = s_.take(NB * GH)
        smax, snmax, ssumx, sden, sesk = s_.take(16), s_.take(16), s_.take(16), s_.take(16), s_.take(16)
        rqm = s_.take(NB)
        wqk, fss, frs = s_.take(1), s_.take(8), s_.take(8)
        msum = s_.take(2)
        epsc, eps64, eps96 = s_.take(1), s_.take(1), s_.take(1)
        cols = s_.take(128)

        A1 = Cut(arena)
        qkv = A1.take(12 * T).rearrange("p (m t) -> p m t", m=12)
        gz = A1.take(NJ * T).rearrange("p (m t) -> p m t", m=NJ)
        sq = A1.take(4 * T).rearrange("p (m t) -> p m t", m=4)
        gates = A1.take(2 * T)
        glog, grow_ = gates[:, 0:T], gates[:, T:2 * T]
        hsq = [tb[i][:, 0:T] for i in range(2)]
        sacc = acc_buf[:, 0:T]
        hrs = [A1.take(T) for _ in range(2)]
        base1 = A1.at
        B1 = Cut(arena, base1)
        raw = [B1.take(T + 3) for _ in range(3)]
        gt = [B1.take(T) for _ in range(4)]
        sk, sv = B1.take(T), B1.take(T)
        B2 = Cut(wscratch)
        vs = B2.take(T).rearrange("p (b d) -> p b d", b=NB)
        kpad = B2.take(4 * T).rearrange("p (g h t) -> p g h t", g=2, h=2)
        alibi = B2.take(8 * 2 * WIN)
        sc = [B2.take(2 * 2 * WIN) for _ in range(2)]
        pr = [B2.take(2 * 2 * WIN) for _ in range(2)]
        prT = [B2.take(4 * WIN) for _ in range(2)]
        C1 = Cut(arena, 0)
        xin = C1.take(4 * D).rearrange("p (b f) -> p b f", b=4)
        rows1, rows2 = C1.take(P), C1.take(P)
        min_ = C1.take(D)
        C1b = Cut(arena, base1)
        hpre = C1b.take(KD * T).rearrange("p (k t) -> p k t", k=KD)
        rbc = C1b.take(META)
        diag = C1b.take(4 * P).rearrange("p (b t) -> p b t", b=4)
        adaacc = [post[:, 0:512], post[:, 512:1024]]
        G1, G2 = Cut(arena, base1), Cut(hscratch)
        blk = [c_.take(NC * P).rearrange("p (n c) -> p n c", n=NC) for c_ in 7 * [G1] + 3 * [G2]]
        state = G1.take(P)
        vnew = [G1.take(P) for _ in range(2)]
        qkw = G2.take(NC * CH).rearrange("p (n c) -> p n c", n=NC)
        g_row, b_row, e_, w1, w2, qe, gx = (G2.take(T).rearrange("p (n c) -> p n c", n=NC) for _ in range(7))
        silug = [tb[i][:, 0:T] for i in range(2)]

        E2 = Cut(arena)
        ybr = E2.take(10 * T).rearrange("p (k t) -> p k t", k=10)
        base2 = E2.at
        M2 = Cut(arena, base2)
        qh = M2.take(8 * T).rearrange("p (h t) -> p h t", h=8)
        kh = M2.take(8 * TM).rearrange("p (h t) -> p h t", h=8)
        vv = M2.take(5 * T).rearrange("p (b d) -> p b d", b=5)
        rest2 = M2.at
        msc = [M2.take(TM) for _ in range(2)]
        mpr = [M2.take(TM) for _ in range(2)]
        mpT = [M2.take(4 * WIN) for _ in range(2)]
        mpR = [arena[:, ARENA - (i + 1) * WIN:ARENA - i * WIN] for i in range(2)]
        M2.at = rest2
        cq = M2.take(2 * T).rearrange("p (k t) -> p k t", k=2)
        ckv, kr = M2.take(TM), M2.take(TM)
        krs = M2.take(TM)
        ksq = krb = acc_buf[:, :]
        rope = M2.take(2 * TM).rearrange("p (s t) -> p s t", s=2)
        qsw = tball[:, 0:2 * T].rearrange("p (h t) -> p h t", h=2)
        N2 = Cut(arena, base2)
        zc = [N2.take(30 + TM) for _ in range(2)]
        ga_ = [N2.take(TM) for _ in range(2)]
        cacc = N2.take(2 * T).rearrange("p (k t) -> p k t", k=2)
        csq = N2.take(2 * T).rearrange("p (k t) -> p k t", k=2)
        cmr = N2.take(2 * T).rearrange("p (k t) -> p k t", k=2)
        bg = N2.take(2 * T).rearrange("p (k t) -> p k t", k=2)
        cgx = [N2.take(TM) for _ in range(2)]
        uu = [N2.take(2 + TM) for _ in range(2)]
        pv = [N2.take(TM) for _ in range(2)]
        pw = [N2.take(TM) for _ in range(3)]
        pg = N2.take(2 * T).rearrange("p (k t) -> p k t", k=2)
        sg = [tb[i][:, 0:T] for i in range(2)]
        sg_mla = [sacc, cst("reset")]
        macc01 = [post[:, 0:T], cst("sel")]
        O2 = Cut(arena, base2 + 2 * KD * T)
        prod = [O2.take(T) for _ in range(2)]
        macc = [O2.take(T) for _ in range(2)]
        xtok = O2.take(4 * D).rearrange("p (b f) -> p b f", b=4)
        O3 = Cut(arena, 0, base2)
        fin = [O3.take(D) for _ in range(4)]
        fjunk = O3.take(512)

        panels, index_of, splits = [], {}, []

        def w_cols(w, c0, n, k0=0, kn=None):
            kn = kn or w.shape[0] // P - k0
            return w[k0 * P:(k0 + kn) * P, c0:c0 + n].rearrange("(k p) n -> p k n", p=P)

        def panel(name, kn, width, parts, split=True):
            if split:
                splits.append(name)
            index_of[name] = len(panels)
            panels.append((name, kn, width, parts))

        w_in, w_ada, w_out = a["w_in"][0], a["w_ada"][0], a["w_out"][0]
        w_gate, w_up, w_down = a["w_gate"][0], a["w_up"][0], a["w_down"][0]
        w_in2 = a["w_in_2"][0]

        def ada_panel(i):
            for h in range(2):
                panel(f"ada{i}{h}", 4, 512, [(0, 512, w_cols(w_ada, 512 * i, 512, 4 * h, 4))], split=False)

        def cols_panel(name, w, c0, n=256):
            panel(name, KD, n, [(0, n, w_cols(w, c0, n))])

        for i in range(4):
            ada_panel(i)
        for i in range(6):
            cols_panel(f"qkv{i}", w_in, 256 * i)
            if i in (2, 3, 4, 5):
                ada_panel(2 + i)
        panel("abk", KD, 168, [(0, 32, w_cols(w_in, 2048, 32)), (32, 8, w_cols(w_in, 2056, 8)),
                               (40, 128, w_cols(w_in, 2576, 128))])
        cols_panel("sv", w_in, 2704, 128)
        ada_panel(8)
        for i in range(2):
            cols_panel(f"sq{i}", w_in, 2064 + 256 * i)
        ada_panel(9)
        for i in range(2):
            cols_panel(f"gz{i}", w_in, 1536 + 256 * i)
        for i in range(4):
            cols_panel(f"out{i}", w_out, 256 * i)
        for part, (c0, n) in enumerate(FFN_PARTS):
            for i in range(c0 // 2, (c0 + n) // 2):
                cols_panel(f"g{i}", w_gate, 256 * i)
                cols_panel(f"u{i}", w_up, 256 * i)
                if i in (1, 3):
                    ada_panel(10 + i // 2)
            for m in range(KD):
                panel(f"down{part}{m}", n, P, [(0, P, w_cols(w_down, P * m, P, c0, n))])
        seg = {"cug": 1696, "cu": 1440, "pv": 0, "pg": 256, "cg": 1952, "bg": 2208, "cgx": 2464, "xv": 2720,
               "sg": 2976, "cq": 512, "mg0": 928}
        for name, c0 in seg.items():
            cols_panel(name, w_in2, c0)
        cols_panel("ckr", w_in2, 768, 192)
        cols_panel("mg1", w_in2, 928 + 256)
        GL0 = 3232
        branch_w = [("w_out_pool_2", 2), ("w_out_mla_2", 4), ("w_out_conf_2", 2), ("w_out_sc_2", 2)]
        for m in range(KD):
            for h in range(2):
                panel(f"gl{m}{h}", KD, 256, [(128 * b, 128, w_cols(w_in2, GL0 + 1024 * (2 * h + b) + 128 * m, 128))
                                             for b in range(2)])
                if m == 2 and h == 0:
                    for m1 in range(2):
                        panel(f"yb{m1}", 4, P, None, split=False)
            if m == 0:
                panel("uq", 2, 768, [(0, 768, w_cols(a["w_uq_2"][0], 0, 768))], split=False)
                panel("ukv", 1, 1024, [(0, 1024, w_cols(a["w_ukv_2"][0], 0, 1024))], split=False)
            if m < 2:
                panel(f"ya{m}", 6, P, None, split=False)
            else:
                panel(f"yw{m}", 10, P, None, split=False)
        for half in range(2):
            for kh_ in range(2):
                panel(f"wo{half}{kh_}", 4, 512, [(0, 512, w_cols(a["w_o_2"][0], 512 * half, 512, 4 * kh_, 4))])

        branches_of = {"ya": (0, 2, 3), "yb": (1,), "yw": (0, 1, 2, 3)}

        def y_place(m, b):
            kind = "yw" if m >= 2 else "yb" if b == 1 else "ya"
            return (f"{kind}{m}", sum(branch_w[i][1] for i in branches_of[kind] if i < b),
                    sum(branch_w[i][1] for i in range(b)), branch_w[b][1])

        loads_of_slot = [0] * NS
        loaded_at = {}
        for i, (name, kn, width, parts) in enumerate(panels):
            n_dma = len(branches_of[name[:2]]) if parts is None else len(parts)
            loads_of_slot[i % NS] += 16 * n_dma
            loaded_at[name] = loads_of_slot[i % NS]

        def W(name):
            i = index_of[name]
            _, kn, width, _ = panels[i]
            return ring[i % NS][:, 0:kn * width].rearrange("p (k n) -> p k n", k=kn)

        def split_of(name):
            _, kn, width, _ = panels[index_of[name]]
            i = splits.index(name) % 2
            return [w[i][:, 0:kn * width].rearrange("p (k n) -> p k n", k=kn) for w in (whi, wlo)]

        def loaded(name):
            return sem(f"loaded{index_of[name] % NS}"), loaded_at[name]

        place, tiles, uses, held, turn = {}, [], [0] * 8, set(), [0]

        def open_tile(pe, *key, hold=False):
            while turn[0] % 8 in held:
                turn[0] += 1
            b = turn[0] % 8
            turn[0] += 1
            place[key] = b, uses[b] + 1
            uses[b] += 1
            tiles.append((key, place[key]))
            if hold:
                held.add(b)
            if uses[b] > 1:
                pe.wait_ge(sem(f"bank{b}_read"), uses[b] - 1)
            return banks[b]

        def let_go(*key):
            held.discard(place[key][0])

        def fill(*key):
            return sem(f"bank{place[key][0]}_filled"), 1

        def filled(*key):
            return sem(f"bank{place[key][0]}_filled"), place[key][1]

        def read(*key):
            return sem(f"bank{place[key][0]}_read"), 1

        def copied(*key):
            return sem(f"bank{place[key][0]}_read"), place[key][1]

        def bank(*key):
            return banks[place[key][0]]

        def arrived(name, n=1):
            return sem("ld_" + name), 16 * n

        MIX_EARLY = [(m, b) for m in range(2) for b in range(4)]

        def macc_of(m):
            return macc01[m] if m < 2 else macc[m % 2]

        def early_gate(i):
            m, b = MIX_EARLY[i]
            if b == 1:
                return sg_mla[m], None
            passing = [x for x in MIX_EARLY if x[1] != 1]
            at = passing.index((m, b))
            return sg[at % 2], passing[at - 2] if at >= 2 else None

        SWU = [(b, hp) for b in range(NB) for hp in range(4)]
        MLU = [(i, h) for i in range(NB) for h in range(8)]
        keys_of = [META + WIN * (i + 1) for i in range(NB)]

        block = ctx.enter_context(nc.Block())
        last_tile_of = {}

        def used(name):
            if name.startswith("wo") and name[-1] == "0":
                return done("fo_part", int(name[2]), 3)
            return filled(*last_tile_of[name])

        def splitter(eng, whole, rest):
            at = [0]

            def step():
                i = at[0]
                at[0] += 1
                if i >= len(splits):
                    return
                name = splits[i]
                _, kn, width, _ = panels[index_of[name]]
                n = kn * width
                raw_, hi, lo = ring[index_of[name] % NS][:, 0:n], whi[i % 2][:, 0:n], wlo[i % 2][:, 0:n]
                if whole:
                    if i >= 2:
                        eng.wait_ge(*used(splits[i - 2]))
                    eng.wait_ge(*loaded(name))
                    whole(hi, raw_).then_inc(*signal("w_hi", name))
                else:
                    eng.wait_ge(*done("w_hi", name))
                    rest(lo, raw_, hi.bitcast(F32)).then_inc(*signal("w_lo", name))
            return step

        @block.tensor
        def _(pe):
            mm, tr = nc.tensor.matmul, nc.tensor.transpose

            def project(key, name, c0, m, rhs, n, release=False):
                o = open_tile(pe, *key)
                pe.wait_ge(*done("w_lo", name))
                hi, lo = split_of(name)
                kn = hi.shape[1]
                for k in range(kn):
                    for i, (w, s) in enumerate(((hi, 0), (hi, 1), (lo, 0))):
                        last = mm(o[0:m, 0:n], w[:, k, c0:c0 + m], rhs(s, k), start=k + i == 0,
                                  stop=k == kn - 1 and i == 2)
                last.then_inc(*fill(*key))
                if release:
                    last_tile_of[name] = key

            def norm_stats(tag):
                o = open_tile(pe, "sum" + tag)
                pe.wait_ge(*done("sqsum" + tag, KD - 1))
                for b in range(4):
                    last = mm(o[:, b:b + 1], sacc[:, b * P:(b + 1) * P], ones[:, 0:1], start=True, stop=True)
                last.then_inc(*fill("sum" + tag))

            def norm_spread(tag, dg):
                o = open_tile(pe, "spread" + tag)
                pe.wait_ge(*done("diag" + tag))
                for b in range(4):
                    last = mm(o[:, b * P:(b + 1) * P], ones, dg[:, b, :], start=True, stop=True)
                last.then_inc(*fill("spread" + tag))

            def ada(i):
                o = open_tile(pe, "ada", i)
                pe.wait_ge(*done("adaacc", i))
                for c in range(4):
                    last = mm(o[:, c:c + 1], adaacc[i % 2][:, c * P:(c + 1) * P], ones[:, 0:1], start=True, stop=True)
                last.then_inc(*fill("ada", i))

            pe.wait_ge(*arrived("const"))
            pe.wait_ge(*arrived("rows", 21))
            o = open_tile(pe, "vec")
            tr(o[:, 0:V1_N], rows1[0:V1_N, :], ident[0:V1_N, 0:V1_N])
            tr(o[:, P:P + V2_N], rows2[0:V2_N, :], ident[0:V2_N, 0:V2_N]).then_inc(*fill("vec"))
            pe.wait_ge(*arrived("x", 2))
            for k in range(KD):
                o = open_tile(pe, "x", k)
                for b in range(4):
                    last = tr(o[:, b * P:(b + 1) * P], xin[:, b, k * P:(k + 1) * P], ident)
                last.then_inc(*fill("x", k))
            o = open_tile(pe, "meta")
            for k in range(KD):
                last = tr(o[:, k * META:(k + 1) * META], min_[0:META, k * P:(k + 1) * P], ident[0:META, 0:META])
            last.then_inc(*fill("meta"))
            norm_spread("1", diag)
            o = open_tile(pe, "spreadmeta")
            pe.wait_ge(*done("diagmeta"))
            mm(o[:, 0:META], ones[0:META, :], rbc[0:META, 0:META], start=True, stop=True).then_inc(*fill("spreadmeta"))
            for i in range(4):
                ada(i)

            hx = lambda s, k: hs[:, s, k, real]

            def first_tile(key, name, tag, n=T, rhs=None):
                o = open_tile(pe, *key)
                pe.wait_ge(*done("w_lo", name))
                hi, lo = split_of(name)
                for k in range(KD):
                    pe.wait_ge(*done("h" + tag, k))
                    for i, (w, s) in enumerate(((hi, 0), (hi, 1), (lo, 0))):
                        last = mm(o[:, 0:n], w[:, k, 0:P], (rhs or hx)(s, k), start=k + i == 0,
                                  stop=k == KD - 1 and i == 2)
                last.then_inc(*fill(*key))

            pick = cst("pick").rearrange("p (w j c) -> p w j c", w=2, j=NJ)
            hs_tile = [None]

            def head_lengths(m):
                if m == 0:
                    hs_tile[0] = open_tile(pe, "hsum", hold=True)
                pe.wait_ge(*done("hsq", m))
                last = mm(hs_tile[0][0:40, :], pick[:, m // 4, m % 4, :], hsq[m % 2], start=m == 0, stop=m == 7)
                last.then_inc(*(fill("hsum") if m == 7 else signal("hsum_step", m)))
                if m == 7:
                    let_go("hsum")

            for m in range(12):
                if m == 0:
                    first_tile(("pj", 0), "qkv0", "1")
                else:
                    project(("pj", m), f"qkv{m // 2}", P * (m % 2), P, hx, T, release=m % 2 == 1)
                if m >= 4:
                    head_lengths(m - 4)
                if m >= 5 and m % 2 == 1:
                    ada((m - 5) // 2 + 4)
            project(("ab",), "abk", 0, P, hx, T)
            project(("sk",), "abk", 40, P, hx, T, release=True)
            project(("sv",), "sv", 0, P, hx, T, release=True)
            o = open_tile(pe, "sksum")
            pe.wait_ge(*done("hsq", 8))
            mm(o[:, :], onesbd, hsq[0], start=True, stop=True).then_inc(*fill("sksum"))
            sqs = open_tile(pe, "sqsum", hold=True)

            def query_lengths(m):
                pe.wait_ge(*done("hsq", 9 + m))
                for b in range(NB):
                    c = (b * 4 + m) * 2
                    last = mm(sqs[:, c:c + 2], hsq[(9 + m) % 2][:, b * P:(b + 1) * P], cst("two"), start=True, stop=True)
                last.then_inc(*(fill("sqsum") if m == 3 else signal("sqsum_step", m)))

            for m in range(4):
                project(("sq", m), f"sq{m // 2}", P * (m % 2), P, hx, T, release=m % 2 == 1)
                if m >= 2:
                    query_lengths(m - 2)
            ada(8)
            for m in range(4):
                project(("gz", m), f"gz{m // 2}", P * (m % 2), P, hx, T, release=m % 2 == 1)
                if m < 2:
                    query_lengths(2 + m)
                if m == 1:
                    let_go("sqsum")
            ada(9)
            o = open_tile(pe, "vs")
            pe.wait_ge(*copied("sv"))
            for b in range(NB):
                last = tr(o[:, b * P:(b + 1) * P], sv[:, b * P:(b + 1) * P], ident)
            last.then_inc(*fill("vs"))

            o = open_tile(pe, "cols")
            pe.wait_ge(*done("grows"))
            for n in range(NC):
                for s, (r0, src) in enumerate(((0, glog), (32, glog), (32, grow_), (64, grow_))):
                    for h in range(2):
                        last = mm(o[h * HD:(h + 1) * HD, n * 32 + 8 * s:n * 32 + 8 * s + 8],
                                  src[0:72, n * CH:(n + 1) * CH], ident[0:72, r0:r0 + 8],
                                  start=True, stop=True)
            last.then_inc(*fill("cols"))

            pe.wait_ge(*done("kpad"))

            def sw_scores(u):
                b, hp = SWU[u]
                k0, wk = (0, WIN) if b == 0 else ((b - 1) * WIN, 2 * WIN)
                o = open_tile(pe, "ss", u)
                for p in range(2):
                    last = mm(o[:, p * wk:(p + 1) * wk], sq[:, hp, b * WIN:(b + 1) * WIN],
                              kpad[:, hp // 2, p, k0:k0 + wk], start=True, stop=True)
                last.then_inc(*fill("ss", u))

            def sw_turn(u):
                b, hp = SWU[u]
                nk = 1 if b == 0 else 2
                o = open_tile(pe, "st", u)
                pe.wait_ge(*done("sprob", u))
                for c in range(2 * nk):
                    last = tr(o[:, c * WIN:(c + 1) * WIN], pr[u % 2][:, c * WIN:(c + 1) * WIN], ident)
                last.then_inc(*fill("st", u))

            def sw_values(u):
                b, hp = SWU[u]
                nk = 1 if b == 0 else 2
                if hp == 0:
                    sw_out[0] = open_tile(pe, "so", b, hold=True)
                o = sw_out[0]
                pe.wait_ge(*copied("st", u))
                g = hp // 2
                for p in range(2):
                    for kb in range(nk):
                        last = mm(o[p * HD:(p + 1) * HD, hp * WIN:(hp + 1) * WIN],
                                  vs[:, b - nk + 1 + kb, g * HD:(g + 1) * HD],
                                  prT[u % 2][:, (p * nk + kb) * WIN:(p * nk + kb + 1) * WIN],
                                  start=kb == 0, stop=kb == nk - 1)
                if hp == 3:
                    last.then_inc(*fill("so", b))
                else:
                    last.then_inc(*signal("so_step", u))

            sw_out = [None]

            def window(j, point):
                u = 6 * j + point
                if 0 <= u - 3 < len(SWU):
                    sw_turn(u - 3)
                if 0 <= u - 4 < len(SWU):
                    sw_values(u - 4)
                if u < len(SWU):
                    sw_scores(u)
                if 0 <= u - 5 < len(SWU) and SWU[u - 5][1] == 3:
                    let_go("so", SWU[u - 5][0])

            for j in range(NJ):
                for s, (r0, src) in enumerate(((0, glog), (32, glog), (0, grow_))):
                    o = open_tile(pe, "rows", j, s)
                    selj = cst("sel", 40)[r0:r0 + 8, j * P:(j + 1) * P]
                    mm(o[:, :], selj, src[r0:r0 + 8, :], start=True, stop=True).then_inc(*fill("rows", j, s))

                def squares(name, left, right, waits=()):
                    for half in range(2):
                        o = open_tile(pe, name, j, half)
                        if half == 0:
                            for w in waits:
                                pe.wait_ge(*w)
                        for n in range(4):
                            nn = 4 * half + n
                            last = mm(o[:, n * P:(n + 1) * P], left[:, nn, :], right[:, nn, :], start=True, stop=True)
                        last.then_inc(*fill(name, j, half))

                def turns(name, src, waits=()):
                    for half in range(2):
                        o = open_tile(pe, name, j, half)
                        if half == 0:
                            for w in waits:
                                pe.wait_ge(*w)
                        for n in range(4):
                            last = tr(o[:, n * P:(n + 1) * P], src[:, 4 * half + n, :], ident)
                        last.then_inc(*fill(name, j, half))

                squares("kk", blk[0], blk[0], [done("kbd", j)])
                o = open_tile(pe, "kq", j)
                for n in range(NC):
                    last = mm(o[:, n * CH:(n + 1) * CH], blk[0][:, n, :],
                              qkv[:, j, n * CH:(n + 1) * CH], start=True, stop=True)
                last.then_inc(*fill("kq", j))
                window(j, 0)
                turns("tA", blk[2], [copied("kk", j, 1)])
                window(j, 1)
                squares("d2", blk[3], blk[5], [done("dT", j), copied("tA", j, 1)])
                squares("d2T", blk[5], blk[3])
                squares("d4", blk[9], blk[8], [copied("d2", j, 1), copied("d2T", j, 1)])
                squares("d4T", blk[8], blk[9])
                squares("p1", blk[8], blk[4], [done("p0", j)])
                turns("kt", blk[0])
                turns("vt", blk[1])
                squares("d8", blk[3], blk[2], [copied("d4", j, 1), copied("d4T", j, 1)])
                squares("p2", blk[2], blk[4], [copied("p1", j, 1)])
                window(j, 2)
                squares("p3", blk[5], blk[4], [copied("d8", j, 1), copied("p2", j, 1)])
                turns("t16", blk[4], [copied("p3", j, 1)])
                squares("z1", blk[6], blk[4])
                window(j, 3)
                squares("i32", blk[2], blk[3], [copied("t16", j, 1), copied("z1", j, 1)])
                turns("t32", blk[4], [copied("i32", j, 1)])
                squares("z2", blk[7], blk[4])
                squares("i64", blk[5], blk[3], [copied("t32", j, 1), copied("z2", j, 1)])
                squares("wT", blk[8], blk[4], [copied("kt", j, 1), copied("i64", j, 1)])
                oo = open_tile(pe, "go", j, hold=True)
                for n in range(NC):
                    if n in (2, 5):
                        window(j, 4 + n // 3)
                    o = open_tile(pe, "vn", j, n)
                    if n == 0:
                        pe.wait_ge(*copied("wT", j, 1))
                        pe.wait_ge(*copied("vt", j, 1))
                        pe.wait_ge(*done("qe", j))
                        pe.wait_ge(*copied("kq", j))
                    last = mm(o[:, 0:P], blk[4][:, n, :], blk[1][:, n, :], start=True, stop=n == 0)
                    if n > 0:
                        pe.wait_ge(*copied("su", j, n - 1))
                        last = mm(o[:, 0:P], blk[6][:, n, :], state, start=False, stop=True)
                    last.then_inc(*fill("vn", j, n))
                    if n > 0:
                        mm(oo[:, n * CH:(n + 1) * CH], state, qe[:, n, :], start=True, stop=False)
                    pe.wait_ge(*copied("vn", j, n))
                    if n < NC - 1:
                        o = open_tile(pe, "su", j, n)
                        mm(o[:, 0:P], blk[0][:, n, :], vnew[n % 2], start=True, stop=True).then_inc(*fill("su", j, n))
                    last = mm(oo[:, n * CH:(n + 1) * CH], vnew[n % 2], qkw[:, n, :], start=n == 0, stop=True)
                    last.then_inc(*(fill("go", j) if n == NC - 1 else signal("go_step", j, n)))
                let_go("go", j)

            o = open_tile(pe, "osum")
            for j in range(NJ):
                pe.wait_ge(*done("osq", j))
                last = mm(o[0:40, :], pick[:, 0, j, :], hsq[j % 2], start=j == 0, stop=j == NJ - 1)
                last.then_inc(*(fill("osum") if j == NJ - 1 else signal("osum_step", j)))
            for j in range(NJ):
                o = open_tile(pe, "ospread", j)
                if j == 0:
                    pe.wait_ge(*done("orow"))
                mm(o[:, :], cst("sel", 40)[0:8, j * P:(j + 1) * P], hrs[1][0:8, :], start=True, stop=True)\
                    .then_inc(*fill("ospread", j))

            for k in range(KD):
                pe.wait_ge(*done("mix", k))
            for m in range(KD):
                project(("mo", m), f"out{m // 2}", P * (m % 2), P, hx, T, release=m % 2 == 1)
            norm_stats("2")
            norm_spread("2", diag)
            for part, (c0, n) in enumerate(FFN_PARTS):
                for i in range(c0 // 2, (c0 + n) // 2):
                    for name, key in (("g", "fg"), ("u", "fu")):
                        for c in range(2):
                            if i == 0 and name == "g" and c == 0:
                                first_tile(("fg", 0), "g0", "2")
                            else:
                                project((key, 2 * i + c), f"{name}{i}", P * c, P, hx, T, release=c == 1)
                    if i == 4:
                        ada(10)
                    if i == 5:
                        ada(11)
                for k in range(n):
                    pe.wait_ge(*done("a", c0 + k))
                for m in range(KD):
                    project(("fd", part, m), f"down{part}{m}", 0, P, lambda s, k: a_s[:, s, k, :], T, release=True)
            norm_stats("3")
            norm_spread("3", diag)

            pe.wait_ge(*done("h3meta"))
            half_of = [slice(0, TM // 2), slice(TM // 2, TM)]
            hall = [lambda s, k: hs[:, s, k, half_of[0]], lambda s, k: hs[:, s, k, half_of[1]]]

            def project_all(key, name, c0, m, release=False):
                for half in range(2):
                    project(key + (half,), name, c0, m, hall[half], TM // 2, release and half == 1)

            def project_real(key, name, m0=0):
                for c in range(2):
                    project((key, m0 + c), name, P * c, P, hx, T, release=c == 1)

            def project_pair(key, name):
                for m in range(2):
                    project_all((key, m), name, P * m, P, release=m == 1)

            first_tile(("cgate", 0, 0), "cug", "3", TM // 2, hall[0])
            project(("cgate", 0, 1), "cug", 0, P, hall[1], TM // 2)
            project_all(("cgate", 1), "cug", P, P, release=True)
            project_pair("cu", "cu")
            project_pair("pv", "pv")
            project_real("pg", "pg")
            project_real("cg", "cg")
            for m in range(2):
                o = open_tile(pe, "py", m)
                pe.wait_ge(*done("pool", m))
                mm(o[:, :], poolw[:, P * m:P * m + P], pw[m][:, META:TM], start=True, stop=True).then_inc(*fill("py", m))
            project_real("bg", "bg")
            project_pair("cgx", "cgx")
            project_pair("xv", "xv")
            project_real("sg", "sg")
            project_real("cq", "cq")

            def conf_stats(tag, src):
                o = open_tile(pe, tag)
                for m in range(2):
                    pe.wait_ge(*done(tag + "_in", m))
                    last = mm(o[:, :], ones, src[:, m, :], start=m == 0, stop=m == 1)
                last.then_inc(*fill(tag))

            project_real("mg", "mg0")
            conf_stats("cmean", cacc)
            project_all(("ckv",), "ckr", 0, P)
            conf_stats("cvar", csq)
            project_all(("kr",), "ckr", 64, P, release=True)
            project_real("mg", "mg1", 2)

            o = open_tile(pe, "cqsum")
            for b in range(4):
                for k in range(2):
                    if b == 0:
                        pe.wait_ge(*done("cqsq", k))
                    last = mm(o[:, b:b + 1], qsw[:, k, b * P:(b + 1) * P], ones[:, 0:1], start=k == 0, stop=k == 1)
            last.then_inc(*fill("cqsum"))
            for half in range(2):
                o = open_tile(pe, "kvsum", half)
                pe.wait_ge(*done("ckvsq"))
                mm(o[:, 0:TM // 2], ones, ksq[:, half * (TM // 2):(half + 1) * (TM // 2)], start=True, stop=True)\
                    .then_inc(*fill("kvsum", half))
            pe.wait_ge(*loaded("uq"))
            pe.wait_ge(*done("cqg", 1))
            for h in range(8):
                o = open_tile(pe, "q", h)
                for k in range(2):
                    last = mm(o[0:QD, :], W("uq")[:, k, h * QD:(h + 1) * QD], cq[:, k, :], start=k == 0, stop=k == 1)
                last.then_inc(*fill("q", h))
            last_tile_of["uq"] = ("q", 7)
            pe.wait_ge(*loaded("ukv"))
            pe.wait_ge(*done("ckvn"))
            wkv = W("ukv")[:, 0, :].rearrange("p (h d) -> p h d", h=8)
            for h in range(8):
                for half in range(2):
                    o = open_tile(pe, "k", h, half)
                    mm(o[0:HD, 0:TM // 2], wkv[:, h, 0:HD], ckv[:, half * (TM // 2):(half + 1) * (TM // 2)],
                       start=True, stop=True).then_inc(*fill("k", h, half))
            for b in range(5):
                n = P if b < 4 else META
                o = open_tile(pe, "v", b)
                mm(o[0:n, :], ckv[:, b * P:b * P + n], wkv[:, :, HD:2 * HD], start=True, stop=True)\
                    .then_inc(*fill("v", b))
            last_tile_of["ukv"] = ("v", 4)

            def ml_scores(u):
                i, h = MLU[u]
                n = keys_of[i]
                o = open_tile(pe, "ms", u)
                m0 = min(n, 512)
                mm(o[:, 0:m0], qh[0:QD, h, i * WIN:(i + 1) * WIN], kh[0:QD, h, 0:m0], start=True, stop=True)\
                    .then_inc(*fill("ms", u))
                if n > 512:
                    o = open_tile(pe, "ms2", u)
                    mm(o[:, 0:n - 512], qh[0:QD, h, i * WIN:(i + 1) * WIN], kh[0:QD, h, 512:n],
                       start=True, stop=True).then_inc(*fill("ms2", u))

            def ml_turn(u):
                i, h = MLU[u]
                o = open_tile(pe, "mt", u)
                pe.wait_ge(*done("mprob", u))
                for c in range(i + 1):
                    last = tr(o[:, c * WIN:(c + 1) * WIN], mpr[u % 2][:, c * WIN:(c + 1) * WIN], ident)
                last.then_inc(*fill("mt", u))
                o = open_tile(pe, "mr", u)
                tr(o[0:META, 0:WIN], mpr[u % 2][:, (i + 1) * WIN:(i + 1) * WIN + META], ident)\
                    .then_inc(*fill("mr", u))

            ml_out = [None]

            def ml_values(u):
                i, h = MLU[u]
                if h == 0:
                    ml_out[0] = open_tile(pe, "mo2", i, hold=True)
                o = ml_out[0]
                p, pair = h % 2, h // 2
                pe.wait_ge(*copied("mt", u))
                for c in range(i + 1):
                    mm(o[p * HD:(p + 1) * HD, pair * WIN:(pair + 1) * WIN], vv[:, c, h * HD:(h + 1) * HD],
                       mpT[u % 2][:, c * WIN:(c + 1) * WIN], start=c == 0, stop=False)
                pe.wait_ge(*copied("mr", u))
                last = mm(o[p * HD:(p + 1) * HD, pair * WIN:(pair + 1) * WIN], vv[:, i + 1, h * HD:(h + 1) * HD],
                          mpR[u % 2], start=False, stop=True)
                last.then_inc(*(fill("mo2", i) if h == 7 else signal("mo_step", u)))
                if h == 7:
                    let_go("mo2", i)

            pe.wait_ge(*done("qrope", 3))
            pe.wait_ge(*done("krope"))
            pe.wait_ge(*copied("k", 7, 1))
            pe.wait_ge(*copied("v", 4))
            pe.wait_ge(*done("vpad"))
            def y_tile(m, b):
                name, k0, kb, nk = y_place(m, b)
                o = open_tile(pe, "y", m, b)
                pe.wait_ge(*loaded(name))
                for k in range(nk):
                    last = mm(o[:, :], W(name)[:, k0 + k, :], ybr[:, kb + k, :], start=k == 0, stop=k == nk - 1)
                last.then_inc(*fill("y", m, b))
                last_tile_of[name] = ("y", m, b)

            early = [None]

            def mix_step(u):
                i, q = u // 4, u % 4
                if i and q == 1:
                    let_go("gl", *MIX_EARLY[i - 1])
                if i and q == 0 and MIX_EARLY[i - 1][1] != 1:
                    if i == 1:
                        for k in range(2):
                            pe.wait_ge(*copied("py", k))
                            pe.wait_ge(*done("yc", k))
                            pe.wait_ge(*done("yd", k))
                    y_tile(*MIX_EARLY[i - 1])
                if i >= len(MIX_EARLY):
                    return
                m, b = MIX_EARLY[i]
                name = f"gl{m}{b // 2}"
                if q == 0:
                    early[0] = open_tile(pe, "gl", m, b, hold=True)
                    pe.wait_ge(*done("w_lo", name))
                hi, lo = split_of(name)
                for k in (2 * q, 2 * q + 1):
                    for x, (w, s) in enumerate(((hi, 0), (hi, 1), (lo, 0))):
                        last = mm(early[0][:, :], w[:, k, P * (b % 2):P * (b % 2) + P], hx(s, k), start=k + x == 0,
                                  stop=k == KD - 1 and x == 2)
                if q == 3:
                    last.then_inc(*fill("gl", m, b))
                    if b % 2:
                        last_tile_of[name] = ("gl", m, b)

            for u in range(len(MLU) + 2):
                if u < len(MLU):
                    ml_scores(u)
                if u >= 2:
                    ml_turn(u - 2)
                mix_step(u)
                if u >= 2:
                    ml_values(u - 2)

            for b in range(NB):
                pe.wait_ge(*copied("mo2", b))
            y_tile(0, 1)
            y_tile(1, 1)
            for m in range(2, KD):
                for b in range(4):
                    project(("gl", m, b), f"gl{m}{b // 2}", P * (b % 2), P, hx, T, release=b % 2 == 1)
                    y_tile(m, b)
            for b in range(4):
                for half in range(2):
                    o = open_tile(pe, "xt", b, half)
                    for c in range(4):
                        last = tr(o[:, c * P:(c + 1) * P], xT[:, 4 * half + c, b * P:(b + 1) * P], ident)
                    last.then_inc(*fill("xt", b, half))
            for k in range(KD):
                pe.wait_ge(*done("m", k))
            for half in range(2):
                fo = [open_tile(pe, "fo", b, half, hold=True) for b in range(4)]
                for kp in range(2):
                    pe.wait_ge(*done("w_lo", f"wo{half}{kp}"))
                    hi, lo = split_of(f"wo{half}{kp}")
                    for b in range(4):
                        for k in range(4):
                            for i, (s, w) in enumerate(((0, hi), (0, lo), (1, hi))):
                                last = mm(fo[b][:, :], ms_[:, s, 4 * kp + k, b * P:(b + 1) * P], w[:, k, :],
                                          start=kp + k + i == 0, stop=kp == 1 and k == 3 and i == 2)
                        last.then_inc(*(fill("fo", b, half) if kp else signal("fo_part", half, b)))
                    last_tile_of[f"wo{half}{kp}"] = ("fo", 3, half)

        @block.sync
        def _(sp):
            sp.dma_start(consts[:, :], a["consts"]).then_inc(sem("ld_const"), 16)
            sp.dma_start(xin, a["x"][0].rearrange("(b p) f -> p b f", p=P)).then_inc(sem("ld_x"), 16)
            sp.dma_start(min_[0:META, :], a["meta_tokens_2"]).then_inc(sem("ld_x"), 16)
            for i, (name, kn, width, parts) in enumerate(panels):
                if i >= NS:
                    before = panels[i - NS][0]
                    sp.wait_ge(*(done("adaacc" if before[-1] == "1" else "adapart", int(before[3:-1]))
                                 if before.startswith("ada") else
                                 done("w_lo", before) if before in splits else filled(*last_tile_of[before])))
                dst = W(name)
                if parts is None:
                    k0 = 0
                    for wname, nk in (branch_w[b] for b in branches_of[name[:2]]):
                        sp.dma_start(dst[:, k0:k0 + nk, :], w_cols(a[wname][0], P * int(name[2:]), P))\
                            .then_inc(sem(f"loaded{i % NS}"), 16)
                        k0 += nk
                else:
                    for c0, n, src in parts:
                        sp.dma_start(dst[:, :, c0:c0 + n], src).then_inc(sem(f"loaded{i % NS}"), 16)
            sp.wait_ge(sem("stored"), 16 * 4)

        @block.gpsimd
        def _(pool):
            vec = [("b_ada", a["b_ada"][0], 48), ("norm1", a["norm1_w"][0], 8), ("norm2", a["norm2_w"][0], 8),
                   ("pre", a["pre_norm_g_2"][0], 8), ("gate_bias", a["gate_bias_2"][0], 32),
                   ("conf_b", a["conf_dw_b_2"][0], 2), ("ln_g", a["conf_ln_g_2"][0], 2),
                   ("ln_b", a["conf_ln_b_2"][0], 2), ("pool_scale", a["pool_scale_2"][0], 2),
                   ("q_norm", a["q_norm_g_2"][0], 2), ("kv_norm", a["kv_norm_g_2"][0], 1), ("c", a["c"][0], 8)]
            for name, src, n in vec:
                r = V1_ROWS[name]
                pool.dma_start(rows1[r:r + n, :], src.rearrange("(r p) -> r p", p=P)).then_inc(sem("ld_rows"), 16)
            for name, src in (("gdn_norm", a["gdn_norm_w"]), ("qn", a["q_norm_w"]), ("kn", a["k_norm_w"])):
                r = V1_ROWS[name]
                for h in range(2):
                    pool.dma_start(rows1[r:r + 1, h * HD:(h + 1) * HD], src).then_inc(sem("ld_rows"), 16)
            pool.dma_start(rows2[0:48, :], a["conv_w"][0, :, 0, :].rearrange("k (m p) -> (k m) p", p=P))\
                .then_inc(sem("ld_rows"), 16)
            pool.dma_start(rows2[48:110, :], a["conf_dw_w_2"][0].rearrange("k (m p) -> (k m) p", p=P))\
                .then_inc(sem("ld_rows"), 16)
            pool.dma_start(rows2[110:116, :], a["sc_dw_w_2"][0].rearrange("k (m p) -> (k m) p", p=P))\
                .then_inc(sem("ld_rows"), 16)
            pool.dma_start(nega[0:8, :], a["a_log"][0].rearrange("(h o) -> h o", o=1)).then_inc(sem("ld_gate"), 16)
            pool.dma_start(dtb[0:8, :], a["dt_bias"][0].rearrange("(h o) -> h o", o=1)).then_inc(sem("ld_gate"), 16)
            pool.dma_start(sinks, a["sinks"].broadcast_to([P, 8])).then_inc(sem("ld_gate"), 16)
            nc.gpsimd.memset(poolw[:, :], 0.0).then_inc(*signal("poolw0"))
            pool.wait_ge(*done("poolw0"))
            for g in range(4):
                r, c = (g % 2) * HD, (g // 2) * P + (g % 2) * HD
                pool.dma_start(poolw[r:r + HD, c:c + HD], a["pool_w_2"][0, g]).then_inc(sem("ld_poolw"), 16)
            pool.wait_ge(*filled("gz", 3))
            pool.dma_start(alibi, a["alibi"]).then_inc(sem("ld_alibi"), 16)
            nc.gpsimd.memset(kpad, 0.0).then_inc(*signal("kpad0"))
            def window(j, point):
                u = 6 * j + point - 2
                if not 0 <= u < len(SWU):
                    return
                b, hp = SWU[u]
                wk = WIN if b == 0 else 2 * WIN
                pool.wait_ge(*done("srec", u))
                v = pr[u % 2][:, 0:2 * wk].rearrange("p (h k) -> p h k", h=2)
                nc.gpsimd.tensor_tensor(v, v, sden[:, 2 * (u % 8):2 * (u % 8) + 2].unsqueeze(2).broadcast_to([P, 2, wk]),
                                        ALU.mult).then_inc(*signal("sprob", u))

            eye8 = ident.unsqueeze(1).broadcast_to([P, NC, P])
            m16T = cst("m16T").unsqueeze(1).broadcast_to([P, NC, P])
            for j in range(NJ):
                pool.wait_ge(*copied("kk", j, 0))
                pool.wait_ge(*copied("kk", j, 1))
                nc.gpsimd.tensor_tensor(blk[3], blk[2], m16T, ALU.mult).then_inc(*signal("dT", j))
                pool.wait_ge(*done("dT", j))
                nc.gpsimd.tensor_tensor(blk[4], eye8, blk[3], ALU.subtract).then_inc(*signal("p0", j))
                for point in range(6):
                    window(j, point)

            def square_sum(tag):
                for m in range(1, KD):
                    pool.wait_ge(*done("xsq" + tag, m))
                    if m > 1:
                        pool.wait_ge(*done("sqsum" + tag, m - 1))
                    nc.gpsimd.tensor_tensor(sacc, sacc, hsq[m % 2], ALU.add).then_inc(*signal("sqsum" + tag, m))

            square_sum("2")
            square_sum("3")
            pool.wait_ge(*filled("fd", 1, 7))
            pool.dma_start(rope[HD:QD, :, :], a["rope"].rearrange("r (s t) -> r s t", s=2)).then_inc(sem("ld_rope"), 16)
            half = QK_ROPE // 2
            pool.wait_ge(*copied("kr", 0))
            pool.wait_ge(*copied("kr", 1))
            for d0, s0 in ((HD, HD + half), (HD + half, HD)):
                pool.dma_start(krs[d0:d0 + half, :], kr[s0:s0 + half, :]).then_inc(sem("ld_krs"), 16)
            for g in range(4):
                for h in (2 * g, 2 * g + 1):
                    pool.wait_ge(*copied("q", h))
                if g:
                    pool.wait_ge(*done("qrope", g - 1))
                for d0, s0 in ((HD, HD + half), (HD + half, HD)):
                    pool.dma_start(qsw[d0:d0 + half, :, :], qh[s0:s0 + half, 2 * g:2 * g + 2, :])\
                        .then_inc(sem("ld_qsw"), 16)
            for u, (i, h) in enumerate(MLU):
                n = keys_of[i]
                pool.wait_ge(*done("mrec", u))
                v = mpr[u % 2][:, 0:n]
                nc.gpsimd.tensor_tensor(v, v, sden[:, u % 16:u % 16 + 1].broadcast_to([P, n]), ALU.mult)\
                    .then_inc(*signal("mprob", u))
            pool.wait_ge(*done("m", 0))
            pool.dma_start(post[:, :], a["post_norm_g_2"].broadcast_to([P, D])).then_inc(sem("ld_post"), 16)

        @block.scalar
        def _(act):
            A = nc.scalar.activation
            act.wait_ge(*filled("vec"))
            A(V1[:, :], bank("vec")[:, 0:V1_N], ACT.Copy).then_inc(*signal("v1"))
            A(V2[:, :], bank("vec")[:, P:P + V2_N], ACT.Copy).then_inc(*read("vec"))
            act.wait_ge(*done("v1"))
            A(cs, V1[:, V1_ROWS["c"]:V1_ROWS["c"] + 8], ACT.Silu).then_inc(*signal("cs"))
            act.wait_ge(*arrived("x", 2))
            for b in range(4):
                A(hpre[:, 0:2, :], xin[:, b, :].rearrange("p (k t) -> p k t", k=2), ACT.Square,
                  accum_out=ssum[:, b:b + 1]).then_inc(*signal("xss", b))
                act.wait_ge(*done("xss", b))
            A(hpre[0:META, 0:2, :], min_[0:META, :].rearrange("p (k t) -> p k t", k=2), ACT.Square,
              accum_out=msum[0:META, 0:1]).then_inc(*signal("mss"))
            act.wait_ge(*done("eps"))
            act.wait_ge(*done("mss"))
            A(sroot, ssum, ACT.Sqrt, bias=epsc, scale=1.0 / D).then_inc(*signal("root1"))
            A(msum[0:META, 0:1], msum[0:META, 0:1], ACT.Sqrt, bias=epsc[0:META, :], scale=1.0 / D)\
                .then_inc(*signal("rootmeta"))
            for k in range(KD):
                act.wait_ge(*filled("x", k))
                A(xT[:, k, :], bank("x", k)[:, :], ACT.Copy).then_inc(*read("x", k))
            act.wait_ge(*filled("meta"))
            A(hmeta, bank("meta")[:, 0:8 * META], ACT.Copy).then_inc(*read("meta"))

            def root(tag, out, key, scale, bias):
                act.wait_ge(*filled(*key))
                A(out, bank(*key)[0:out.shape[0], 0:out.shape[1]], ACT.Sqrt, bias=bias, scale=scale).then_inc(*read(*key))

            split_hi = splitter(act, lambda hi, src: A(hi, src, ACT.Copy), None)

            def hi_part(stage, index, dst, src):
                A(dst, src, ACT.Copy).then_inc(*signal(stage + "_hi", *index))

            def modulate(tag, scale, shift):
                for k in range(KD + 1):
                    if k < KD:
                        act.wait_ge(*done("xn" + tag, k))
                        A(hpre[:, k, :], hpre[:, k, :], ACT.Identity, scale=scale[:, k:k + 1],
                          bias=modT[:, shift + k:shift + k + 1]).then_inc(*signal("mod" + tag, k))
                    if k:
                        act.wait_ge(*done("mod" + tag, k - 1))
                        hi_part("h" + tag, (k - 1,), hs[:, 0, k - 1, real], hpre[:, k - 1, :])

            split_hi()
            split_hi()
            act.wait_ge(*done("modA1"))
            modulate("1", modA1, 0)
            def conv_in(m):
                act.wait_ge(*filled("pj", m))
                if m >= 3:
                    act.wait_ge(*done("conv", m - 3, 3))
                A(raw[m % 3][:, 3:], bank("pj", m)[:, :], ACT.Copy).then_inc(*read("pj", m))

            def conv_out(m):
                act.wait_ge(*done("conv", m, 3))
                A(qkv[:, m, :], qkv[:, m, :], ACT.Silu).then_inc(*signal("silu", m))

            act.wait_ge(*done("rawpad"))
            def head_square(m):
                if m >= 2:
                    act.wait_ge(*done("hsum_step", m - 2))
                act.wait_ge(*done("silu", m))
                A(hsq[m % 2], qkv[:, m, :], ACT.Square).then_inc(*signal("hsq", m))

            for m in range(14):
                if m < 12:
                    conv_in(m)
                    if m % 2:
                        split_hi()
                if m >= 2:
                    conv_out(m - 2)
                if 3 <= m < 11:
                    head_square(m - 3)
            act.wait_ge(*filled("ab"))
            A(gt[3][0:40, :], bank("ab")[0:40, :], ACT.Copy).then_inc(*read("ab"))
            act.wait_ge(*filled("hsum"))
            A(hrs[0][0:40, :], bank("hsum")[0:40, :], ACT.Sqrt, bias=epsc[0:40, :]).then_inc(*read("hsum"))
            act.wait_ge(*filled("sk"))
            A(sk, bank("sk")[:, :], ACT.Copy).then_inc(*read("sk"))
            act.wait_ge(*copied("sk"))
            A(hsq[0], sk, ACT.Square).then_inc(*signal("hsq", 8))
            split_hi()
            act.wait_ge(*filled("sv"))
            A(sv, bank("sv")[:, :], ACT.Copy).then_inc(*read("sv"))
            split_hi()
            act.wait_ge(*filled("sksum"))
            A(hrs[1], bank("sksum")[:, :], ACT.Sqrt, bias=epsc, scale=1.0 / HD).then_inc(*read("sksum"))
            for m in range(4):
                act.wait_ge(*filled("sq", m))
                A(sq[:, m, :], bank("sq", m)[:, :], ACT.Copy).then_inc(*read("sq", m))
                if m >= 2:
                    act.wait_ge(*done("sqsum_step", m - 2))
                act.wait_ge(*copied("sq", m))
                A(hsq[(9 + m) % 2], sq[:, m, :], ACT.Square).then_inc(*signal("hsq", 9 + m))
                if m % 2:
                    split_hi()
            for m in range(4):
                act.wait_ge(*filled("gz", m))
                A(gz[:, m, :], bank("gz", m)[:, :], ACT.Silu).then_inc(*read("gz", m))
                if m == 1:
                    act.wait_ge(*filled("sqsum"))
                    A(rq, bank("sqsum")[:, 0:32], ACT.Sqrt, bias=eps64).then_inc(*read("sqsum"))
            act.wait_ge(*filled("vs"))
            A(vs, bank("vs")[:, :].rearrange("p (b d) -> p b d", b=NB), ACT.Copy).then_inc(*read("vs"))
            act.wait_ge(*copied("ab"))
            A(gt[0][32:40, :], gt[3][32:40, :], ACT.Exp, scale=-1.0).then_inc(*signal("egb"))
            act.wait_ge(*arrived("gate", 3))
            A(nega[0:8, :], nega[0:8, :], ACT.Exp).then_inc(*signal("ealog"))
            act.wait_ge(*done("nabs"))
            A(gt[2][0:8, :], gt[2][0:8, :], ACT.Exp).then_inc(*signal("eabs"))
            act.wait_ge(*done("eabs"))
            A(gt[2][0:8, :], gt[2][0:8, :], ACT.Ln, bias=1.0).then_inc(*signal("lnabs"))
            act.wait_ge(*done("skn"))
            act.wait_ge(*done("kpad0"))
            for g in range(2):
                for p in range(2):
                    last = A(kpad[p * HD:(p + 1) * HD, g, p, :], sk[g * HD:(g + 1) * HD, :], ACT.Copy)
                    last.then_inc(*(signal("kpad") if g and p else signal("kpad_part")))
            act.wait_ge(*filled("cols"))
            cps = bank("cols")[:, 0:256].rearrange("p (n s j h) -> p h n s j", n=NC, s=4, j=NJ)
            colv = cols.rearrange("p (n s j) -> p n s j", n=NC, s=4)
            for h in range(2):
                rows = slice(h * HD, (h + 1) * HD)
                A(colv[rows].rearrange("p n s j -> p n (s j)"), cps[rows, h].rearrange("p n s j -> p n (s j)"), ACT.Copy)\
                    .then_inc(*(read("cols") if h else signal("cols_low")))

            def sw_exp(u):
                b, hp = SWU[u]
                wk = WIN if b == 0 else 2 * WIN
                act.wait_ge(*done("snmax", u))
                if u >= 2:
                    act.wait_ge(*filled("st", u - 2))
                s2 = 2 * (u % 8)
                for p in range(2):
                    A(pr[u % 2][:, p * wk:(p + 1) * wk], sc[u % 2][:, p * wk:(p + 1) * wk], ACT.Exp,
                      bias=snmax[:, s2 + p:s2 + p + 1], accum_out=ssumx[:, s2 + p:s2 + p + 1])\
                        .then_inc(*signal("sexp", u, p))
                A(sesk[:, s2:s2 + 2], sesk[:, s2:s2 + 2], ACT.Exp).then_inc(*signal("sesk", u))

            def sw_copy(u):
                b, hp = SWU[u]
                n = 2 * WIN if b == 0 else 4 * WIN
                act.wait_ge(*filled("st", u))
                if u >= 2:
                    b2, hp2 = SWU[u - 2]
                    act.wait_ge(*(filled("so", b2) if hp2 == 3 else done("so_step", u - 2)))
                A(prT[u % 2][:, 0:n], bank("st", u)[:, 0:n], ACT.Copy).then_inc(*read("st", u))

            def sw_result(u):
                b, hp = SWU[u]
                if hp == 3:
                    act.wait_ge(*filled("so", b))
                    A(sq[:, :, b * WIN:(b + 1) * WIN], bank("so", b)[:, :].rearrange("p (h t) -> p h t", h=4),
                      ACT.Copy).then_inc(*read("so", b))

            def window(j, point):
                u = 6 * j + point
                if 0 <= u - 3 < len(SWU):
                    sw_copy(u - 3)
                if 0 <= u - 4 < len(SWU):
                    sw_result(u - 4)
                if 0 <= u - 1 < len(SWU):
                    sw_exp(u - 1)
                if u in (20, 21):
                    split_hi()

            v4 = lambda t: t.rearrange("p (n c) -> p n c", n=4)
            for j in range(NJ):
                if j == 0:
                    act.wait_ge(*done("bdzero"))
                else:
                    act.wait_ge(*filled("go", j - 1))
                for half, (dst, m) in enumerate(((blk[0], 4 + j), (blk[1], 8 + j))):
                    for h in range(2):
                        rows = slice(h * HD, (h + 1) * HD)
                        A(dst[rows, :, h * HD:(h + 1) * HD],
                          qkv[rows, m, :].rearrange("p (n c) -> p n c", n=NC), ACT.Copy)\
                            .then_inc(*(signal("kbd", j) if half and h else signal("bd_part", j, half, h)))
                act.wait_ge(*filled("rows", j, 0))
                A(g_row, bank("rows", j, 0)[:, :].rearrange("p (n c) -> p n c", n=NC), ACT.Copy).then_inc(*read("rows", j, 0))
                act.wait_ge(*done("emin", j))
                A(e_, e_, ACT.Exp).then_inc(*signal("e", j))
                act.wait_ge(*copied("rows", j, 0))
                A(gx, g_row, ACT.Exp).then_inc(*signal("gx", j))
                A(cA, colv[:, :, 0, j], ACT.Exp).then_inc(*signal("cAexp", j))
                A(eglast, g_row[:, :, CH - 1], ACT.Exp).then_inc(*signal("eglast", j))
                act.wait_ge(*done("cBarg", j))
                A(cB, cB, ACT.Exp).then_inc(*signal("cBexp", j))

                def move(name, dst, scale=1.0, waits=()):
                    for w in waits:
                        act.wait_ge(*w)
                    for half in range(2):
                        act.wait_ge(*filled(name, j, half))
                        A(dst[:, 4 * half:4 * half + 4, :], v4(bank(name, j, half)[:, :]), ACT.Copy, scale=scale)\
                            .then_inc(*read(name, j, half))

                window(j, 0)
                move("d2", blk[8])
                move("d2T", blk[9])
                window(j, 1)
                move("d4", blk[2], waits=[done("p0", j)])
                move("d4T", blk[3])
                move("d8", blk[5])
                window(j, 2)
                move("t16", blk[2])
                move("z1", blk[3])
                window(j, 3)
                move("t32", blk[5])
                move("z2", blk[3])
                move("wT", blk[6], scale=-1.0)
                for n in range(NC):
                    if n in (2, 5):
                        window(j, 4 + n // 3)
                    act.wait_ge(*filled("vn", j, n))
                    A(vnew[n % 2], bank("vn", j, n)[:, 0:P], ACT.Copy).then_inc(*read("vn", j, n))
                act.wait_ge(*filled("go", j))
                A(qkv[:, j, :], bank("go", j)[:, :], ACT.Copy).then_inc(*read("go", j))
            for j in range(NJ):
                act.wait_ge(*copied("go", j))
                if j >= 2:
                    act.wait_ge(*done("osum_step", j - 2))
                A(hsq[j % 2], qkv[:, j, :], ACT.Square).then_inc(*signal("osq", j))
            act.wait_ge(*filled("osum"))
            A(hrs[1][0:40, :], bank("osum")[0:40, :], ACT.Sqrt, bias=epsc[0:40, :], scale=1.0 / HD).then_inc(*read("osum"))

            for k in (4, 5, 6, 7, 0, 1, 2, 3):
                if k < 4:
                    act.wait_ge(*done("mixg", k))
                else:
                    act.wait_ge(*copied("so", NB - 1))
                hi_part("mix", (k,), hs[:, 0, k, real], qkv[:, k, :] if k < 4 else sq[:, k - 4, :])

            def square_of(tag, m):
                if m >= 3:
                    act.wait_ge(*done("sqsum" + tag, m - 2))
                A(hsq[m % 2] if m else sacc, xT[:, m, :], ACT.Square).then_inc(*signal("xsq" + tag, m))

            for m in range(KD):
                act.wait_ge(*copied("mo", m))
                square_of("2", m)
                if m % 2:
                    split_hi()
            root("2", sroot, ("sum2",), 1.0 / D, epsc)
            act.wait_ge(*done("modA2"))
            modulate("2", modA2, 24)
            for part, (c0, n) in enumerate(FFN_PARTS):
                for i in range(c0 // 2, (c0 + n) // 2):
                    for k in (2 * i, 2 * i + 1):
                        act.wait_ge(*filled("fg", k))
                        if k >= 2:
                            act.wait_ge(*done("a", k - 2))
                        A(silug[k % 2], bank("fg", k)[:, :], ACT.Silu).then_inc(*read("fg", k))
                    split_hi()
                    for k in (2 * i, 2 * i + 1):
                        act.wait_ge(*copied("fu", k))
                        hi_part("a", (k,), a_s[:, 0, k - c0, :], silug[k % 2])
                    split_hi()
                for m in range(KD):
                    act.wait_ge(*copied("fd", part, m))
                    if part:
                        square_of("3", m)
                    split_hi()
            act.wait_ge(*filled("fu", KF - 1))
            A(hs[:, 0, :, 0:META], hmeta.rearrange("p (k t) -> p k t", k=KD), ACT.Copy).then_inc(*signal("meta_hi"))
            root("3", sroot, ("sum3",), 1.0 / D, epsc)
            for k in range(KD):
                act.wait_ge(*done("xn3", k))
                hi_part("h3", (k,), hs[:, 0, k, real], hpre[:, k, :])

            H2 = TM // 2

            def both(key, dst, func=ACT.Copy):
                for half in range(2):
                    act.wait_ge(*filled(*key, half))
                    A(dst[:, half * H2:(half + 1) * H2], bank(*key, half)[:, 0:H2], func).then_inc(*read(*key, half))

            for m in range(2):
                both(("cgate", m), ga_[m], ACT.Sigmoid)
            split_hi()
            split_hi()
            for m in range(2):
                both(("pv", m), pv[m])
            split_hi()
            for m in range(2):
                act.wait_ge(*filled("pg", m))
                A(pg[:, m, :], bank("pg", m)[:, :], ACT.Silu).then_inc(*read("pg", m))
            split_hi()
            for m in range(2):
                act.wait_ge(*filled("cg", m))
                A(ybr[:, 6 + m, :], bank("cg", m)[:, :], ACT.Silu).then_inc(*read("cg", m))
            split_hi()
            for m in range(2):
                act.wait_ge(*filled("bg", m))
                A(bg[:, m, :], bank("bg", m)[:, :], ACT.Copy).then_inc(*read("bg", m))
            split_hi()
            for m in range(2):
                both(("cgx", m), cgx[m])
            split_hi()
            split_hi()
            for m in range(2):
                act.wait_ge(*filled("sg", m))
                A(ybr[:, 8 + m, :], bank("sg", m)[:, :], ACT.Silu).then_inc(*read("sg", m))
            split_hi()
            for m in range(2):
                act.wait_ge(*filled("cq", m))
                A(cq[:, m, :], bank("cq", m)[:, :], ACT.Copy).then_inc(*read("cq", m))
            split_hi()

            def mla_gate(m):
                act.wait_ge(*filled("mg", m))
                A(ybr[:, 2 + m, :], bank("mg", m)[:, :], ACT.Silu).then_inc(*read("mg", m))

            mla_gate(0)
            mla_gate(1)
            split_hi()
            act.wait_ge(*filled("cmean"))
            A(cmr[:, 0, :], bank("cmean")[:, :], ACT.Copy, scale=1.0 / 256).then_inc(*read("cmean"))
            for m in range(2):
                act.wait_ge(*done("ccen", m))
                A(csq[:, m, :], cacc[:, m, :], ACT.Square).then_inc(*signal("cvar_in", m))
            both(("ckv",), ckv)
            act.wait_ge(*filled("cvar"))
            A(cmr[:, 1, :], bank("cvar")[:, :], ACT.Sqrt, scale=1.0 / 256, bias=epsc).then_inc(*read("cvar"))
            for half in range(2):
                act.wait_ge(*filled("kr", half))
                A(kr[HD:QD, half * H2:(half + 1) * H2], bank("kr", half)[HD:QD, 0:H2], ACT.Copy).then_inc(*read("kr", half))
            split_hi()
            mla_gate(2)
            mla_gate(3)
            split_hi()
            for m in range(2):
                act.wait_ge(*done("cnorm", m))
                A(cacc[:, m, :], cacc[:, m, :], ACT.Silu, scale=V1[:, V1_ROWS["ln_g"] + m:V1_ROWS["ln_g"] + m + 1],
                  bias=V1[:, V1_ROWS["ln_b"] + m:V1_ROWS["ln_b"] + m + 1]).then_inc(*signal("csilu", m))
            for k in range(2):
                act.wait_ge(*copied("cq", k))
                A(qsw[:, k, :], cq[:, k, :], ACT.Square).then_inc(*signal("cqsq", k))
            act.wait_ge(*copied("ckv", 1))
            A(ksq, ckv, ACT.Square).then_inc(*signal("ckvsq"))
            act.wait_ge(*filled("cqsum"))
            A(rqm, bank("cqsum")[:, 0:4], ACT.Sqrt, scale=float(QD) / 256, bias=eps96).then_inc(*read("cqsum"))
            for half in range(2):
                act.wait_ge(*filled("kvsum", half))
                A(krb[:, half * H2:(half + 1) * H2], bank("kvsum", half)[:, 0:H2], ACT.Sqrt, scale=1.0 / P, bias=epsc)\
                    .then_inc(*read("kvsum", half))
            for k in range(2):
                act.wait_ge(*copied("py", k))
                act.wait_ge(*done("yc", k))
                act.wait_ge(*done("yd", k))
            for h in range(8):
                act.wait_ge(*filled("q", h))
                A(qh[0:QD, h, :], bank("q", h)[0:QD, :], ACT.Copy).then_inc(*read("q", h))
            for h in range(8):
                for half in range(2):
                    act.wait_ge(*filled("k", h, half))
                    A(kh[0:HD, h, half * H2:(half + 1) * H2], bank("k", h, half)[0:HD, 0:H2], ACT.Copy)\
                        .then_inc(*read("k", h, half))
            for b in range(5):
                n = P if b < 4 else META
                act.wait_ge(*filled("v", b))
                if b == 4:
                    act.wait_ge(*done("vpad"))
                A(vv[0:n, b, :], bank("v", b)[0:n, :], ACT.Copy).then_inc(*read("v", b))

            act.wait_ge(*done("rqm"))

            def ml_in(u):
                i, h = MLU[u]
                n = keys_of[i]
                m0 = min(n, 512)
                if u >= 2:
                    act.wait_ge(*done("mexp", u - 2))
                act.wait_ge(*filled("ms", u))
                A(msc[u % 2][:, 0:m0], bank("ms", u)[:, 0:m0], ACT.Copy, scale=rqm[:, i:i + 1]).then_inc(*read("ms", u))
                if n > 512:
                    act.wait_ge(*filled("ms2", u))
                    A(msc[u % 2][:, 512:n], bank("ms2", u)[:, 0:n - 512], ACT.Copy, scale=rqm[:, i:i + 1])\
                        .then_inc(*read("ms2", u))

            def ml_exp(u):
                i, h = MLU[u]
                n = keys_of[i]
                act.wait_ge(*done("mmax", u))
                if u >= 2:
                    act.wait_ge(*filled("mr", u - 2))
                c = u % 16
                A(mpr[u % 2][:, 0:n], msc[u % 2][:, 0:n], ACT.Exp, bias=snmax[:, c:c + 1], accum_out=ssumx[:, c:c + 1])\
                    .then_inc(*signal("mexp", u))

            def ml_copy(u):
                i, h = MLU[u]
                act.wait_ge(*filled("mt", u))
                if u >= 2:
                    i2, h2 = MLU[u - 2]
                    act.wait_ge(*(filled("mo2", i2) if h2 == 7 else done("mo_step", u - 2)))
                A(mpT[u % 2][:, 0:(i + 1) * WIN], bank("mt", u)[:, 0:(i + 1) * WIN], ACT.Copy).then_inc(*read("mt", u))
                act.wait_ge(*filled("mr", u))
                if u < 2:
                    act.wait_ge(*done("vpad"))
                A(mpR[u % 2][0:META, :], bank("mr", u)[0:META, 0:WIN], ACT.Copy).then_inc(*read("mr", u))

            def gate(dst, m, b):
                act.wait_ge(*filled("gl", m, b))
                c = V1_ROWS["gate_bias"] + 8 * b + m
                A(dst, bank("gl", m, b)[:, :], ACT.Sigmoid, bias=V1[:, c:c + 1]).then_inc(*read("gl", m, b))

            for u in range(len(MLU) + 2):
                if u < len(MLU):
                    ml_in(u)
                if 1 <= u <= len(MLU):
                    ml_exp(u - 1)
                if u >= 2:
                    ml_copy(u - 2)
                if u and u % 4 == 0:
                    m, b = MIX_EARLY[u // 4 - 1]
                    dst, before = early_gate(u // 4 - 1)
                    if before:
                        act.wait_ge(*(done("gadd", *before) if before[1] else copied("y", *before)))
                    gate(dst, m, b)
                    if u in (8, 16, 24):
                        split_hi()
            split_hi()
            for m in range(2):
                act.wait_ge(*done("macc", m))
                hi_part("m", (m,), ms_[:, 0, m, :], macc_of(m))
            act.wait_ge(*done("gadd", 1, 3))

            for m in range(2, KD):
                for b in range(4):
                    x = 4 * m + b
                    if x >= 10:
                        act.wait_ge(*copied("y", (x - 2) // 4, (x - 2) % 4))
                    gate(sg[x % 2], m, b)
                    if b % 2:
                        split_hi()
                    if b == 0 and m > 2:
                        act.wait_ge(*done("macc", m - 1))
                        hi_part("m", (m - 1,), ms_[:, 0, m - 1, :], macc_of(m - 1))
            act.wait_ge(*done("macc", KD - 1))
            hi_part("m", (KD - 1,), ms_[:, 0, KD - 1, :], macc[(KD - 1) % 2])
            for b in range(4):
                for half in range(2):
                    act.wait_ge(*filled("xt", b, half))
                    A(xtok[:, b, half * 512:(half + 1) * 512], bank("xt", b, half)[:, :], ACT.Copy)\
                        .then_inc(*read("xt", b, half))
            split_hi()
            for half in range(2):
                for b in range(4):
                    if b or half:
                        act.wait_ge(*done("fss", *((b - 1, half) if b else (3, 0))))
                    act.wait_ge(*filled("fo", b, half))
                    A(fjunk, bank("fo", b, half)[:, :], ACT.Square, accum_out=fss[:, 2 * b + half:2 * b + half + 1])\
                        .then_inc(*signal("fss", b, half))
                if half == 0:
                    split_hi()
            for b in range(4):
                act.wait_ge(*done("ftot", b))
                A(frs[:, b:b + 1], fss[:, 2 * b:2 * b + 1], ACT.Sqrt, scale=1.0 / D, bias=epsc).then_inc(*signal("froot", b))
                act.wait_ge(*done("fin", b))
                act.dma_start(out[0].rearrange("(b p) f -> b p f", p=P)[b], fin[b]).then_inc(sem("stored"), 16)

        @block.vector
        def _(dve):
            v = nc.vector
            chain = [0]

            def link(ins):
                chain[0] += 1
                ins.then_inc(sem("dve_chain"), 1)
                dve.wait_ge(sem("dve_chain"), chain[0])

            def col(name, i=0, n=1):
                r = V1_ROWS[name] + i
                return V1[:, r:r + n]

            tt, ts, stt = v.tensor_tensor, v.tensor_scalar, v.scalar_tensor_tensor

            link(v.memset(gates, 0.0))
            v.memset(epsc, EPS)
            v.memset(eps64, EPS * HD)
            v.memset(eps96, EPS * QD).then_inc(*signal("eps"))
            split_lo = splitter(dve, None, lambda lo, src, hi: tt(lo, src, hi, ALU.subtract))

            def lo_part(stage, index, dst, src, hi):
                dve.wait_ge(*done(stage + "_hi", *index))
                tt(dst, src, hi.bitcast(F32), ALU.subtract).then_inc(*signal(stage, *index))

            def spread(tag, dg):
                dve.wait_ge(*(done("root1") if tag == "1" else copied("sum" + tag)))
                link(v.reciprocal(srstd, sroot))
                for b in range(4):
                    last = ts(dg[:, b, :], ident, srstd[:, b:b + 1], None, ALU.mult)
                    last.then_inc(*(signal("diag" + tag) if b == 3 else signal("diag_part" + tag)))

            spread("1", diag)
            dve.wait_ge(*done("rootmeta"))
            link(v.reciprocal(msum[0:META, 1:2], msum[0:META, 0:1]))
            ts(rbc[0:META, 0:META], ident[0:META, 0:META], msum[0:META, 1:2], None, ALU.mult)\
                .then_inc(*signal("diagmeta"))
            dve.wait_ge(*copied("meta"))
            hm = hmeta.rearrange("p (k t) -> p k t", k=KD)
            dve.wait_ge(*filled("spreadmeta"))
            for k in range(KD):
                last = stt(out=hm[:, k, :], in0=hm[:, k, :], scalar=col("pre", k), in1=bank("spreadmeta")[:, 0:META],
                           op0=ALU.mult, op1=ALU.mult)
                last.then_inc(*(read("spreadmeta") if k == KD - 1 else signal("hmeta", k)))

            def ada_sum(i):
                if i >= 2:
                    dve.wait_ge(*filled("ada", i - 2))
                acc = adaacc[i % 2]
                for h in range(2):
                    dve.wait_ge(*loaded(f"ada{i}{h}"))
                    w = W(f"ada{i}{h}")
                    for k in range(4):
                        c = cs[:, 4 * h + k:4 * h + k + 1]
                        if h + k == 0:
                            link(ts(acc, w[:, 0, :], c, None, ALU.mult))
                            continue
                        last = stt(out=acc, in0=w[:, k, :], scalar=c, in1=acc, op0=ALU.mult, op1=ALU.add)
                        if k < 3:
                            link(last)
                    last.then_inc(*signal("adaacc" if h else "adapart", i))
                    if h == 0:
                        dve.wait_ge(*done("adapart", i))

            def ada_mod(i):
                dve.wait_ge(*filled("ada", i))
                tt(modT[:, 4 * i:4 * i + 4], bank("ada", i)[:, 0:4], col("b_ada", 4 * i, 4), ALU.add)\
                    .then_inc(*read("ada", i))

            def normed(tag, stage):
                dve.wait_ge(*filled("spread" + tag))
                for k in range(KD):
                    ins = tt(hpre[:, k, :], xT[:, k, :], bank("spread" + tag)[:, :], ALU.mult)
                    ins.then_inc(*signal(stage, k))
                dve.wait_ge(*done(stage, KD - 1))
                v.engine_nop().then_inc(*read("spread" + tag))

            def h_rest(tag):
                for k in range(KD):
                    lo_part("h" + tag, (k,), hs[:, 1, k, real], hpre[:, k, :], hs[:, 0, k, real])

            normed("1", "xn1")
            dve.wait_ge(*done("cs"))
            for i in range(4):
                ada_sum(i)
                if i:
                    ada_mod(i - 1)
            ada_mod(3)
            dve.wait_ge(*copied("ada", 3))
            stt(out=modA1, in0=modT[:, 8:16], scalar=1.0, in1=col("norm1", 0, 8), op0=ALU.add, op1=ALU.mult)\
                .then_inc(*signal("modA1"))

            split_lo()
            h_rest("1")
            split_lo()
            dve.wait_ge(*done("h1", KD - 1))
            for i in range(2):
                v.memset(raw[i][:, 0:3], 0.0)
            v.memset(raw[2][:, 0:3], 0.0).then_inc(*signal("rawpad"))

            def conv4(m):
                dve.wait_ge(*copied("pj", m))
                tap = lambda k: V2[:, 12 * k + m:12 * k + m + 1]
                ts(qkv[:, m, :], raw[m % 3][:, 0:T], tap(0), None, ALU.mult).then_inc(*signal("conv", m, 0))
                for k in range(1, 4):
                    dve.wait_ge(*done("conv", m, k - 1))
                    stt(out=qkv[:, m, :], in0=raw[m % 3][:, k:k + T], scalar=tap(k), in1=qkv[:, m, :],
                        op0=ALU.mult, op1=ALU.add).then_inc(*signal("conv", m, k))

            for m in range(12):
                conv4(m)
                if m % 2:
                    split_lo()
                    if m >= 5:
                        ada_mod(4 + (m - 5) // 2)
                    if m <= 7:
                        ada_sum(4 + (m - 1) // 2)
            ada_sum(8)
            dve.wait_ge(*copied("ab"))
            dve.wait_ge(*arrived("gate", 3))
            link(ts(gt[1][0:8, :], gt[3][0:8, :], dtb[0:8, :], None, ALU.add))
            stt(out=gt[2][0:8, :], in0=gt[1][0:8, :], scalar=-1.0, in1=gt[1][0:8, :], op0=ALU.mult, op1=ALU.min)\
                .then_inc(*signal("nabs"))
            dve.wait_ge(*copied("hsum"))
            link(v.reciprocal(grow_[0:40, :], hrs[0][0:40, :]))
            link(ts(grow_[0:8, :], grow_[0:8, :], float(HD) ** -0.5, None, ALU.mult))
            split_lo()
            split_lo()
            ada_sum(9)
            dve.wait_ge(*copied("sksum"))
            link(v.reciprocal(hrs[1], hrs[1]))
            link(tt(wqk, col("qn"), col("kn"), ALU.mult))
            dve.wait_ge(*copied("sk"))
            stt(out=sk, in0=sk, scalar=wqk, in1=hrs[1], op0=ALU.mult, op1=ALU.mult).then_inc(*signal("skn"))
            split_lo()
            split_lo()
            ada_mod(8)
            dve.wait_ge(*copied("sqsum"))
            link(v.reciprocal(rq, rq))
            ada_mod(9)
            dve.wait_ge(*copied("ada", 9))
            stt(out=modA2, in0=modT[:, 32:40], scalar=1.0, in1=col("norm2", 0, 8), op0=ALU.add, op1=ALU.mult)\
                .then_inc(*signal("modA2"))
            dve.wait_ge(*done("egb"))
            link(ts(gt[0][32:40, :], gt[0][32:40, :], 1.0, None, ALU.add))
            link(v.reciprocal(gt[0][32:40, :], gt[0][32:40, :]))
            link(v.tensor_copy(grow_[64:72, :], gt[0][32:40, :]))
            link(tt(glog[32:40, :], gt[0][32:40, :], grow_[32:40, :], ALU.mult))
            dve.wait_ge(*done("lnabs"))
            dve.wait_ge(*done("ealog"))
            link(ts(gt[1][0:8, :], gt[1][0:8, :], 0.0, None, ALU.max))
            link(tt(gt[1][0:8, :], gt[1][0:8, :], gt[2][0:8, :], ALU.add))
            link(ts(gt[1][0:8, :], gt[1][0:8, :], nega[0:8, :], -1.0, ALU.mult, ALU.mult))
            v.tensor_tensor_scan(glog[0:8, :], cst("reset", 8), gt[1][0:8, :], 0.0, ALU.mult, ALU.add)\
                .then_inc(*signal("grows"))

            dve.wait_ge(*arrived("alibi"))

            def sw_bias(u):
                b, hp = SWU[u]
                wk = WIN if b == 0 else 2 * WIN
                dve.wait_ge(*filled("ss", u))
                if u >= 2:
                    dve.wait_ge(*done("sexp", u - 2, 1))
                for p in range(2):
                    h = 2 * hp + p
                    al = alibi[:, h * 2 * WIN + (2 * WIN - wk):(h + 1) * 2 * WIN]
                    ins = stt(out=sc[u % 2][:, p * wk:(p + 1) * wk], in0=bank("ss", u)[:, p * wk:(p + 1) * wk],
                              scalar=rq[:, b * 8 + h:b * 8 + h + 1], in1=al, op0=ALU.mult, op1=ALU.add)
                    ins.then_inc(*(read("ss", u) if p else signal("sbias", u)))
                dve.wait_ge(*copied("ss", u))
                s2 = 2 * (u % 8)
                link(v.reduce_max(smax[:, s2:s2 + 2], sc[u % 2][:, 0:2 * wk].rearrange("p (h k) -> p h k", h=2), AX.X))
                link(tt(smax[:, s2:s2 + 2], smax[:, s2:s2 + 2], sinks[:, 2 * hp:2 * hp + 2], ALU.max))
                link(ts(snmax[:, s2:s2 + 2], smax[:, s2:s2 + 2], -1.0, None, ALU.mult))
                tt(sesk[:, s2:s2 + 2], sinks[:, 2 * hp:2 * hp + 2], snmax[:, s2:s2 + 2], ALU.add)\
                    .then_inc(*signal("snmax", u))

            def sw_sum(u):
                s2 = 2 * (u % 8)
                dve.wait_ge(*done("sexp", u, 1))
                dve.wait_ge(*done("sesk", u))
                link(tt(sden[:, s2:s2 + 2], ssumx[:, s2:s2 + 2], sesk[:, s2:s2 + 2], ALU.add))
                v.reciprocal(sden[:, s2:s2 + 2], sden[:, s2:s2 + 2]).then_inc(*signal("srec", u))

            def window(j, point):
                u = 6 * j + point
                if u < len(SWU):
                    sw_bias(u)
                if 0 <= u - 2 < len(SWU):
                    sw_sum(u - 2)
                if u in (20, 21):
                    split_lo()

            v4 = lambda t: t.rearrange("p (n c) -> p n c", n=4)
            v8 = lambda t: t.rearrange("p (n c) -> p n c", n=NC)
            over_c = lambda c: c.unsqueeze(2).broadcast_to([P, NC, CH])
            colv = cols.rearrange("p (n s j) -> p n s j", n=NC, s=4)
            mask64 = lambda name: cst(name).unsqueeze(1).broadcast_to([P, NC, CH])
            mask4 = lambda name: cst(name).unsqueeze(1).broadcast_to([P, 4, P])
            link(v.memset(blk[0], 0.0))
            v.memset(blk[1], 0.0).then_inc(*signal("bdzero"))
            dve.wait_ge(*copied("cols"))
            for j in range(NJ):
                gcolj, brkj, rkj, betaj = (colv[:, :, s, j] for s in range(4))
                dve.wait_ge(*copied("rows", j, 0))
                link(tt(e_, g_row, over_c(gcolj), ALU.subtract))
                ts(e_, e_, 0.0, None, ALU.min).then_inc(*signal("emin", j))
                tt(cB, g_row[:, :, CH - 1], gcolj, ALU.subtract).then_inc(*signal("cBarg", j))
                dve.wait_ge(*done("e", j))
                link(tt(e_, e_, over_c(rkj), ALU.mult))
                dve.wait_ge(*filled("rows", j, 1))
                tt(w1, e_, v8(bank("rows", j, 1)[:, :]), ALU.mult).then_inc(*read("rows", j, 1))
                dve.wait_ge(*copied("rows", j, 1))
                link(tt(w1, w1, mask64("strictT"), ALU.mult))
                dve.wait_ge(*filled("rows", j, 2))
                link(tt(w2, e_, v8(bank("rows", j, 2)[:, :]), ALU.mult))
                link(tt(w2, w2, mask64("inclT"), ALU.mult))
                dve.wait_ge(*done("gx", j))
                tt(qe, gx, v8(bank("rows", j, 2)[:, :]), ALU.mult).then_inc(*read("rows", j, 2))
                dve.wait_ge(*copied("rows", j, 2))
                tt(qe, qe, v8(qkv[:, j, :]), ALU.mult).then_inc(*signal("qe", j))
                for half in range(2):
                    dve.wait_ge(*filled("kk", j, half))
                    w = w1[:, 4 * half:4 * half + 4, :].unsqueeze(2).broadcast_to([P, 4, 2, CH])
                    tt(blk[2][:, 4 * half:4 * half + 4, :].rearrange("p n (h c) -> p n h c", h=2),
                       bank("kk", j, half)[:, :].rearrange("p (n h c) -> p n h c", n=4, h=2), w, ALU.mult)\
                        .then_inc(*read("kk", j, half))
                dve.wait_ge(*filled("kq", j))
                tt(qkw, v8(bank("kq", j)[:, :]), w2, ALU.mult).then_inc(*read("kq", j))
                for half in range(2):
                    dve.wait_ge(*filled("tA", j, half))
                    src = v4(bank("tA", j, half)[:, :])
                    for i, (dst, name) in enumerate(((blk[5], "m16"), (blk[6], "m32"), (blk[7], "m64"))):
                        ins = tt(dst[:, 4 * half:4 * half + 4, :], src, mask4(name), ALU.mult)
                        ins.then_inc(*(read("tA", j, half) if i == 2 else signal("tA_part", j, half, i)))

                def add(name, op=ALU.add):
                    for half in range(2):
                        dve.wait_ge(*filled(name, j, half))
                        d = blk[4][:, 4 * half:4 * half + 4, :]
                        tt(d, d, v4(bank(name, j, half)[:, :]), op).then_inc(*read(name, j, half))

                def scaled(name, parts):
                    for half in range(2):
                        dve.wait_ge(*filled(name, j, half))
                        src = v4(bank(name, j, half)[:, :])
                        for i, (dst, c) in enumerate(parts):
                            ins = tt(dst[:, 4 * half:4 * half + 4, :], src,
                                     c[:, 4 * half:4 * half + 4].unsqueeze(2).broadcast_to([P, 4, P]), ALU.mult)
                            ins.then_inc(*(read(name, j, half) if i == len(parts) - 1 else signal(name + "_part", j, half)))

                window(j, 0)
                window(j, 1)
                dve.wait_ge(*done("p0", j))
                add("p1")
                dve.wait_ge(*done("cBexp", j))
                link(tt(cA, cA, brkj, ALU.mult))
                link(tt(cB, cB, rkj, ALU.mult))
                scaled("kt", ((blk[8], cA), (blk[0], cB)))
                scaled("vt", ((blk[1], betaj),))
                add("p2")
                add("p3")
                window(j, 2)
                add("i32", ALU.subtract)
                window(j, 3)
                add("i64", ALU.subtract)
                dve.wait_ge(*done("eglast", j))
                for n in range(NC - 1):
                    if n in (2, 5):
                        window(j, 4 + n // 3)
                    dve.wait_ge(*filled("su", j, n))
                    ps = bank("su", j, n)[:, 0:P]
                    if n == 0:
                        v.tensor_copy(state, ps).then_inc(*read("su", j, n))
                    else:
                        dve.wait_ge(*copied("su", j, n - 1))
                        stt(out=state, in0=state, scalar=eglast[:, n:n + 1], in1=ps, op0=ALU.mult, op1=ALU.add)\
                            .then_inc(*read("su", j, n))
            dve.wait_ge(*copied("osum"))
            v.reciprocal(hrs[1][0:40, :], hrs[1][0:40, :]).then_inc(*signal("orow"))
            for j in range(NJ):
                dve.wait_ge(*filled("ospread", j))
                stt(out=qkv[:, j, :], in0=qkv[:, j, :], scalar=col("gdn_norm"), in1=bank("ospread", j)[:, :],
                    op0=ALU.mult, op1=ALU.mult).then_inc(*read("ospread", j))
                dve.wait_ge(*copied("ospread", j))
                tt(qkv[:, j, :], qkv[:, j, :], gz[:, j, :], ALU.mult).then_inc(*signal("mixg", j))

            for k in (4, 5, 6, 7, 0, 1, 2, 3):
                lo_part("mix", (k,), hs[:, 1, k, real], qkv[:, k, :] if k < 4 else sq[:, k - 4, :], hs[:, 0, k, real])

            def residual(key, m, gate):
                dve.wait_ge(*filled(*key))
                stt(out=xT[:, m, :], in0=bank(*key)[:, :], scalar=modT[:, gate + m:gate + m + 1], in1=xT[:, m, :],
                    op0=ALU.mult, op1=ALU.add).then_inc(*read(*key))

            for m in range(KD):
                residual(("mo", m), m, 16)
                if m % 2:
                    split_lo()
            spread("2", diag)
            normed("2", "xn2")
            h_rest("2")
            for part, (c0, n) in enumerate(FFN_PARTS):
                for i in range(c0 // 2, (c0 + n) // 2):
                    split_lo()
                    if i in (1, 3):
                        ada_sum(10 + i // 2)
                    for k in (2 * i, 2 * i + 1):
                        dve.wait_ge(*copied("fg", k))
                        dve.wait_ge(*filled("fu", k))
                        tt(silug[k % 2], bank("fu", k)[:, :], silug[k % 2], ALU.mult).then_inc(*read("fu", k))
                    for k in (2 * i, 2 * i + 1):
                        lo_part("a", (k,), a_s[:, 1, k - c0, :], silug[k % 2], a_s[:, 0, k - c0, :])
                    split_lo()
                    if i == 5:
                        ada_mod(10)
                        ada_mod(11)
                        dve.wait_ge(*copied("ada", 11))
                for m in range(KD):
                    residual(("fd", part, m), m, 40)
                    split_lo()
            spread("3", diag)
            dve.wait_ge(*done("meta_hi"))
            tt(hs[:, 1, :, 0:META], hm, hs[:, 0, :, 0:META].bitcast(F32), ALU.subtract).then_inc(*signal("h3meta"))
            dve.wait_ge(*filled("spread3"))
            for k in range(KD):
                stt(out=hpre[:, k, :], in0=xT[:, k, :], scalar=col("pre", k), in1=bank("spread3")[:, :],
                    op0=ALU.mult, op1=ALU.mult).then_inc(*signal("xn3", k))
            dve.wait_ge(*done("xn3", KD - 1))
            v.engine_nop().then_inc(*read("spread3"))
            h_rest("3")
            dve.wait_ge(*done("h3", KD - 1))

            H2 = TM // 2
            v.memset(zc[0][:, 0:30], 0.0)
            v.memset(zc[1][:, 0:30], 0.0)
            v.memset(uu[0][:, 0:2], 0.0)
            link(v.memset(uu[1][:, 0:2], 0.0))
            lo, hi = slice(0, HD), slice(HD, P)

            def shifted(dst, src, by, first, rows=slice(0, P)):
                link(tt(dst[rows, first:TM], src[rows, first:TM], src[rows, first - by:TM - by], ALU.add))

            def pooled(m, rows, src):
                return stt(out=pw[m][rows, META:TM], in0=src[rows, META:TM],
                           scalar=cst("invw")[rows, m:m + 1], in1=pv[m][rows, META:TM], op0=ALU.mult, op1=ALU.subtract)

            tap_at = [0]

            def taps(n):
                for k in range(tap_at[0], min(tap_at[0] + n, CONF_K)):
                    for m in range(2):
                        if k == 0:
                            dve.wait_ge(*copied("cu", m, 1))
                        else:
                            dve.wait_ge(*done("cconv", k - 1, m))
                        tap = V2[:, V2_ROWS["conf"] + 2 * k + m:V2_ROWS["conf"] + 2 * k + m + 1]
                        src = zc[m][:, META + k:META + k + T]
                        ins = (ts(cacc[:, m, :], src, tap, col("conf_b", m), ALU.mult, ALU.add) if k == 0 else
                               stt(out=cacc[:, m, :], in0=src, scalar=tap, in1=cacc[:, m, :], op0=ALU.mult, op1=ALU.add))
                        ins.then_inc(*(signal("cmean_in", m) if k == CONF_K - 1 else signal("cconv", k, m)))
                tap_at[0] += n

            split_lo()
            for m in range(2):
                for half in range(2):
                    dve.wait_ge(*copied("cgate", m, half))
                    dve.wait_ge(*filled("cu", m, half))
                    tt(zc[m][:, 30 + half * H2:30 + (half + 1) * H2], bank("cu", m, half)[:, 0:H2],
                       ga_[m][:, half * H2:(half + 1) * H2], ALU.mult).then_inc(*read("cu", m, half))
            split_lo()
            taps(3)
            for m in range(2):
                dve.wait_ge(*copied("pv", m, 1))
                shifted(pw[m], pv[m], 1, 1)
                if m == 0:
                    shifted(pw[2], pw[0], 2, 3, hi)
                else:
                    shifted(pw[2], pw[1], 2, 3)
                    shifted(pw[1], pw[2], 4, 7)
                    shifted(pw[2], pw[1], 8, 15, hi)
                link(pooled(m, lo, pw[m]))
                pooled(m, hi, pw[2]).then_inc(*signal("pool", m))
                dve.wait_ge(*done("pool", m))
            split_lo()
            taps(4)
            split_lo()
            taps(4)
            split_lo()
            for m in range(2):
                dve.wait_ge(*filled("py", m))
                dve.wait_ge(*copied("pg", m))
                stt(out=ybr[:, m, :], in0=bank("py", m)[:, :], scalar=col("pool_scale", m), in1=pg[:, m, :],
                    op0=ALU.mult, op1=ALU.mult).then_inc(*read("py", m))
            taps(4)
            split_lo()
            taps(4)
            split_lo()
            for m in range(2):
                for half in range(2):
                    dve.wait_ge(*copied("cgx", m, half))
                    dve.wait_ge(*filled("xv", m, half))
                    tt(uu[m][:, 2 + half * H2:2 + (half + 1) * H2], bank("xv", m, half)[:, 0:H2],
                       cgx[m][:, half * H2:(half + 1) * H2], ALU.mult).then_inc(*read("xv", m, half))
            split_lo()
            taps(4)
            for m in range(2):
                dve.wait_ge(*copied("xv", m, 1))
                acc = cgx[m][:, 0:T]
                for k in range(SC_K):
                    tap = V2[:, V2_ROWS["sc"] + 2 * k + m:V2_ROWS["sc"] + 2 * k + m + 1]
                    src = uu[m][:, META + k:META + k + T]
                    link(ts(acc, src, tap, None, ALU.mult) if k == 0 else
                         stt(out=acc, in0=src, scalar=tap, in1=acc, op0=ALU.mult, op1=ALU.add))
                dve.wait_ge(*copied("bg", m))
                link(tt(acc, acc, bg[:, m, :], ALU.mult))
                dve.wait_ge(*copied("sg", m))
                tt(ybr[:, 8 + m, :], ybr[:, 8 + m, :], acc, ALU.mult).then_inc(*signal("yd", m))
            split_lo()
            taps(CONF_K)
            split_lo()
            split_lo()
            dve.wait_ge(*copied("cmean"))
            for m in range(2):
                tt(cacc[:, m, :], cacc[:, m, :], cmr[:, 0, :], ALU.subtract).then_inc(*signal("ccen", m))
            split_lo()
            dve.wait_ge(*copied("cvar"))
            link(v.reciprocal(cmr[:, 1, :], cmr[:, 1, :]))
            for m in range(2):
                dve.wait_ge(*done("cvar_in", m))
                tt(cacc[:, m, :], cacc[:, m, :], cmr[:, 1, :], ALU.mult).then_inc(*signal("cnorm", m))
            for m in range(2):
                dve.wait_ge(*done("csilu", m))
                tt(ybr[:, 6 + m, :], ybr[:, 6 + m, :], cacc[:, m, :], ALU.mult).then_inc(*signal("yc", m))
            split_lo()
            for k in range(2):
                dve.wait_ge(*done("cqsq", k))
                ts(cq[:, k, :], cq[:, k, :], col("q_norm", k), None, ALU.mult).then_inc(*signal("cqg", k))
            dve.wait_ge(*done("ckvsq"))
            for half in range(2):
                dve.wait_ge(*copied("kvsum", half))
            link(v.reciprocal(krb, krb))
            stt(out=ckv, in0=ckv, scalar=col("kv_norm"), in1=krb, op0=ALU.mult, op1=ALU.mult).then_inc(*signal("ckvn"))
            dve.wait_ge(*copied("cqsum"))
            v.reciprocal(rqm, rqm).then_inc(*signal("rqm"))
            for k in range(2):
                dve.wait_ge(*done("yc", k))
            v.memset(mpR[0], 0.0)
            v.memset(mpR[1], 0.0)
            v.memset(vv[:, 4, :], 0.0).then_inc(*signal("vpad"))
            r3 = slice(HD, QD)
            dve.wait_ge(*arrived("rope"))
            dve.wait_ge(*arrived("krs", 2))
            link(tt(kr[r3, :], kr[r3, :], rope[r3, 0, :], ALU.mult))
            link(tt(krs[r3, :], krs[r3, :], rope[r3, 1, :], ALU.mult))
            tt(kh[r3, :, :], kr[r3, :].unsqueeze(1).broadcast_to([QK_ROPE, 8, TM]),
               krs[r3, :].unsqueeze(1).broadcast_to([QK_ROPE, 8, TM]), ALU.add).then_inc(*signal("krope"))
            for g in range(4):
                q2 = qh[r3, 2 * g:2 * g + 2, :]
                dve.wait_ge(*arrived("qsw", 2 * (g + 1)))
                cs2 = [rope[r3, s, META:TM].unsqueeze(1).broadcast_to([QK_ROPE, 2, T]) for s in range(2)]
                link(tt(q2, q2, cs2[0], ALU.mult))
                link(tt(qsw[r3, :, :], qsw[r3, :, :], cs2[1], ALU.mult))
                tt(q2, q2, qsw[r3, :, :], ALU.add).then_inc(*signal("qrope", g))
                dve.wait_ge(*done("qrope", g))

            def ml_max(u):
                i, h = MLU[u]
                n = keys_of[i]
                dve.wait_ge(*copied("ms2" if n > 512 else "ms", u))
                s, c = msc[u % 2], u % 16
                link(tt(s[:, n - WIN:n], s[:, n - WIN:n], cst("causal"), ALU.add))
                link(v.reduce_max(smax[:, c:c + 1], s[:, 0:n], AX.X))
                ts(snmax[:, c:c + 1], smax[:, c:c + 1], -1.0, None, ALU.mult).then_inc(*signal("mmax", u))

            def ml_rec(u):
                i, h = MLU[u]
                c = u % 16
                dve.wait_ge(*done("mexp", u))
                v.reciprocal(sden[:, c:c + 1], ssumx[:, c:c + 1]).then_inc(*signal("mrec", u))

            for u in range(len(MLU) + 3):
                if u >= 3 and MLU[u - 3][1] == 7:
                    i = MLU[u - 3][0]
                    dve.wait_ge(*filled("mo2", i))
                    for pair in range(4):
                        dve.wait_ge(*copied("mg", pair))
                    y = ybr[:, 2:6, i * WIN:(i + 1) * WIN]
                    tt(y, bank("mo2", i)[:, :].rearrange("p (h t) -> p h t", h=4), y, ALU.mult)\
                        .then_inc(*read("mo2", i))
                if u < len(MLU):
                    ml_max(u)
                if 1 <= u <= len(MLU):
                    ml_rec(u - 1)
                if u > 4 and u % 4 == 1:
                    m, b = MIX_EARLY[u // 4 - 1]
                    if b != 1:
                        g_, _ = early_gate(u // 4 - 1)
                        dve.wait_ge(*copied("gl", m, b))
                        dve.wait_ge(*filled("y", m, b))
                        tt(macc_of(m) if b == 0 else g_, bank("y", m, b)[:, :], g_, ALU.mult).then_inc(*read("y", m, b))
                        if b:
                            dve.wait_ge(*copied("y", m, b))
                            tt(macc_of(m), macc_of(m), g_, ALU.add).then_inc(*signal("gadd", m, b))
                    if u in (9, 17, 25):
                        split_lo()
            split_lo()
            for m in range(2):
                dve.wait_ge(*filled("y", m, 1))
                tt(prod[m], bank("y", m, 1)[:, :], sg_mla[m], ALU.mult).then_inc(*read("y", m, 1))
                dve.wait_ge(*copied("y", m, 1))
                dve.wait_ge(*done("gadd", m, 3))
                tt(macc_of(m), macc_of(m), prod[m], ALU.add).then_inc(*signal("macc", m))
            for m in range(2):
                lo_part("m", (m,), ms_[:, 1, m, :], macc_of(m), ms_[:, 0, m, :])
            for m in range(2, KD):
                for b in range(4):
                    x = 4 * m + b
                    dve.wait_ge(*copied("gl", m, b))
                    dve.wait_ge(*filled("y", m, b))
                    dst = macc[m % 2] if b == 0 else prod[b % 2]
                    if b == 0 and m >= 4:
                        dve.wait_ge(*done("m", m - 2))
                    tt(dst, bank("y", m, b)[:, :], sg[x % 2], ALU.mult).then_inc(*read("y", m, b))
                    dve.wait_ge(*copied("y", m, b))
                    if b:
                        ins = tt(macc[m % 2], macc[m % 2], prod[b % 2], ALU.add)
                        if b < 3:
                            link(ins)
                        else:
                            ins.then_inc(*signal("macc", m))
                    elif m > 2:
                        lo_part("m", (m - 1,), ms_[:, 1, m - 1, :], macc[(m - 1) % 2], ms_[:, 0, m - 1, :])
                    if b % 2:
                        split_lo()
            lo_part("m", (KD - 1,), ms_[:, 1, KD - 1, :], macc[(KD - 1) % 2], ms_[:, 0, KD - 1, :])
            split_lo()
            split_lo()
            dve.wait_ge(*arrived("post"))
            for b in range(4):
                for half in range(2):
                    dve.wait_ge(*copied("xt", b, half))
                dve.wait_ge(*done("fss", b, 1))
                tt(fss[:, 2 * b:2 * b + 1], fss[:, 2 * b:2 * b + 1], fss[:, 2 * b + 1:2 * b + 2], ALU.add)\
                    .then_inc(*signal("ftot", b))
                dve.wait_ge(*done("froot", b))
                link(v.reciprocal(frs[:, 4 + b:5 + b], frs[:, b:b + 1]))
                for half in range(2):
                    c = slice(512 * half, 512 * half + 512)
                    f = fin[b][:, c]
                    stt(out=f, in0=bank("fo", b, half)[:, :], scalar=frs[:, 4 + b:5 + b], in1=post[:, c],
                        op0=ALU.mult, op1=ALU.mult).then_inc(*read("fo", b, half))
                    dve.wait_ge(*copied("fo", b, half))
                    tt(f, f, xtok[:, b, c], ALU.add).then_inc(*(signal("fin", b) if half else signal("fin_half", b)))

    counted["tiles"] = tiles
    return counted


_INS = ["x", "c", "w_ada", "b_ada", "norm1_w", "w_in", "conv_w", "a_log", "dt_bias", "gdn_norm_w", "q_norm_w",
        "k_norm_w", "sinks", "w_out", "norm2_w", "w_gate", "w_up", "w_down", "meta_tokens_2", "pre_norm_g_2",
        "w_in_2", "gate_bias_2", "pool_w_2", "pool_scale_2", "w_out_pool_2", "q_norm_g_2", "w_uq_2", "kv_norm_g_2",
        "w_ukv_2", "w_out_mla_2", "conf_dw_w_2", "conf_dw_b_2", "conf_ln_g_2", "conf_ln_b_2", "w_out_conf_2",
        "sc_dw_w_2", "w_out_sc_2", "w_o_2", "post_norm_g_2"]


def kernel(**inputs):
    import concourse.bacc as _bacc
    from concourse.bass_utils import run_bass_kernel_spmd as _run

    consts, alibi, rope = shape_constants()
    arrays = {f"in_{name}_dram": np.ascontiguousarray(inputs[name]) for name in _INS}
    arrays |= {"in_consts_dram": consts, "in_alibi_dram": alibi, "in_rope_dram": rope}

    def build(known):
        nc = _bacc.Bacc("TRN2", target_bir_lowering=False, num_devices=1)
        aps = {n[3:-5]: nc.dram_tensor(n, v.shape, mybir.dt.from_np(v.dtype), kind="ExternalInput").ap()
               for n, v in arrays.items()}
        o = nc.dram_tensor("out_0_dram", (1, T, D), F32, kind="ExternalOutput").ap()
        return nc, program(nc, aps, o, known)

    nc, _ = build(build(None)[1])
    return _run(nc, [arrays], core_ids=[0]).results[0]["out_0_dram"]
```

```python
from contextlib import ExitStack

import numpy as np

import concourse.bass as bass
from concourse import mybir

F32 = mybir.dt.float32
F32R = mybir.dt.float32r
ALU = mybir.AluOpType
ACT = mybir.ActivationFunctionType
AX = mybir.AxisListType

P = 128
D = 1024
KD = D // P
T = 512
META = 16
TM = T + META
HD = 64
GH = 8
NJ = GH // 2
CH = 64
NC = T // CH
WIN = 128
NB = T // WIN
FF = 2816
KF = FF // P
FFN_PARTS = ((0, 12), (12, 10))
EPS = 1e-6
QK_NOPE, QK_ROPE, V_DIM = 64, 32, 64
QD = QK_NOPE + QK_ROPE
CONF_K = 31
SC_K = 3
NEG = -1e30

CONST_W = {}
_at = 0
for _name, _w in (("ident", 128), ("ones", 128), ("onesbd", 128), ("m16", 128), ("m16T", 128), ("m32", 128),
                  ("m64", 128), ("strictT", 64), ("inclT", 64), ("stack", 64), ("sel", 512), ("pick", 4 * 40 * 2),
                  ("two", 2), ("reset", 512), ("invw", 2), ("causal", 128)):
    CONST_W[_name] = (_at, _w)
    _at += _w
CONST_COLS = _at
CONST_FIRST = 3 * P

V1_ROWS = {"b_ada": 0, "norm1": 48, "norm2": 56, "pre": 64, "gate_bias": 72, "conf_b": 104, "ln_g": 106,
           "ln_b": 108, "pool_scale": 110, "q_norm": 112, "kv_norm": 114, "gdn_norm": 115, "qn": 116, "kn": 117}
V1_N = 118
V2_ROWS = {"conv": 0, "conf": 48, "sc": 110}
V2_N = 116


def shape_constants():
    c = np.zeros((P, CONST_COLS), np.float32)

    def put(name, a):
        o, w = CONST_W[name]
        c[:a.shape[0], o:o + w] = a.reshape(a.shape[0], -1)

    r = np.arange(P)
    head, tok = r // 64, r % 64
    same = head[:, None] == head[None, :]
    lower = tok[:, None] > tok[None, :]
    b16 = tok[:, None] // 16 == tok[None, :] // 16
    b32 = tok[:, None] // 32 == tok[None, :] // 32
    put("ident", np.eye(P))
    put("ones", np.ones((P, P)))
    put("onesbd", same)
    put("m16", same & lower & b16)
    put("m16T", (same & lower & b16).T)
    put("m32", same & lower & b32 & ~b16)
    put("m64", same & lower & ~b32)
    t = np.arange(64)
    put("strictT", t[None, :] > tok[:, None])
    put("inclT", t[None, :] >= tok[:, None])
    put("stack", t[None, :] == tok[:, None])
    sel = np.zeros((40, NJ, P))
    pick = np.zeros((P, 2, NJ, 40))
    for j in range(NJ):
        for h in (0, 1):
            sel[2 * j + h, j, 64 * h:64 * h + 64] = 1
            sel[32 + 2 * j + h, j, 64 * h:64 * h + 64] = 1
            pick[64 * h:64 * h + 64, 0, j, 2 * j + h] = 1
            pick[64 * h:64 * h + 64, 1, j, 32 + 2 * j + h] = 1
    put("sel", sel)
    put("pick", pick)
    two = np.zeros((P, 2))
    two[:64, 0] = 1
    two[64:, 1] = 1
    put("two", two)
    reset = np.ones((P, T))
    reset[:, ::CH] = 0
    put("reset", reset)
    w = np.zeros((P, 2))
    w[:64, 0], w[64:, 0], w[:64, 1], w[64:, 1] = 1 / 2, 1 / 4, 1 / 8, 1 / 16
    put("invw", w)
    put("causal", np.where(r[None, :] <= r[:, None], 0.0, NEG))

    slopes = 2.0 ** (-8.0 * (np.arange(8, dtype=np.float32) + 1.0) / 8)
    dist = (r[:, None] + WIN - np.arange(2 * WIN)[None, :]).astype(np.float32)
    inside = (dist >= 0) & (dist < WIN)
    alibi = np.where(inside[:, None, :], -slopes[None, :, None] * dist[:, None, :], NEG)
    inv = (1.0 / (np.float32(10000.0) ** (np.arange(0, QK_ROPE, 2, dtype=np.float32) / QK_ROPE))).astype(np.float32)
    ang = inv[:, None] * np.arange(TM, dtype=np.float32)[None, :]
    rope = np.zeros((QK_ROPE, 2, TM), np.float32)
    rope[:16, 0] = rope[16:, 0] = np.cos(ang)
    rope[:16, 1], rope[16:, 1] = -np.sin(ang), np.sin(ang)
    return c, alibi.astype(np.float32).reshape(P, 8 * 2 * WIN), rope.reshape(QK_ROPE, 2 * TM)


def program(nc, a, out, known):
    ctx = ExitStack()
    counted, reached = {}, {}
    with ctx:
        sems = {}

        def sem(name):
            if name not in sems:
                sems[name] = ctx.enter_context(nc.semaphore(name))
            return sems[name]

        def signal(stage, *index):
            reached[stage] = reached.get(stage, 0) + 1
            counted[(stage,) + index] = reached[stage]
            return sem(stage), 1

        def done(stage, *index):
            return sem(stage), (known[(stage,) + index] if known else 1)

        def sb(name, width, rows=P):
            return ctx.enter_context(nc.sbuf_tensor(name, [rows, width], F32))

        banks = [ctx.enter_context(nc.psum_tensor(f"bank{i}", [P, 512], F32)) for i in range(8)]

        xT = sb("xT", KD * T)[:, :].rearrange("p (k t) -> p k t", k=KD)
        NS = 3
        PANEL = 2048
        ring = [sb(f"ring{i}", PANEL) for i in range(NS)]
        consts = sb("consts", CONST_COLS)
        V1 = sb("V1", V1_N)
        V2 = sb("V2", V2_N)
        post = sb("post", D)
        poolw = sb("poolw", 2 * P)
        small = sb("small", 672)
        acc_buf = sb("acc", TM)
        tball = sb("tb", 2 * TM)
        tb = [tball[:, i * TM:(i + 1) * TM] for i in range(2)]
        with ExitStack() as over:
            wscratch = over.enter_context(nc.sbuf_tensor("wscratch", [P, 4 * PANEL], F32))
        whi = [ctx.enter_context(nc.sbuf_tensor(f"whi{i}", [P, PANEL], F32R)) for i in range(2)]
        wlo = [ctx.enter_context(nc.sbuf_tensor(f"wlo{i}", [P, PANEL], F32R)) for i in range(2)]
        with ExitStack() as over:
            hscratch = over.enter_context(nc.sbuf_tensor("hscratch", [P, 2 * KD * TM], F32))
        hsplit = ctx.enter_context(nc.sbuf_tensor("hsplit", [P, 2 * KD * TM], F32R))
        h_split = hsplit[:, :].rearrange("p (s k t) -> p s k t", s=2, k=KD)
        ARENA = 19960
        with ExitStack() as over:
            arena = over.enter_context(nc.sbuf_tensor("arena", [P, ARENA], F32))
        KA = FFN_PARTS[0][1]
        with ExitStack() as over:
            a_buf = over.enter_context(nc.sbuf_tensor("a_split", [P, 2 * KA * T], F32R))
        act_split = a_buf[:, :].rearrange("p (s k t) -> p s k t", s=2, k=KA)
        ctx.enter_context(nc.sbuf_tensor("ybr_place", [P, 10 * T], F32))
        m_buf = ctx.enter_context(nc.sbuf_tensor("m_split", [P, 2 * KD * T], F32R))
        mix_split = m_buf[:, :].rearrange("p (s k t) -> p s k t", s=2, k=KD)
        real = slice(META, TM)

        def cst(name, rows=P):
            o, w = CONST_W[name]
            return consts[0:rows, o:o + w]

        ident, ones, onesbd = cst("ident"), cst("ones"), cst("onesbd")

        class Cut:
            def __init__(self, buf, at=0, end=None):
                self.buf, self.at = buf, at
                self.end = end or buf.shape[1]

            def take(self, width, rows=P, lo=0):
                r = self.buf[lo:lo + rows, self.at:self.at + width]
                self.at += width
                assert self.at <= self.end, (self.at, self.end)
                return r

        small_cut = Cut(small)
        modT, modA1, modA2, cs = small_cut.take(48), small_cut.take(8), small_cut.take(8), small_cut.take(8)
        sinks, nega, dtb = small_cut.take(8), small_cut.take(1), small_cut.take(1)
        ssum, sroot, srstd = small_cut.take(4), small_cut.take(4), small_cut.take(4)
        hmeta = small_cut.take(8 * META)
        cA, cB = small_cut.take(NC), small_cut.take(NC)
        eglast = [small_cut.take(NC) for _ in range(2)]
        rq = small_cut.take(NB * GH)
        smax, snmax, ssumx, sden, sesk = (small_cut.take(16) for _ in range(5))
        rqm = small_cut.take(NB)
        wqk, fss, frs = small_cut.take(1), small_cut.take(8), small_cut.take(8)
        msum = small_cut.take(2)
        epsc, eps64, eps96 = small_cut.take(1), small_cut.take(1), small_cut.take(1)
        cols = small_cut.take(128)
        warm = small_cut.take(1)

        A1 = Cut(arena)
        qkv = A1.take(12 * T).rearrange("p (m t) -> p m t", m=12)
        gz = A1.take(NJ * T).rearrange("p (m t) -> p m t", m=NJ)
        sq = A1.take(4 * T).rearrange("p (m t) -> p m t", m=4)
        gates = A1.take(2 * T)
        glog, grow = gates[:, 0:T], gates[:, T:2 * T]
        hsq = [tb[i][:, 0:T] for i in range(2)]
        sacc = acc_buf[:, 0:T]
        row_buf = [A1.take(T) for _ in range(2)]
        base1 = A1.at
        B1 = Cut(arena, base1)
        raw = [B1.take(T + 3) for _ in range(3)]
        gate_tmp = [B1.take(T) for _ in range(4)]
        sk, sv = sacc, B1.take(T)
        B2 = Cut(wscratch)
        vs = B2.take(T).rearrange("p (b d) -> p b d", b=NB)
        kpad = B2.take(4 * T).rearrange("p (g h t) -> p g h t", g=2, h=2)
        alibi = B2.take(8 * 2 * WIN)
        sc = [B2.take(2 * 2 * WIN) for _ in range(2)]
        pr = [B2.take(2 * 2 * WIN) for _ in range(2)]
        prT = [B2.take(4 * WIN) for _ in range(2)]
        C1 = Cut(arena, 0)
        x_in = C1.take(4 * D).rearrange("p (b f) -> p b f", b=4)
        rows1, rows2 = C1.take(P), C1.take(P)
        meta_in = C1.take(D)
        C1b = Cut(arena, base1)
        hpre = C1b.take(KD * T).rearrange("p (k t) -> p k t", k=KD)
        rbc = C1b.take(META)
        diag = C1b.take(4 * P).rearrange("p (b t) -> p b t", b=4)
        adaacc = [post[:, 0:512], post[:, 512:1024]]
        G1, G2 = Cut(arena, base1), Cut(hscratch)
        block_diag = [cut_.take(NC * P).rearrange("p (n c) -> p n c", n=NC) for cut_ in 7 * [G1] + 3 * [G2]]
        state = G1.take(P)
        vnew = [G1.take(P) for _ in range(2)]
        qkw = G2.take(NC * CH).rearrange("p (n c) -> p n c", n=NC)
        g_row, e_, w1, w2, qe0, qe1, gx = (G2.take(T).rearrange("p (n c) -> p n c", n=NC) for _ in range(7))
        qe = [qe0, qe1]
        silug = [tb[i][:, 0:T] for i in range(2)]

        E2 = Cut(arena)
        ybr = E2.take(10 * T).rearrange("p (k t) -> p k t", k=10)
        base2 = E2.at
        M2 = Cut(arena, base2)
        q_mla = M2.take(8 * T).rearrange("p (h t) -> p h t", h=8)
        k_mla = M2.take(8 * TM).rearrange("p (h t) -> p h t", h=8)
        v_mla = M2.take(5 * T).rearrange("p (b d) -> p b d", b=5)
        rest2 = M2.at
        msc = [M2.take(TM) for _ in range(2)]
        mpr = [M2.take(TM) for _ in range(2)]
        mpT = [M2.take(4 * WIN) for _ in range(2)]
        mpR = [arena[:, ARENA - (i + 1) * WIN:ARENA - i * WIN] for i in range(2)]
        M2.at = rest2
        cq = M2.take(2 * T).rearrange("p (k t) -> p k t", k=2)
        ckv, kr = M2.take(TM), M2.take(TM)
        krs = M2.take(TM)
        ksq = krb = acc_buf[:, :]
        rope = M2.take(2 * TM).rearrange("p (s t) -> p s t", s=2)
        qsw2 = [buf_[:, 0:2 * T].rearrange("p (h t) -> p h t", h=2) for buf_ in (tball, post)]
        qsw = qsw2[0]
        N2 = Cut(arena, base2)
        conf_in = [N2.take(30 + TM) for _ in range(2)]
        conf_gate = [N2.take(TM) for _ in range(2)]
        conf_sum = N2.take(2 * T).rearrange("p (k t) -> p k t", k=2)
        conf_sq = N2.take(2 * T).rearrange("p (k t) -> p k t", k=2)
        conf_stats_ = N2.take(2 * T).rearrange("p (k t) -> p k t", k=2)
        bg = N2.take(2 * T).rearrange("p (k t) -> p k t", k=2)
        cgx = [N2.take(TM) for _ in range(2)]
        short_in = [N2.take(2 + TM) for _ in range(2)]
        pv = [N2.take(TM) for _ in range(2)]
        pool_sum = [N2.take(TM) for _ in range(3)]
        pg = N2.take(2 * T).rearrange("p (k t) -> p k t", k=2)
        sg = [tb[i][:, 0:T] for i in range(2)]
        mla_gate_buf = [sacc, cst("reset")]
        mix_sum_early = [post[:, 0:T], cst("sel")]
        O2 = Cut(arena, base2 + 2 * KD * T)
        prod = [O2.take(T) for _ in range(2)]
        mix_sum = [O2.take(T) for _ in range(2)]
        xtok = O2.take(4 * D).rearrange("p (b f) -> p b f", b=4)
        O3 = Cut(arena, 0, base2)
        fin = [O3.take(D) for _ in range(4)]
        fjunk = O3.take(512)

        panels, index_of, splits = [], {}, []

        def w_cols(w, c0, n, k0=0, kn=None):
            kn = kn or w.shape[0] // P - k0
            return w[k0 * P:(k0 + kn) * P, c0:c0 + n].rearrange("(k p) n -> p k n", p=P)

        def panel(name, kn, width, parts, split=True):
            if split:
                splits.append(name)
            index_of[name] = len(panels)
            panels.append((name, kn, width, parts))

        w_in, w_ada, w_out = a["w_in"][0], a["w_ada"][0], a["w_out"][0]
        w_gate, w_up, w_down = a["w_gate"][0], a["w_up"][0], a["w_down"][0]
        w_in2 = a["w_in_2"][0]

        def ada_panel(i):
            for h in range(2):
                panel(f"ada{i}{h}", 4, 512, [(0, 512, w_cols(w_ada, 512 * i, 512, 4 * h, 4))], split=False)

        def cols_panel(name, w, c0, n=256):
            panel(name, KD, n, [(0, n, w_cols(w, c0, n))])

        for i in range(4):
            ada_panel(i)
        for i in range(6):
            cols_panel(f"qkv{i}", w_in, 256 * i)
            if i in (2, 3, 4, 5):
                ada_panel(2 + i)
        panel("abk", KD, 168, [(0, 32, w_cols(w_in, 2048, 32)), (32, 8, w_cols(w_in, 2056, 8)),
                               (40, 128, w_cols(w_in, 2576, 128))])
        cols_panel("sv", w_in, 2704, 128)
        ada_panel(8)
        for i in range(2):
            cols_panel(f"sq{i}", w_in, 2064 + 256 * i)
        ada_panel(9)
        for i in range(2):
            cols_panel(f"gz{i}", w_in, 1536 + 256 * i)
        for i in range(4):
            cols_panel(f"out{i}", w_out, 256 * i)
        for part, (c0, n) in enumerate(FFN_PARTS):
            for i in range(c0 // 2, (c0 + n) // 2):
                cols_panel(f"g{i}", w_gate, 256 * i)
                cols_panel(f"u{i}", w_up, 256 * i)
                if i in (1, 3):
                    ada_panel(10 + i // 2)
            for m in range(KD):
                panel(f"down{part}{m}", n, P, [(0, P, w_cols(w_down, P * m, P, c0, n))])
        seg = {"cug": 1696, "cu": 1440, "pv": 0, "pg": 256, "cg": 1952, "bg": 2208, "cgx": 2464, "xv": 2720,
               "sg": 2976, "cq": 512, "mg0": 928}
        for name, c0 in seg.items():
            cols_panel(name, w_in2, c0)
        cols_panel("ckr", w_in2, 768, 192)
        cols_panel("mg1", w_in2, 928 + 256)
        GL0 = 3232
        branch_w = [("w_out_pool_2", 2), ("w_out_mla_2", 4), ("w_out_conf_2", 2), ("w_out_sc_2", 2)]
        for m in range(KD):
            for h in range(2):
                panel(f"gl{m}{h}", KD, 256, [(128 * b, 128, w_cols(w_in2, GL0 + 1024 * (2 * h + b) + 128 * m, 128))
                                             for b in range(2)])
                if m == 2 and h == 0:
                    for m1 in range(2):
                        panel(f"yb{m1}", 4, P, None, split=False)
            if m == 0:
                panel("uq", 2, 768, [(0, 768, w_cols(a["w_uq_2"][0], 0, 768))], split=False)
                panel("ukv", 1, 1024, [(0, 1024, w_cols(a["w_ukv_2"][0], 0, 1024))], split=False)
            if m < 2:
                panel(f"ya{m}", 6, P, None, split=False)
            else:
                panel(f"yw{m}", 10, P, None, split=False)
        for half in range(2):
            for kpart in range(2):
                panel(f"wo{half}{kpart}", 4, 512, [(0, 512, w_cols(a["w_o_2"][0], 512 * half, 512, 4 * kpart, 4))])

        branches_of = {"ya": (0, 2, 3), "yb": (1,), "yw": (0, 1, 2, 3)}

        def y_place(m, b):
            kind = "yw" if m >= 2 else "yb" if b == 1 else "ya"
            return (f"{kind}{m}", sum(branch_w[i][1] for i in branches_of[kind] if i < b),
                    sum(branch_w[i][1] for i in range(b)), branch_w[b][1])

        loads_of_slot = [0] * NS
        loaded_at = {}
        for i, (name, kn, width, parts) in enumerate(panels):
            n_dma = len(branches_of[name[:2]]) if parts is None else len(parts)
            loads_of_slot[i % NS] += 16 * n_dma
            loaded_at[name] = loads_of_slot[i % NS]

        def W(name):
            i = index_of[name]
            _, kn, width, _ = panels[i]
            return ring[i % NS][:, 0:kn * width].rearrange("p (k n) -> p k n", k=kn)

        def split_of(name):
            _, kn, width, _ = panels[index_of[name]]
            i = splits.index(name) % 2
            return [w[i][:, 0:kn * width].rearrange("p (k n) -> p k n", k=kn) for w in (whi, wlo)]

        def loaded(name):
            return sem(f"loaded{index_of[name] % NS}"), loaded_at[name]

        place, uses, held, turn = {}, [0] * 8, set(), [0]

        def open_tile(pe, *key, hold=False):
            while turn[0] % 8 in held:
                turn[0] += 1
            b = turn[0] % 8
            turn[0] += 1
            place[key] = b, uses[b] + 1
            uses[b] += 1
            if hold:
                held.add(b)
            if uses[b] > 1:
                pe.wait_ge(sem(f"bank{b}_read"), uses[b] - 1)
            return banks[b]

        def let_go(*key):
            held.discard(place[key][0])

        def fill(*key):
            return sem(f"bank{place[key][0]}_filled"), 1

        def filled(*key):
            return sem(f"bank{place[key][0]}_filled"), place[key][1]

        def read(*key):
            return sem(f"bank{place[key][0]}_read"), 1

        def copied(*key):
            return sem(f"bank{place[key][0]}_read"), place[key][1]

        def bank(*key):
            return banks[place[key][0]]

        def arrived(name, n=1):
            return sem("ld_" + name), 16 * n

        MIX_EARLY = [(m, b) for m in range(2) for b in range(4)]

        def mix_sum_of(m):
            return mix_sum_early[m] if m < 2 else mix_sum[m % 2]

        def early_gate(i):
            m, b = MIX_EARLY[i]
            if b == 1:
                return mla_gate_buf[m], None
            passing = [x for x in MIX_EARLY if x[1] != 1]
            at = passing.index((m, b))
            return sg[at % 2], passing[at - 2] if at >= 2 else None

        MIX_ORDER = (4, 5, 6, 7, 0, 1, 2, 3)
        SWU = [(b, hp) for b in range(NB) for hp in range(4)]
        MLU = [(i, h) for i in range(NB) for h in range(8)]
        keys_of = [META + WIN * (i + 1) for i in range(NB)]

        block = ctx.enter_context(nc.Block())
        last_tile_of = {}

        def used(name):
            if name.startswith("wo") and name[-1] == "0":
                return done("fo_part", int(name[2]), 3)
            return filled(*last_tile_of[name])

        def splitter(eng, whole, rest):
            at = [0]

            def step(half=None):
                i = at[0]
                at[0] += half != 0
                if i >= len(splits):
                    return
                name = splits[i]
                _, kn, width, _ = panels[index_of[name]]
                n = kn * width
                c = slice(n // 2 if half == 1 else 0, n // 2 if half == 0 else n)
                whole_panel, hi, lo = (t[:, c] for t in (ring[index_of[name] % NS], whi[i % 2], wlo[i % 2]))
                if whole:
                    if i >= 2 and half != 1:
                        eng.wait_ge(*used(splits[i - 2]))
                    eng.wait_ge(*loaded(name))
                    ins = whole(hi, whole_panel)
                    if half != 0:
                        ins.then_inc(*signal("w_hi", name))
                else:
                    eng.wait_ge(*done("w_hi", name))
                    ins = rest(lo, whole_panel, hi.bitcast(F32))
                    if half != 0:
                        ins.then_inc(*signal("w_lo", name))
            return step

        @block.tensor
        def _(pe):
            mm, tr = nc.tensor.matmul, nc.tensor.transpose

            def project(key, name, c0, m, rhs, n, release=False):
                o = open_tile(pe, *key)
                pe.wait_ge(*done("w_lo", name))
                hi, lo = split_of(name)
                kn = hi.shape[1]
                for k in range(kn):
                    for i, (w, s) in enumerate(((hi, 0), (hi, 1), (lo, 0))):
                        last = mm(o[0:m, 0:n], w[:, k, c0:c0 + m], rhs(s, k), start=k + i == 0,
                                  stop=k == kn - 1 and i == 2)
                last.then_inc(*fill(*key))
                if release:
                    last_tile_of[name] = key

            def norm_stats(tag):
                o = open_tile(pe, "sum" + tag)
                pe.wait_ge(*done("sqsum" + tag, KD - 2))
                for b in range(4):
                    mm(o[:, b:b + 1], sacc[:, b * P:(b + 1) * P], ones[:, 0:1], start=True, stop=False)
                    if b == 0:
                        pe.wait_ge(*done("xsq" + tag, KD - 1))
                    last = mm(o[:, b:b + 1], hsq[1][:, b * P:(b + 1) * P], ones[:, 0:1], start=False, stop=True)
                last.then_inc(*fill("sum" + tag))

            def norm_spread(tag, dg):
                o = open_tile(pe, "spread" + tag)
                pe.wait_ge(*done("diag" + tag))
                for b in range(4):
                    last = mm(o[:, b * P:(b + 1) * P], ones, dg[:, b, :], start=True, stop=True)
                last.then_inc(*fill("spread" + tag))

            def ada_rows(i):
                o = open_tile(pe, "adar", i)
                pe.wait_ge(*done("cs"))
                for h in range(2):
                    pe.wait_ge(*loaded(f"ada{i}{h}"))
                    for k in range(4):
                        last = mm(o[0:1, :], cs[:, 4 * h + k:4 * h + k + 1], W(f"ada{i}{h}")[:, k, :],
                                  start=h + k == 0, stop=h == 1 and k == 3)
                    last.then_inc(*(fill("adar", i) if h else signal("adarow_half", i)))

            def ada_turn(i):
                o = open_tile(pe, "ada", i)
                pe.wait_ge(*copied("adar", i))
                for c in range(4):
                    last = mm(o[:, c:c + 1], row_buf[i % 2][0:1, c * P:(c + 1) * P], ones[0:1, 0:1], start=True, stop=True)
                last.then_inc(*fill("ada", i))

            def ada(i):
                o = open_tile(pe, "ada", i)
                pe.wait_ge(*done("adaacc", i))
                for c in range(4):
                    last = mm(o[:, c:c + 1], adaacc[i % 2][:, c * P:(c + 1) * P], ones[:, 0:1], start=True, stop=True)
                last.then_inc(*fill("ada", i))

            pe.wait_ge(*arrived("const"))
            pe.wait_ge(*arrived("x", 2))
            for k in range(KD):
                o = open_tile(pe, "x", k)
                for b in range(4):
                    last = tr(o[:, b * P:(b + 1) * P], x_in[:, b, k * P:(k + 1) * P], ident)
                last.then_inc(*fill("x", k))
            o = open_tile(pe, "meta")
            for k in range(KD):
                last = tr(o[:, k * META:(k + 1) * META], meta_in[0:META, k * P:(k + 1) * P], ident[0:META, 0:META])
            last.then_inc(*fill("meta"))
            ada(0)
            pe.wait_ge(*arrived("rows", 20))
            o = open_tile(pe, "vec")
            tr(o[:, 0:V1_N], rows1[0:V1_N, :], ident[0:V1_N, 0:V1_N])
            tr(o[:, P:P + V2_N], rows2[0:V2_N, :], ident[0:V2_N, 0:V2_N]).then_inc(*fill("vec"))
            ada(1)
            norm_spread("1", diag)
            o = open_tile(pe, "spreadmeta")
            pe.wait_ge(*done("diagmeta"))
            mm(o[:, 0:META], ones[0:META, :], rbc[0:META, 0:META], start=True, stop=True).then_inc(*fill("spreadmeta"))
            ada_rows(3)
            ada(2)
            ada_turn(3)

            hx = lambda s, k: h_split[:, s, k, real]

            def first_tiles(name, chunk_ready, parts, order=range(KD)):
                outs = [open_tile(pe, *part[0]) for part in parts]
                pe.wait_ge(*done("w_lo", name))
                hi, lo = split_of(name)
                for at, k in enumerate(order):
                    pe.wait_ge(*chunk_ready(k))
                    for o, (key, c0, n, rhs) in zip(outs, parts):
                        for i, (w, s) in enumerate(((hi, 0), (hi, 1), (lo, 0))):
                            last = mm(o[:, 0:n], w[:, k, c0:c0 + P], rhs(s, k), start=at + i == 0,
                                      stop=at == len(order) - 1 and i == 2)
                        if at == len(order) - 1:
                            last.then_inc(*fill(*key))
                last_tile_of[name] = parts[-1][0]

            def h_ready(tag):
                return lambda k: done("h" + tag, k)

            pick = cst("pick").rearrange("p (w j c) -> p w j c", w=2, j=NJ)
            length_tile = [None]

            def head_lengths(m):
                if m == 0:
                    length_tile[0] = open_tile(pe, "hsum", hold=True)
                    pe.wait_ge(*arrived("const_rest"))
                pe.wait_ge(*done("hsq", m))
                last = mm(length_tile[0][0:40, :], pick[:, m // 4, m % 4, :], hsq[m % 2], start=m == 0, stop=m == 7)
                last.then_inc(*(fill("hsum") if m == 7 else signal("hsum_step", m)))
                if m == 7:
                    let_go("hsum")

            for m in range(12):
                if m == 0:
                    first_tiles("qkv0", h_ready("1"), [(("pj", c), P * c, T, hx) for c in range(2)])
                elif m > 1:
                    project(("pj", m), f"qkv{m // 2}", P * (m % 2), P, hx, T, release=m % 2 == 1)
                if m >= 4:
                    head_lengths(m - 4)
                if m >= 5 and m % 2 == 1:
                    ada((m - 5) // 2 + 4)
            project(("ab",), "abk", 0, P, hx, T)
            project(("sk",), "abk", 40, P, hx, T, release=True)
            project(("sv",), "sv", 0, P, hx, T, release=True)
            o = open_tile(pe, "sksum")
            pe.wait_ge(*done("hsq", 8))
            mm(o[:, :], onesbd, hsq[0], start=True, stop=True).then_inc(*fill("sksum"))
            query_tile = open_tile(pe, "sqsum", hold=True)

            def query_lengths(m):
                pe.wait_ge(*done("hsq", 9 + m))
                for b in range(NB):
                    c = (b * 4 + m) * 2
                    last = mm(query_tile[:, c:c + 2], hsq[(9 + m) % 2][:, b * P:(b + 1) * P], cst("two"), start=True, stop=True)
                last.then_inc(*(fill("sqsum") if m == 3 else signal("sqsum_step", m)))

            for m in range(4):
                project(("sq", m), f"sq{m // 2}", P * (m % 2), P, hx, T, release=m % 2 == 1)
                if m >= 2:
                    query_lengths(m - 2)
            ada(8)
            for m in range(4):
                project(("gz", m), f"gz{m // 2}", P * (m % 2), P, hx, T, release=m % 2 == 1)
                if m < 2:
                    query_lengths(2 + m)
                if m == 1:
                    let_go("sqsum")
                    for turned, (r0, r1, src) in enumerate(((0, 40, glog), (32, 72, grow))):
                        o = open_tile(pe, "cols", turned)
                        if turned == 0:
                            pe.wait_ge(*done("grows"))
                        for n in range(NC):
                            for h in range(2):
                                last = mm(o[h * HD:(h + 1) * HD, n * 64:n * 64 + 40], src[0:r1, n * CH:(n + 1) * CH],
                                          ident[0:r1, r0:r1], start=True, stop=True)
                        last.then_inc(*fill("cols", turned))
            ada(9)
            o = open_tile(pe, "vs")
            pe.wait_ge(*copied("sv"))
            for b in range(NB):
                last = tr(o[:, b * P:(b + 1) * P], sv[:, b * P:(b + 1) * P], ident)
            last.then_inc(*fill("vs"))


            def sw_scores(u):
                b, hp = SWU[u]
                k0, wk = (0, WIN) if b == 0 else ((b - 1) * WIN, 2 * WIN)
                if u == 0:
                    pe.wait_ge(*done("kpad"))
                o = open_tile(pe, "ss", u)
                for p in range(2):
                    last = mm(o[:, p * wk:(p + 1) * wk], sq[:, hp, b * WIN:(b + 1) * WIN],
                              kpad[:, hp // 2, p, k0:k0 + wk], start=True, stop=True)
                last.then_inc(*fill("ss", u))

            def sw_turn(u):
                b, hp = SWU[u]
                nk = 1 if b == 0 else 2
                o = open_tile(pe, "st", u)
                pe.wait_ge(*done("sprob", u))
                for c in range(2 * nk):
                    last = tr(o[:, c * WIN:(c + 1) * WIN], pr[u % 2][:, c * WIN:(c + 1) * WIN], ident)
                last.then_inc(*fill("st", u))

            def sw_values(u):
                b, hp = SWU[u]
                nk = 1 if b == 0 else 2
                if hp == 0:
                    sw_out[0] = open_tile(pe, "so", b, hold=True)
                o = sw_out[0]
                pe.wait_ge(*copied("st", u))
                g = hp // 2
                for p in range(2):
                    for kb in range(nk):
                        last = mm(o[p * HD:(p + 1) * HD, hp * WIN:(hp + 1) * WIN],
                                  vs[:, b - nk + 1 + kb, g * HD:(g + 1) * HD],
                                  prT[u % 2][:, (p * nk + kb) * WIN:(p * nk + kb + 1) * WIN],
                                  start=kb == 0, stop=kb == nk - 1)
                if hp == 3:
                    last.then_inc(*fill("so", b))
                else:
                    last.then_inc(*signal("so_step", u))

            sw_out = [None]

            def window(j, point):
                u = 6 * j + point
                if 0 <= u - 3 < len(SWU):
                    sw_turn(u - 3)
                if 0 <= u - 4 < len(SWU):
                    sw_values(u - 4)
                if u < len(SWU):
                    sw_scores(u)
                if 0 <= u - 5 < len(SWU) and SWU[u - 5][1] == 3:
                    let_go("so", SWU[u - 5][0])

            def head_sums(j):
                o = open_tile(pe, "osum", j)
                pe.wait_ge(*done("osq", j))
                for b in range(NB):
                    last = mm(o[:, 2 * b:2 * b + 2], hsq[j % 2][:, b * P:(b + 1) * P], cst("two"), start=True, stop=True)
                last.then_inc(*fill("osum", j))

            def head_spread(j):
                o = open_tile(pe, "ospread", j)
                pe.wait_ge(*done("oexp", j))
                for b in range(NB):
                    last = mm(o[:, b * P:(b + 1) * P], row_buf[j % 2][:, b * P:(b + 1) * P], ident, start=True, stop=True)
                last.then_inc(*fill("ospread", j))

            def gate_rows(j, s):
                r0, src = ((0, glog), (32, glog), (0, grow))[s]
                o = open_tile(pe, "rows", j, s)
                selj = cst("sel", 40)[r0:r0 + 8, j * P:(j + 1) * P]
                mm(o[:, :], selj, src[r0:r0 + 8, :], start=True, stop=True).then_inc(*fill("rows", j, s))

            for s in range(3):
                gate_rows(0, s)
            for j in range(NJ):

                def squares(name, left, right, waits=()):
                    for half in range(2):
                        o = open_tile(pe, name, j, half)
                        for w in waits:
                            pe.wait_ge(*w(half))
                        for n in range(4):
                            nn = 4 * half + n
                            last = mm(o[:, n * P:(n + 1) * P], left[:, nn, :], right[:, nn, :], start=True, stop=True)
                        last.then_inc(*fill(name, j, half))

                def turns(name, src, waits=()):
                    for half in range(2):
                        o = open_tile(pe, name, j, half)
                        for w in waits:
                            pe.wait_ge(*w(half))
                        for n in range(4):
                            last = tr(o[:, n * P:(n + 1) * P], src[:, 4 * half + n, :], ident)
                        last.then_inc(*fill(name, j, half))

                def of(name):
                    return lambda half: copied(name, j, half)

                squares("kk", block_diag[0], block_diag[0], [lambda half: done("kbd", j)])
                o = open_tile(pe, "kq", j)
                for n in range(NC):
                    last = mm(o[:, n * CH:(n + 1) * CH], block_diag[0][:, n, :],
                              qkv[:, j, n * CH:(n + 1) * CH], start=True, stop=True)
                last.then_inc(*fill("kq", j))
                if j:
                    head_sums(j - 1)
                turns("tA", block_diag[2], [of("kk")])
                window(j, 0)
                squares("d2", block_diag[3], block_diag[5],
                        [lambda half: done("dT", j), lambda half: done("tA_part", j, half, 0)])
                window(j, 1)
                turns("d2T", block_diag[8], [of("d2")])
                squares("p1", block_diag[8], block_diag[4], [lambda half: done("p0", j)])
                squares("d4", block_diag[9], block_diag[8], [of("d2T")])
                turns("kt", block_diag[0])
                turns("vt", block_diag[1], [lambda half: done("vbd", j)])
                turns("d4T", block_diag[2], [of("d4")])
                squares("p2", block_diag[2], block_diag[4], [of("p1")])
                squares("d8", block_diag[3], block_diag[2], [of("d4T")])
                window(j, 2)
                if j:
                    head_spread(j - 1)
                squares("p3", block_diag[5], block_diag[4], [of("d8"), of("p2")])
                turns("t16", block_diag[4], [of("p3")])
                squares("z1", block_diag[6], block_diag[4], [of("tA")])
                window(j, 3)
                squares("i32", block_diag[2], block_diag[3], [of("t16"), of("z1")])
                turns("t32", block_diag[4], [of("i32")])
                squares("z2", block_diag[7], block_diag[4])
                squares("i64", block_diag[5], block_diag[3], [of("t32"), of("z2")])
                squares("wT", block_diag[8], block_diag[4], [of("kt"), of("i64")])
                oo = open_tile(pe, "go", j, hold=True)
                for n in range(NC):
                    if n in (2, 5):
                        window(j, 4 + n // 3)
                    if n in (1, 3, 6) and j < NJ - 1:
                        gate_rows(j + 1, n // 3)
                    o = open_tile(pe, "vn", j, n)
                    if n == 0:
                        pe.wait_ge(*copied("wT", j, 1))
                        pe.wait_ge(*copied("vt", j, 1))
                        pe.wait_ge(*done("qe", j))
                        pe.wait_ge(*copied("kq", j))
                    last = mm(o[:, 0:P], block_diag[4][:, n, :], block_diag[1][:, n, :], start=True, stop=n == 0)
                    if n > 0:
                        pe.wait_ge(*copied("su", j, n - 1))
                        last = mm(o[:, 0:P], block_diag[6][:, n, :], state, start=False, stop=True)
                    last.then_inc(*fill("vn", j, n))
                    if n > 0:
                        mm(oo[:, n * CH:(n + 1) * CH], state, qe[j % 2][:, n, :], start=True, stop=False)
                    pe.wait_ge(*copied("vn", j, n))
                    if n < NC - 1:
                        o = open_tile(pe, "su", j, n)
                        mm(o[:, 0:P], block_diag[0][:, n, :], vnew[n % 2], start=True, stop=True).then_inc(*fill("su", j, n))
                    last = mm(oo[:, n * CH:(n + 1) * CH], vnew[n % 2], qkw[:, n, :], start=n == 0, stop=True)
                    last.then_inc(*(fill("go", j) if n == NC - 1 else signal("go_step", j, n)))
                let_go("go", j)
            head_sums(NJ - 1)
            head_spread(NJ - 1)

            first_tiles("out0", lambda k: done("mix", k), [(("mo", c), P * c, T, hx) for c in range(2)], MIX_ORDER)
            for m in range(2, KD):
                project(("mo", m), f"out{m // 2}", P * (m % 2), P, hx, T, release=m % 2 == 1)
            norm_stats("2")
            norm_spread("2", diag)
            for part, (c0, n) in enumerate(FFN_PARTS):
                for i in range(c0 // 2, (c0 + n) // 2):
                    for name, key in (("g", "fg"), ("u", "fu")):
                        if i == 0 and name == "g":
                            first_tiles("g0", h_ready("2"), [(("fg", c), P * c, T, hx) for c in range(2)])
                            continue
                        for c in range(2):
                            project((key, 2 * i + c), f"{name}{i}", P * c, P, hx, T, release=c == 1)
                    if i == 4:
                        ada(10)
                    if i == 5:
                        ada(11)
                act_of = lambda s, k: act_split[:, s, k, :]
                first_tiles(f"down{part}0", lambda k: done("a", c0 + k), [(("fd", part, 0), 0, T, act_of)], range(n))
                for m in range(1, KD):
                    project(("fd", part, m), f"down{part}{m}", 0, P, act_of, T, release=True)
            norm_stats("3")
            norm_spread("3", diag)

            pe.wait_ge(*done("h3meta"))
            half_of = [slice(0, TM // 2), slice(TM // 2, TM)]
            hall = [lambda s, k: h_split[:, s, k, half_of[0]], lambda s, k: h_split[:, s, k, half_of[1]]]

            def project_all(key, name, c0, m, release=False):
                for half in range(2):
                    project(key + (half,), name, c0, m, hall[half], TM // 2, release and half == 1)

            def project_real(key, name, m0=0):
                for c in range(2):
                    project((key, m0 + c), name, P * c, P, hx, T, release=c == 1)

            def project_pair(key, name):
                for m in range(2):
                    project_all((key, m), name, P * m, P, release=m == 1)

            first_tiles("cug", h_ready("3"), [(("cgate", m, half), P * m, TM // 2, hall[half])
                                              for m in range(2) for half in range(2)])
            project_pair("cu", "cu")
            project_pair("pv", "pv")
            project_real("pg", "pg")
            project_real("cg", "cg")
            for m in range(2):
                o = open_tile(pe, "py", m)
                pe.wait_ge(*done("pool", m))
                mm(o[:, :], poolw[:, P * m:P * m + P], pool_sum[m][:, META:TM], start=True, stop=True).then_inc(*fill("py", m))
            project_real("bg", "bg")
            project_pair("cgx", "cgx")
            project_pair("xv", "xv")
            project_real("sg", "sg")
            project_real("cq", "cq")

            def conf_stats(tag, src):
                o = open_tile(pe, tag)
                for m in range(2):
                    pe.wait_ge(*done(tag + "_in", m))
                    last = mm(o[:, :], ones, src[:, m, :], start=m == 0, stop=m == 1)
                last.then_inc(*fill(tag))

            project_real("mg", "mg0")
            o = open_tile(pe, "cqsum")
            for b in range(4):
                for k in range(2):
                    if b == 0:
                        pe.wait_ge(*done("cqsq", k))
                    last = mm(o[:, b:b + 1], qsw[:, k, b * P:(b + 1) * P], ones[:, 0:1], start=k == 0, stop=k == 1)
            last.then_inc(*fill("cqsum"))
            conf_stats("cmean", conf_sum)
            project_all(("ckv",), "ckr", 0, P)
            conf_stats("cvar", conf_sq)
            project_all(("kr",), "ckr", 64, P, release=True)
            for half in range(2):
                o = open_tile(pe, "kvsum", half)
                pe.wait_ge(*done("ckvsq"))
                mm(o[:, 0:TM // 2], ones, ksq[:, half * (TM // 2):(half + 1) * (TM // 2)], start=True, stop=True)\
                    .then_inc(*fill("kvsum", half))
            project_real("mg", "mg1", 2)

            pe.wait_ge(*loaded("uq"))
            pe.wait_ge(*done("cqg", 1))
            for h in range(8):
                o = open_tile(pe, "q", h)
                for k in range(2):
                    last = mm(o[0:QD, :], W("uq")[:, k, h * QD:(h + 1) * QD], cq[:, k, :], start=k == 0, stop=k == 1)
                last.then_inc(*fill("q", h))
            last_tile_of["uq"] = ("q", 7)
            pe.wait_ge(*loaded("ukv"))
            pe.wait_ge(*done("ckvn"))
            wkv = W("ukv")[:, 0, :].rearrange("p (h d) -> p h d", h=8)
            for h in range(8):
                for half in range(2):
                    o = open_tile(pe, "k", h, half)
                    mm(o[0:HD, 0:TM // 2], wkv[:, h, 0:HD], ckv[:, half * (TM // 2):(half + 1) * (TM // 2)],
                       start=True, stop=True).then_inc(*fill("k", h, half))
            for b in range(5):
                n = P if b < 4 else META
                o = open_tile(pe, "v", b)
                mm(o[0:n, :], ckv[:, b * P:b * P + n], wkv[:, :, HD:2 * HD], start=True, stop=True)\
                    .then_inc(*fill("v", b))
            last_tile_of["ukv"] = ("v", 4)

            def ml_scores(u):
                i, h = MLU[u]
                n = keys_of[i]
                if i == 0:
                    pe.wait_ge(*done("qrope", h // 2))
                o = open_tile(pe, "ms", u)
                m0 = min(n, 512)
                mm(o[:, 0:m0], q_mla[0:QD, h, i * WIN:(i + 1) * WIN], k_mla[0:QD, h, 0:m0], start=True, stop=True)\
                    .then_inc(*fill("ms", u))
                if n > 512:
                    o = open_tile(pe, "ms2", u)
                    mm(o[:, 0:n - 512], q_mla[0:QD, h, i * WIN:(i + 1) * WIN], k_mla[0:QD, h, 512:n],
                       start=True, stop=True).then_inc(*fill("ms2", u))

            def ml_turn(u):
                i, h = MLU[u]
                o = open_tile(pe, "mt", u)
                pe.wait_ge(*done("mprob", u))
                for c in range(i + 1):
                    last = tr(o[:, c * WIN:(c + 1) * WIN], mpr[u % 2][:, c * WIN:(c + 1) * WIN], ident)
                last.then_inc(*fill("mt", u))
                o = open_tile(pe, "mr", u)
                tr(o[0:META, 0:WIN], mpr[u % 2][:, (i + 1) * WIN:(i + 1) * WIN + META], ident)\
                    .then_inc(*fill("mr", u))

            ml_out = [None]

            def ml_values(u):
                i, h = MLU[u]
                if h == 0:
                    ml_out[0] = open_tile(pe, "mo2", i, hold=True)
                o = ml_out[0]
                p, pair = h % 2, h // 2
                pe.wait_ge(*copied("mt", u))
                for c in range(i + 1):
                    mm(o[p * HD:(p + 1) * HD, pair * WIN:(pair + 1) * WIN], v_mla[:, c, h * HD:(h + 1) * HD],
                       mpT[u % 2][:, c * WIN:(c + 1) * WIN], start=c == 0, stop=False)
                pe.wait_ge(*copied("mr", u))
                last = mm(o[p * HD:(p + 1) * HD, pair * WIN:(pair + 1) * WIN], v_mla[:, i + 1, h * HD:(h + 1) * HD],
                          mpR[u % 2], start=False, stop=True)
                last.then_inc(*(fill("mo2", i) if h == 7 else signal("mo_step", u)))
                if h == 7:
                    let_go("mo2", i)

            pe.wait_ge(*done("krope"))
            pe.wait_ge(*copied("k", 7, 1))
            pe.wait_ge(*copied("v", 4))
            pe.wait_ge(*done("vpad"))
            def y_tile(m, b):
                name, k0, kb, nk = y_place(m, b)
                o = open_tile(pe, "y", m, b)
                pe.wait_ge(*loaded(name))
                for k in range(nk):
                    last = mm(o[:, :], W(name)[:, k0 + k, :], ybr[:, kb + k, :], start=k == 0, stop=k == nk - 1)
                last.then_inc(*fill("y", m, b))
                last_tile_of[name] = ("y", m, b)

            early = [None]

            def mix_quarter(x):
                i, q = x // 4, x % 4
                if i and q == 1:
                    let_go("gl", *MIX_EARLY[i - 1])
                if i and q == 0 and MIX_EARLY[i - 1][1] != 1:
                    if i == 1:
                        for k in range(2):
                            pe.wait_ge(*copied("py", k))
                            pe.wait_ge(*done("yc", k))
                            pe.wait_ge(*done("yd", k))
                    y_tile(*MIX_EARLY[i - 1])
                if i >= len(MIX_EARLY):
                    return
                m, b = MIX_EARLY[i]
                name = f"gl{m}{b // 2}"
                if q == 0:
                    early[0] = open_tile(pe, "gl", m, b, hold=True)
                    pe.wait_ge(*done("w_lo", name))
                hi, lo = split_of(name)
                for k in (2 * q, 2 * q + 1):
                    for x, (w, s) in enumerate(((hi, 0), (hi, 1), (lo, 0))):
                        last = mm(early[0][:, :], w[:, k, P * (b % 2):P * (b % 2) + P], hx(s, k), start=k + x == 0,
                                  stop=k == KD - 1 and x == 2)
                if q == 3:
                    last.then_inc(*fill("gl", m, b))
                    if b % 2:
                        last_tile_of[name] = ("gl", m, b)

            for u in range(len(MLU) + 2):
                if u < len(MLU):
                    ml_scores(u)
                if u >= 2:
                    ml_turn(u - 2)
                for x in range(4)[2 * u:2 * u + 2] if u < 2 else (u + 2,):
                    mix_quarter(x)
                if u >= 2:
                    ml_values(u - 2)

            for b in range(NB):
                pe.wait_ge(*copied("mo2", b))
            y_tile(0, 1)
            y_tile(1, 1)
            for m in range(2, KD):
                for b in range(4):
                    project(("gl", m, b), f"gl{m}{b // 2}", P * (b % 2), P, hx, T, release=b % 2 == 1)
                    y_tile(m, b)
            for b in range(4):
                for half in range(2):
                    o = open_tile(pe, "xt", b, half)
                    for c in range(4):
                        last = tr(o[:, c * P:(c + 1) * P], xT[:, 4 * half + c, b * P:(b + 1) * P], ident)
                    last.then_inc(*fill("xt", b, half))
            for k in range(KD):
                pe.wait_ge(*done("m", k))
            for half in range(2):
                fo = [open_tile(pe, "fo", b, half, hold=True) for b in range(4)]
                for kp in range(2):
                    pe.wait_ge(*done("w_lo", f"wo{half}{kp}"))
                    hi, lo = split_of(f"wo{half}{kp}")
                    for b in range(4):
                        for k in range(4):
                            for i, (s, w) in enumerate(((0, hi), (0, lo), (1, hi))):
                                last = mm(fo[b][:, :], mix_split[:, s, 4 * kp + k, b * P:(b + 1) * P], w[:, k, :],
                                          start=kp + k + i == 0, stop=kp == 1 and k == 3 and i == 2)
                        last.then_inc(*(fill("fo", b, half) if kp else signal("fo_part", half, b)))
                    last_tile_of[f"wo{half}{kp}"] = ("fo", 3, half)

        @block.sync
        def _(sp):
            for i, (name, kn, width, parts) in enumerate(panels):
                if i >= NS:
                    before = panels[i - NS][0]
                    if before[:4] == "ada3":
                        sp.wait_ge(*(filled("adar", 3) if before[-1] == "1" else done("adarow_half", 3)))
                    elif before.startswith("ada"):
                        sp.wait_ge(*done("adaacc" if before[-1] == "1" else "adapart", int(before[3:-1])))
                    elif before in splits:
                        sp.wait_ge(*done("w_lo", before))
                    else:
                        sp.wait_ge(*filled(*last_tile_of[before]))
                if name == "qkv1":
                    sp.dma_start(consts[:, CONST_FIRST:], a["consts"][:, CONST_FIRST:]).then_inc(sem("ld_const_rest"), 16)
                dst = W(name)
                if parts is None:
                    k0 = 0
                    for wname, nk in (branch_w[b] for b in branches_of[name[:2]]):
                        sp.dma_start(dst[:, k0:k0 + nk, :], w_cols(a[wname][0], P * int(name[2:]), P))\
                            .then_inc(sem(f"loaded{i % NS}"), 16)
                        k0 += nk
                else:
                    for c0, n, src in parts:
                        sp.dma_start(dst[:, :, c0:c0 + n], src).then_inc(sem(f"loaded{i % NS}"), 16)
            for b in range(4):
                sp.wait_ge(*done("fin_left", b))
                sp.wait_ge(*done("fin_right", b))
                sp.dma_start(out[0].rearrange("(b p) f -> b p f", p=P)[b], fin[b]).then_inc(sem("stored"), 16)
            sp.wait_ge(sem("stored"), 16 * 4)

        @block.gpsimd
        def _(pool):
            vec = [("b_ada", a["b_ada"][0], 48), ("norm1", a["norm1_w"][0], 8), ("norm2", a["norm2_w"][0], 8),
                   ("pre", a["pre_norm_g_2"][0], 8), ("gate_bias", a["gate_bias_2"][0], 32),
                   ("conf_b", a["conf_dw_b_2"][0], 2), ("ln_g", a["conf_ln_g_2"][0], 2),
                   ("ln_b", a["conf_ln_b_2"][0], 2), ("pool_scale", a["pool_scale_2"][0], 2),
                   ("q_norm", a["q_norm_g_2"][0], 2), ("kv_norm", a["kv_norm_g_2"][0], 1)]
            for name, src, n in vec:
                r = V1_ROWS[name]
                pool.dma_start(rows1[r:r + n, :], src.rearrange("(r p) -> r p", p=P)).then_inc(sem("ld_rows"), 16)
            for name, src in (("gdn_norm", a["gdn_norm_w"]), ("qn", a["q_norm_w"]), ("kn", a["k_norm_w"])):
                r = V1_ROWS[name]
                for h in range(2):
                    pool.dma_start(rows1[r:r + 1, h * HD:(h + 1) * HD], src).then_inc(sem("ld_rows"), 16)
            pool.dma_start(rows2[0:48, :], a["conv_w"][0, :, 0, :].rearrange("k (m p) -> (k m) p", p=P))\
                .then_inc(sem("ld_rows"), 16)
            pool.dma_start(rows2[48:110, :], a["conf_dw_w_2"][0].rearrange("k (m p) -> (k m) p", p=P))\
                .then_inc(sem("ld_rows"), 16)
            pool.dma_start(rows2[110:116, :], a["sc_dw_w_2"][0].rearrange("k (m p) -> (k m) p", p=P))\
                .then_inc(sem("ld_rows"), 16)
            pool.dma_start(nega[0:8, :], a["a_log"][0].rearrange("(h o) -> h o", o=1)).then_inc(sem("ld_gate"), 16)
            pool.dma_start(dtb[0:8, :], a["dt_bias"][0].rearrange("(h o) -> h o", o=1)).then_inc(sem("ld_gate"), 16)
            pool.dma_start(sinks, a["sinks"].broadcast_to([P, 8])).then_inc(sem("ld_gate"), 16)
            nc.gpsimd.memset(poolw[:, :], 0.0).then_inc(*signal("poolw0"))
            pool.wait_ge(*done("poolw0"))
            for g in range(4):
                r, c = (g % 2) * HD, (g // 2) * P + (g % 2) * HD
                pool.dma_start(poolw[r:r + HD, c:c + HD], a["pool_w_2"][0, g]).then_inc(sem("ld_poolw"), 16)
            pool.wait_ge(*filled("gz", 3))
            pool.dma_start(alibi, a["alibi"]).then_inc(sem("ld_alibi"), 16)
            nc.gpsimd.memset(kpad, 0.0).then_inc(*signal("kpad0"))
            def window(j, point):
                u = 6 * j + point - 2
                if not 0 <= u < len(SWU):
                    return
                b, hp = SWU[u]
                wk = WIN if b == 0 else 2 * WIN
                pool.wait_ge(*done("srec", u))
                v = pr[u % 2][:, 0:2 * wk].rearrange("p (h k) -> p h k", h=2)
                nc.gpsimd.tensor_tensor(v, v, sden[:, 2 * (u % 8):2 * (u % 8) + 2].unsqueeze(2).broadcast_to([P, 2, wk]),
                                        ALU.mult).then_inc(*signal("sprob", u))

            eye8 = ident.unsqueeze(1).broadcast_to([P, NC, P])
            m16T = cst("m16T").unsqueeze(1).broadcast_to([P, NC, P])
            for j in range(NJ):
                pool.wait_ge(*copied("kk", j, 0))
                pool.wait_ge(*copied("kk", j, 1))
                nc.gpsimd.tensor_tensor(block_diag[3], block_diag[2], m16T, ALU.mult).then_inc(*signal("dT", j))
                window(j, 0)
                pool.wait_ge(*done("dT", j))
                nc.gpsimd.tensor_tensor(block_diag[4], eye8, block_diag[3], ALU.subtract).then_inc(*signal("p0", j))
                for point in range(1, 6):
                    window(j, point)

            def square_sum(tag):
                for m in range(1, KD - 1):
                    pool.wait_ge(*done("xsq" + tag, m))
                    if m > 1:
                        pool.wait_ge(*done("sqsum" + tag, m - 1))
                    nc.gpsimd.tensor_tensor(sacc, sacc, hsq[m % 2], ALU.add).then_inc(*signal("sqsum" + tag, m))

            square_sum("2")
            square_sum("3")
            pool.wait_ge(*filled("fd", 1, 7))
            pool.dma_start(rope[HD:QD, :, :], a["rope"].rearrange("r (s t) -> r s t", s=2)).then_inc(sem("ld_rope"), 16)
            half = QK_ROPE // 2
            pool.wait_ge(*copied("kr", 0))
            pool.wait_ge(*copied("kr", 1))
            for d0, s0 in ((HD, HD + half), (HD + half, HD)):
                pool.dma_start(krs[d0:d0 + half, :], kr[s0:s0 + half, :]).then_inc(sem("ld_krs"), 16)
            for g in range(4):
                for h in (2 * g, 2 * g + 1):
                    pool.wait_ge(*copied("q", h))
                if g >= 2:
                    pool.wait_ge(*done("qrope", g - 2))
                for d0, s0 in ((HD, HD + half), (HD + half, HD)):
                    pool.dma_start(qsw2[g % 2][d0:d0 + half, :, :], q_mla[s0:s0 + half, 2 * g:2 * g + 2, :])\
                        .then_inc(sem(f"ld_qsw{g % 2}"), 16)
            for u, (i, h) in enumerate(MLU):
                n = keys_of[i]
                pool.wait_ge(*done("mrec", u))
                v = mpr[u % 2][:, 0:n]
                nc.gpsimd.tensor_tensor(v, v, sden[:, u % 16:u % 16 + 1].broadcast_to([P, n]), ALU.mult)\
                    .then_inc(*signal("mprob", u))
            pool.wait_ge(*done("m", 0))
            pool.dma_start(post[:, :], a["post_norm_g_2"].broadcast_to([P, D])).then_inc(sem("ld_post"), 16)
            for b in range(4):
                pool.wait_ge(*copied("xt", b, 0))
                pool.wait_ge(*copied("fo", b, 0))
                f = fin[b][:, 0:512]
                nc.gpsimd.tensor_tensor(f, f, xtok[:, b, 0:512], ALU.add).then_inc(*signal("fin_left", b))

        @block.scalar
        def _(act):
            A = nc.scalar.activation
            with nc.allow_non_contiguous_dma(reason="c, one float at a time"):
                act.dma_start(cs, a["c"][0].rearrange("(k p) -> p k", p=P)).then_inc(sem("ld_c"), 16)
            act.dma_start(consts[:, 0:CONST_FIRST], a["consts"][:, 0:CONST_FIRST]).then_inc(sem("ld_const"), 16)
            act.dma_start(x_in, a["x"][0].rearrange("(b p) f -> p b f", p=P)).then_inc(sem("ld_x"), 16)
            act.dma_start(meta_in[0:META, :], a["meta_tokens_2"]).then_inc(sem("ld_x"), 16)
            act.wait_ge(*arrived("c"))
            A(cs, cs, ACT.Silu).then_inc(*signal("cs"))
            act.wait_ge(*arrived("x", 2))
            for b in range(4):
                A(hpre[:, 0:2, :], x_in[:, b, :].rearrange("p (k t) -> p k t", k=2), ACT.Square,
                  accum_out=ssum[:, b:b + 1]).then_inc(*signal("xss", b))
                act.wait_ge(*done("xss", b))
            A(hpre[0:META, 0:2, :], meta_in[0:META, :].rearrange("p (k t) -> p k t", k=2), ACT.Square,
              accum_out=msum[0:META, 0:1]).then_inc(*signal("mss"))
            act.wait_ge(*done("eps"))
            act.wait_ge(*done("mss"))
            A(sroot, ssum, ACT.Sqrt, bias=epsc, scale=1.0 / D).then_inc(*signal("root1"))
            A(msum[0:META, 0:1], msum[0:META, 0:1], ACT.Sqrt, bias=epsc[0:META, :], scale=1.0 / D)\
                .then_inc(*signal("rootmeta"))
            for k in range(KD):
                act.wait_ge(*filled("x", k))
                A(xT[:, k, :], bank("x", k)[:, :], ACT.Copy).then_inc(*read("x", k))
            act.wait_ge(*filled("meta"))
            A(hmeta, bank("meta")[:, 0:8 * META], ACT.Copy).then_inc(*read("meta"))

            def root(tag, out, key, scale, bias):
                act.wait_ge(*filled(*key))
                A(out, bank(*key)[0:out.shape[0], 0:out.shape[1]], ACT.Sqrt, bias=bias, scale=scale).then_inc(*read(*key))

            act.wait_ge(*filled("vec"))
            A(V1[:, :], bank("vec")[:, 0:V1_N], ACT.Copy).then_inc(*signal("v1"))
            A(V2[:, :], bank("vec")[:, P:P + V2_N], ACT.Copy).then_inc(*read("vec"))
            split_hi = splitter(act, lambda hi, src: A(hi, src, ACT.Copy), None)

            def hi_part(stage, index, dst, src):
                A(dst, src, ACT.Copy).then_inc(*signal(stage + "_hi", *index))

            def modulate(tag, scale, shift):
                for k in range(KD + 1):
                    if k < KD:
                        act.wait_ge(*done("xn" + tag, k))
                        A(hpre[:, k, :], hpre[:, k, :], ACT.Identity, scale=scale[:, k:k + 1],
                          bias=modT[:, shift + k:shift + k + 1]).then_inc(*signal("mod" + tag, k))
                    if k:
                        act.wait_ge(*done("mod" + tag, k - 1))
                        hi_part("h" + tag, (k - 1,), h_split[:, 0, k - 1, real], hpre[:, k - 1, :])

            split_hi()
            act.wait_ge(*filled("adar", 3))
            A(row_buf[1][0:1, :], bank("adar", 3)[0:1, :], ACT.Copy).then_inc(*read("adar", 3))
            act.wait_ge(*done("modA1"))
            modulate("1", modA1, 0)
            split_hi()
            def conv_in(m):
                act.wait_ge(*filled("pj", m))
                if m >= 3:
                    act.wait_ge(*done("conv", m - 3, 3))
                A(raw[m % 3][:, 3:], bank("pj", m)[:, :], ACT.Copy).then_inc(*read("pj", m))

            def conv_out(m):
                act.wait_ge(*done("conv", m, 3))
                A(qkv[:, m, :], qkv[:, m, :], ACT.Silu).then_inc(*signal("silu", m))

            act.wait_ge(*done("rawpad"))
            def head_square(m):
                if m >= 2:
                    act.wait_ge(*done("hsum_step", m - 2))
                act.wait_ge(*done("silu", m))
                A(hsq[m % 2], qkv[:, m, :], ACT.Square).then_inc(*signal("hsq", m))

            for m in range(14):
                if m < 12:
                    conv_in(m)
                    if m % 2:
                        split_hi()
                if m >= 2:
                    conv_out(m - 2)
                if 3 <= m < 11:
                    head_square(m - 3)
            act.wait_ge(*filled("ab"))
            A(gate_tmp[3][0:40, :], bank("ab")[0:40, :], ACT.Copy).then_inc(*read("ab"))
            act.wait_ge(*filled("hsum"))
            A(row_buf[0][0:40, :], bank("hsum")[0:40, :], ACT.Sqrt, bias=epsc[0:40, :]).then_inc(*read("hsum"))
            act.wait_ge(*filled("sk"))
            A(sk, bank("sk")[:, :], ACT.Copy).then_inc(*read("sk"))
            act.wait_ge(*copied("sk"))
            A(hsq[0], sk, ACT.Square).then_inc(*signal("hsq", 8))
            split_hi()
            act.wait_ge(*filled("sv"))
            A(sv, bank("sv")[:, :], ACT.Copy).then_inc(*read("sv"))
            split_hi()
            act.wait_ge(*filled("sksum"))
            A(row_buf[1], bank("sksum")[:, :], ACT.Sqrt, bias=epsc, scale=1.0 / HD).then_inc(*read("sksum"))
            act.wait_ge(*copied("ab"))
            A(gate_tmp[0][32:40, :], gate_tmp[3][32:40, :], ACT.Exp, scale=-1.0).then_inc(*signal("egb"))
            act.wait_ge(*arrived("gate", 3))
            A(nega[0:8, :], nega[0:8, :], ACT.Exp).then_inc(*signal("ealog"))
            act.wait_ge(*done("nabs"))
            A(gate_tmp[2][0:8, :], gate_tmp[2][0:8, :], ACT.Exp).then_inc(*signal("eabs"))
            act.wait_ge(*done("eabs"))
            A(gate_tmp[2][0:8, :], gate_tmp[2][0:8, :], ACT.Ln, bias=1.0).then_inc(*signal("lnabs"))
            for m in range(4):
                act.wait_ge(*filled("sq", m))
                A(sq[:, m, :], bank("sq", m)[:, :], ACT.Copy).then_inc(*read("sq", m))
                if m >= 2:
                    act.wait_ge(*done("sqsum_step", m - 2))
                act.wait_ge(*copied("sq", m))
                A(hsq[(9 + m) % 2], sq[:, m, :], ACT.Square).then_inc(*signal("hsq", 9 + m))
                if m % 2:
                    split_hi()
            for m in range(4):
                act.wait_ge(*filled("gz", m))
                A(gz[:, m, :], bank("gz", m)[:, :], ACT.Silu).then_inc(*read("gz", m))
                if m == 1:
                    act.wait_ge(*filled("sqsum"))
                    A(rq, bank("sqsum")[:, 0:32], ACT.Sqrt, bias=eps64).then_inc(*read("sqsum"))
                    colv = cols.rearrange("p (n s j) -> p n s j", n=NC, s=4)
                    for turned in range(2):
                        act.wait_ge(*filled("cols", turned))
                        cps = bank("cols", turned)[:, :].rearrange("p (n s j h) -> p h s n j", n=NC, s=2, h=2)
                        for h in range(2):
                            rows = slice(h * HD, (h + 1) * HD)
                            for s2 in range(2):
                                last = A(colv[rows, :, 2 * turned + s2, :], cps[rows, h, s2, :, 0:NJ], ACT.Copy)
                                last.then_inc(*(read("cols", turned) if h and s2 else signal("cols_part")))
            act.wait_ge(*filled("vs"))
            A(vs, bank("vs")[:, :].rearrange("p (b d) -> p b d", b=NB), ACT.Copy).then_inc(*read("vs"))
            def sw_exp(u):
                b, hp = SWU[u]
                wk = WIN if b == 0 else 2 * WIN
                act.wait_ge(*done("snmax", u))
                if u >= 2:
                    act.wait_ge(*filled("st", u - 2))
                s2 = 2 * (u % 8)
                for p in range(2):
                    A(pr[u % 2][:, p * wk:(p + 1) * wk], sc[u % 2][:, p * wk:(p + 1) * wk], ACT.Exp,
                      bias=snmax[:, s2 + p:s2 + p + 1], accum_out=ssumx[:, s2 + p:s2 + p + 1])\
                        .then_inc(*signal("sexp", u, p))
                A(sesk[:, s2:s2 + 2], sesk[:, s2:s2 + 2], ACT.Exp).then_inc(*signal("sesk", u))

            def sw_copy(u):
                b, hp = SWU[u]
                n = 2 * WIN if b == 0 else 4 * WIN
                act.wait_ge(*filled("st", u))
                if u >= 2:
                    b2, hp2 = SWU[u - 2]
                    act.wait_ge(*(filled("so", b2) if hp2 == 3 else done("so_step", u - 2)))
                A(prT[u % 2][:, 0:n], bank("st", u)[:, 0:n], ACT.Copy).then_inc(*read("st", u))

            def sw_result(u):
                b, hp = SWU[u]
                if hp == 3:
                    act.wait_ge(*filled("so", b))
                    A(sq[:, :, b * WIN:(b + 1) * WIN], bank("so", b)[:, :].rearrange("p (h t) -> p h t", h=4),
                      ACT.Copy).then_inc(*read("so", b))

            def window(j, point):
                u = 6 * j + point
                if 0 <= u - 3 < len(SWU):
                    sw_copy(u - 3)
                if 0 <= u - 4 < len(SWU):
                    sw_result(u - 4)
                if 0 <= u - 1 < len(SWU):
                    sw_exp(u - 1)
                if u in (20, 21):
                    split_hi()

            v4 = lambda t: t.rearrange("p (n c) -> p n c", n=4)

            def head_root(j):
                act.wait_ge(*filled("osum", j))
                A(fss, bank("osum", j)[:, 0:8], ACT.Sqrt, bias=epsc, scale=1.0 / HD).then_inc(*read("osum", j))

            def diagonal(j, which):
                dst, m, stage = ((block_diag[0], 4 + j, "kbd"), (block_diag[1], 8 + j, "vbd"))[which]
                for h in range(2):
                    rows = slice(h * HD, (h + 1) * HD)
                    A(dst[rows, :, h * HD:(h + 1) * HD], qkv[rows, m, :].rearrange("p (n c) -> p n c", n=NC), ACT.Copy)\
                        .then_inc(*(signal(stage, j) if h else signal("bd_part")))

            def decays(j, part):
                if part == 0:
                    act.wait_ge(*filled("rows", j, 0))
                    A(g_row, bank("rows", j, 0)[:, :].rearrange("p (n c) -> p n c", n=NC), ACT.Copy)\
                        .then_inc(*read("rows", j, 0))
                if part == 1:
                    act.wait_ge(*done("emin", j))
                    A(e_, e_, ACT.Exp).then_inc(*signal("e", j))
                    act.wait_ge(*copied("rows", j, 0))
                    A(gx, g_row, ACT.Exp).then_inc(*signal("gx", j))
                if part == 2:
                    A(cA, colv[:, :, 0, j], ACT.Exp).then_inc(*signal("cAexp", j))
                    A(eglast[j % 2], g_row[:, :, CH - 1], ACT.Exp).then_inc(*signal("eglast", j))
                    act.wait_ge(*done("cBarg", j))
                    A(cB, cB, ACT.Exp).then_inc(*signal("cBexp", j))

            for j in range(NJ):
                if j == 0:
                    act.wait_ge(*done("bdzero"))
                    diagonal(0, 0)
                    diagonal(0, 1)
                if j == 0:
                    for part in range(3):
                        decays(0, part)
                    act.wait_ge(*done("skn"))
                    act.wait_ge(*done("kpad0"))
                    for g in range(2):
                        for p in range(2):
                            last = A(kpad[p * HD:(p + 1) * HD, g, p, :], sk[g * HD:(g + 1) * HD, :], ACT.Copy)
                            last.then_inc(*(signal("kpad") if g and p else signal("kpad_part")))

                def move(name, dst, scale=1.0, waits=()):
                    for w in waits:
                        act.wait_ge(*w)
                    for half in range(2):
                        act.wait_ge(*filled(name, j, half))
                        A(dst[:, 4 * half:4 * half + 4, :], v4(bank(name, j, half)[:, :]), ACT.Copy, scale=scale)\
                            .then_inc(*read(name, j, half))

                if j:
                    head_root(j - 1)
                window(j, 0)
                move("d2", block_diag[8])
                move("d2T", block_diag[9])
                window(j, 1)
                move("d4", block_diag[2], waits=[done("p0", j)])
                move("d4T", block_diag[3])
                move("d8", block_diag[5])
                window(j, 2)
                move("t16", block_diag[2])
                move("z1", block_diag[3])
                window(j, 3)
                move("t32", block_diag[5])
                move("z2", block_diag[3])
                move("wT", block_diag[6], scale=-1.0)
                for n in range(NC):
                    if n in (2, 5):
                        window(j, 4 + n // 3)
                    if n in (1, 3, 4) and j < NJ - 1:
                        decays(j + 1, n // 2)
                    act.wait_ge(*filled("vn", j, n))
                    A(vnew[n % 2], bank("vn", j, n)[:, 0:P], ACT.Copy).then_inc(*read("vn", j, n))
                if j < NJ - 1:
                    diagonal(j + 1, 0)
                act.wait_ge(*filled("go", j))
                A(hsq[j % 2], bank("go", j)[:, :], ACT.Square).then_inc(*signal("osq", j))
                A(qkv[:, j, :], bank("go", j)[:, :], ACT.Copy).then_inc(*read("go", j))
                if j < NJ - 1:
                    diagonal(j + 1, 1)
            for k in MIX_ORDER:
                if k == 5:
                    head_root(NJ - 1)
                if k < 4:
                    act.wait_ge(*done("mixg", k))
                else:
                    act.wait_ge(*copied("so", NB - 1))
                hi_part("mix", (k,), h_split[:, 0, k, real], qkv[:, k, :] if k < 4 else sq[:, k - 4, :])

            def load_sqrt():
                act.wait_ge(*done("eps"))
                A(warm, epsc, ACT.Sqrt)

            def square_of(tag, m):
                if m == KD - 2:
                    load_sqrt()
                if m >= 3:
                    act.wait_ge(*done("sqsum" + tag, m - 2))
                A(hsq[m % 2] if m else sacc, xT[:, m, :], ACT.Square).then_inc(*signal("xsq" + tag, m))

            for m in range(KD):
                act.wait_ge(*copied("mo", m))
                square_of("2", m)
                if m in (1, 3, 5):
                    split_hi()
            root("2", sroot, ("sum2",), 1.0 / D, epsc)
            act.wait_ge(*done("modA2"))
            modulate("2", modA2, 24)
            split_hi()
            for part, (c0, n) in enumerate(FFN_PARTS):
                for i in range(c0 // 2, (c0 + n) // 2):
                    for k in (2 * i, 2 * i + 1):
                        act.wait_ge(*filled("fg", k))
                        if k >= 2:
                            act.wait_ge(*done("a", k - 2))
                        A(silug[k % 2], bank("fg", k)[:, :], ACT.Silu).then_inc(*read("fg", k))
                    split_hi()
                    for k in (2 * i, 2 * i + 1):
                        act.wait_ge(*copied("fu", k))
                        hi_part("a", (k,), act_split[:, 0, k - c0, :], silug[k % 2])
                    split_hi()
                for m in range(KD):
                    act.wait_ge(*copied("fd", part, m))
                    if part:
                        square_of("3", m)
                    if not part or m < KD - 1:
                        split_hi()
            root("3", sroot, ("sum3",), 1.0 / D, epsc)
            act.wait_ge(*filled("fu", KF - 1))
            A(h_split[:, 0, :, 0:META], hmeta.rearrange("p (k t) -> p k t", k=KD), ACT.Copy).then_inc(*signal("meta_hi"))
            for k in range(KD):
                act.wait_ge(*done("xn3", k))
                hi_part("h3", (k,), h_split[:, 0, k, real], hpre[:, k, :])
            split_hi()

            H2 = TM // 2

            def both(key, dst, func=ACT.Copy):
                for half in range(2):
                    act.wait_ge(*filled(*key, half))
                    A(dst[:, half * H2:(half + 1) * H2], bank(*key, half)[:, 0:H2], func).then_inc(*read(*key, half))

            for m in range(2):
                both(("cgate", m), conf_gate[m], ACT.Sigmoid)
            split_hi()
            split_hi()
            for m in range(2):
                both(("pv", m), pv[m])
            split_hi()
            for m in range(2):
                act.wait_ge(*filled("pg", m))
                A(pg[:, m, :], bank("pg", m)[:, :], ACT.Silu).then_inc(*read("pg", m))
            split_hi()
            for m in range(2):
                act.wait_ge(*filled("cg", m))
                A(ybr[:, 6 + m, :], bank("cg", m)[:, :], ACT.Silu).then_inc(*read("cg", m))
            split_hi()
            for m in range(2):
                act.wait_ge(*filled("bg", m))
                A(bg[:, m, :], bank("bg", m)[:, :], ACT.Copy).then_inc(*read("bg", m))
            split_hi()
            for m in range(2):
                both(("cgx", m), cgx[m])
            split_hi()
            split_hi()
            for m in range(2):
                act.wait_ge(*filled("sg", m))
                A(ybr[:, 8 + m, :], bank("sg", m)[:, :], ACT.Silu).then_inc(*read("sg", m))
            split_hi()
            for m in range(2):
                act.wait_ge(*filled("cq", m))
                A(cq[:, m, :], bank("cq", m)[:, :], ACT.Copy).then_inc(*read("cq", m))
            for k in range(2):
                act.wait_ge(*copied("cq", k))
                A(qsw[:, k, :], cq[:, k, :], ACT.Square).then_inc(*signal("cqsq", k))
            split_hi()

            def mla_gate(m):
                act.wait_ge(*filled("mg", m))
                A(ybr[:, 2 + m, :], bank("mg", m)[:, :], ACT.Silu).then_inc(*read("mg", m))

            mla_gate(0)
            mla_gate(1)
            split_hi()
            act.wait_ge(*filled("cqsum"))
            A(rqm, bank("cqsum")[:, 0:4], ACT.Sqrt, scale=float(QD) / 256, bias=eps96).then_inc(*read("cqsum"))
            act.wait_ge(*filled("cmean"))
            A(conf_stats_[:, 0, :], bank("cmean")[:, :], ACT.Copy, scale=1.0 / 256).then_inc(*read("cmean"))
            for m in range(2):
                act.wait_ge(*done("ccen", m))
                A(conf_sq[:, m, :], conf_sum[:, m, :], ACT.Square).then_inc(*signal("cvar_in", m))
            both(("ckv",), ckv)
            act.wait_ge(*copied("ckv", 1))
            A(ksq, ckv, ACT.Square).then_inc(*signal("ckvsq"))
            act.wait_ge(*filled("cvar"))
            A(conf_stats_[:, 1, :], bank("cvar")[:, :], ACT.Sqrt, scale=1.0 / 256, bias=epsc).then_inc(*read("cvar"))
            for half in range(2):
                act.wait_ge(*filled("kr", half))
                A(kr[HD:QD, half * H2:(half + 1) * H2], bank("kr", half)[HD:QD, 0:H2], ACT.Copy).then_inc(*read("kr", half))
            split_hi()
            for half in range(2):
                act.wait_ge(*filled("kvsum", half))
                A(krb[:, half * H2:(half + 1) * H2], bank("kvsum", half)[:, 0:H2], ACT.Sqrt, scale=1.0 / P, bias=epsc)\
                    .then_inc(*read("kvsum", half))
            mla_gate(2)
            mla_gate(3)
            split_hi()
            for m in range(2):
                act.wait_ge(*done("cnorm", m))
                A(conf_sum[:, m, :], conf_sum[:, m, :], ACT.Silu, scale=V1[:, V1_ROWS["ln_g"] + m:V1_ROWS["ln_g"] + m + 1],
                  bias=V1[:, V1_ROWS["ln_b"] + m:V1_ROWS["ln_b"] + m + 1]).then_inc(*signal("csilu", m))
            for k in range(2):
                act.wait_ge(*copied("py", k))
                act.wait_ge(*done("yc", k))
                act.wait_ge(*done("yd", k))
            for h in range(8):
                act.wait_ge(*filled("q", h))
                A(q_mla[0:QD, h, :], bank("q", h)[0:QD, :], ACT.Copy).then_inc(*read("q", h))
            for h in range(8):
                for half in range(2):
                    act.wait_ge(*filled("k", h, half))
                    A(k_mla[0:HD, h, half * H2:(half + 1) * H2], bank("k", h, half)[0:HD, 0:H2], ACT.Copy)\
                        .then_inc(*read("k", h, half))
            for b in range(5):
                n = P if b < 4 else META
                act.wait_ge(*filled("v", b))
                if b == 4:
                    act.wait_ge(*done("vpad"))
                A(v_mla[0:n, b, :], bank("v", b)[0:n, :], ACT.Copy).then_inc(*read("v", b))

            act.wait_ge(*done("rqm"))

            def ml_in(u):
                i, h = MLU[u]
                n = keys_of[i]
                m0 = min(n, 512)
                if u >= 2:
                    act.wait_ge(*done("mexp", u - 2))
                act.wait_ge(*filled("ms", u))
                A(msc[u % 2][:, 0:m0], bank("ms", u)[:, 0:m0], ACT.Copy, scale=rqm[:, i:i + 1]).then_inc(*read("ms", u))
                if n > 512:
                    act.wait_ge(*filled("ms2", u))
                    A(msc[u % 2][:, 512:n], bank("ms2", u)[:, 0:n - 512], ACT.Copy, scale=rqm[:, i:i + 1])\
                        .then_inc(*read("ms2", u))

            def ml_exp(u):
                i, h = MLU[u]
                n = keys_of[i]
                act.wait_ge(*done("mmax", u))
                if u >= 2:
                    act.wait_ge(*filled("mr", u - 2))
                c = u % 16
                A(mpr[u % 2][:, 0:n], msc[u % 2][:, 0:n], ACT.Exp, bias=snmax[:, c:c + 1], accum_out=ssumx[:, c:c + 1])\
                    .then_inc(*signal("mexp", u))

            def ml_copy(u):
                i, h = MLU[u]
                act.wait_ge(*filled("mt", u))
                if u >= 2:
                    i2, h2 = MLU[u - 2]
                    act.wait_ge(*(filled("mo2", i2) if h2 == 7 else done("mo_step", u - 2)))
                A(mpT[u % 2][:, 0:(i + 1) * WIN], bank("mt", u)[:, 0:(i + 1) * WIN], ACT.Copy).then_inc(*read("mt", u))
                act.wait_ge(*filled("mr", u))
                if u < 2:
                    act.wait_ge(*done("vpad"))
                A(mpR[u % 2][0:META, :], bank("mr", u)[0:META, 0:WIN], ACT.Copy).then_inc(*read("mr", u))

            def gate(dst, m, b):
                act.wait_ge(*filled("gl", m, b))
                c = V1_ROWS["gate_bias"] + 8 * b + m
                A(dst, bank("gl", m, b)[:, :], ACT.Sigmoid, bias=V1[:, c:c + 1]).then_inc(*read("gl", m, b))

            for u in range(len(MLU) + 2):
                if u < len(MLU):
                    ml_in(u)
                if 1 <= u <= len(MLU):
                    ml_exp(u - 1)
                if u >= 2:
                    ml_copy(u - 2)
                x = u + 2
                if x >= 4 and x % 4 == 0 and x <= 32:
                    m, b = MIX_EARLY[x // 4 - 1]
                    dst, before = early_gate(x // 4 - 1)
                    if before:
                        act.wait_ge(*(done("gadd", *before) if before[1] else copied("y", *before)))
                    gate(dst, m, b)
                if x in (8, 16, 24):
                    split_hi(0)
                if x in (9, 17, 25):
                    split_hi(1)
            split_hi()
            for m in range(2):
                act.wait_ge(*done("macc", m))
                hi_part("m", (m,), mix_split[:, 0, m, :], mix_sum_of(m))
            act.wait_ge(*done("gadd", 1, 3))

            for m in range(2, KD):
                for b in range(4):
                    x = 4 * m + b
                    if x >= 10:
                        act.wait_ge(*copied("y", (x - 2) // 4, (x - 2) % 4))
                    gate(sg[x % 2], m, b)
                    if b % 2:
                        split_hi()
                    if b == 0 and m > 2:
                        act.wait_ge(*done("macc", m - 1))
                        hi_part("m", (m - 1,), mix_split[:, 0, m - 1, :], mix_sum_of(m - 1))
            act.wait_ge(*done("macc", KD - 1))
            hi_part("m", (KD - 1,), mix_split[:, 0, KD - 1, :], mix_sum[(KD - 1) % 2])
            for b in range(4):
                for half in range(2):
                    act.wait_ge(*filled("xt", b, half))
                    A(xtok[:, b, half * 512:(half + 1) * 512], bank("xt", b, half)[:, :], ACT.Copy)\
                        .then_inc(*read("xt", b, half))
            split_hi()
            def final_square(b, half):
                if b or half:
                    act.wait_ge(*done("fss", *((b - 1, half) if b else (3, 0))))
                act.wait_ge(*filled("fo", b, half))
                A(fjunk, bank("fo", b, half)[:, :], ACT.Square, accum_out=fss[:, 2 * b + half:2 * b + half + 1])\
                    .then_inc(*signal("fss", b, half))

            for b in range(4):
                final_square(b, 0)
            split_hi()
            for b in range(4):
                final_square(b, 1)
                act.wait_ge(*done("ftot", b))
                A(frs[:, b:b + 1], fss[:, 2 * b:2 * b + 1], ACT.Sqrt, scale=1.0 / D, bias=epsc).then_inc(*signal("froot", b))

        @block.vector
        def _(dve):
            v = nc.vector
            chain = [0]

            def link(ins):
                chain[0] += 1
                ins.then_inc(sem("dve_chain"), 1)
                dve.wait_ge(sem("dve_chain"), chain[0])

            def col(name, i=0, n=1):
                r = V1_ROWS[name] + i
                return V1[:, r:r + n]

            tt, ts, stt = v.tensor_tensor, v.tensor_scalar, v.scalar_tensor_tensor

            link(v.memset(gates, 0.0))
            v.memset(epsc, EPS)
            v.memset(eps64, EPS * HD)
            v.memset(eps96, EPS * QD).then_inc(*signal("eps"))
            split_lo = splitter(dve, None, lambda lo, src, hi: tt(lo, src, hi, ALU.subtract))

            def lo_part(stage, index, dst, src, hi):
                dve.wait_ge(*done(stage + "_hi", *index))
                tt(dst, src, hi.bitcast(F32), ALU.subtract).then_inc(*signal(stage, *index))

            def spread(tag, dg):
                dve.wait_ge(*(done("root1") if tag == "1" else copied("sum" + tag)))
                link(v.reciprocal(srstd, sroot))
                for b in range(4):
                    last = ts(dg[:, b, :], ident, srstd[:, b:b + 1], None, ALU.mult)
                    last.then_inc(*(signal("diag" + tag) if b == 3 else signal("diag_part" + tag)))

            def ada_sum(i):
                if i >= 2:
                    dve.wait_ge(*filled("ada", i - 2 if i != 5 else 1))
                acc = adaacc[i % 2]
                for h in range(2):
                    dve.wait_ge(*loaded(f"ada{i}{h}"))
                    w = W(f"ada{i}{h}")
                    for k in range(4):
                        c = cs[:, 4 * h + k:4 * h + k + 1]
                        if h + k == 0:
                            link(ts(acc, w[:, 0, :], c, None, ALU.mult))
                            continue
                        last = stt(out=acc, in0=w[:, k, :], scalar=c, in1=acc, op0=ALU.mult, op1=ALU.add)
                        if k < 3:
                            link(last)
                    last.then_inc(*signal("adaacc" if h else "adapart", i))
                    if h == 0:
                        dve.wait_ge(*done("adapart", i))

            def ada_mod(i):
                dve.wait_ge(*filled("ada", i))
                tt(modT[:, 4 * i:4 * i + 4], bank("ada", i)[:, 0:4], col("b_ada", 4 * i, 4), ALU.add)\
                    .then_inc(*read("ada", i))

            def normed(tag, stage):
                dve.wait_ge(*filled("spread" + tag))
                for k in range(KD):
                    ins = tt(hpre[:, k, :], xT[:, k, :], bank("spread" + tag)[:, :], ALU.mult)
                    ins.then_inc(*signal(stage, k))
                dve.wait_ge(*done(stage, KD - 1))
                v.engine_nop().then_inc(*read("spread" + tag))

            def h_rest(tag, chunks=range(KD)):
                for k in chunks:
                    lo_part("h" + tag, (k,), h_split[:, 1, k, real], hpre[:, k, :], h_split[:, 0, k, real])

            AHEAD = 3

            def normed_and_rest(tag, weight=None):
                dve.wait_ge(*filled("spread" + tag))
                for k in range(KD + AHEAD):
                    if k < KD:
                        src = bank("spread" + tag)[:, :]
                        ins = (stt(out=hpre[:, k, :], in0=xT[:, k, :], scalar=col(weight, k), in1=src,
                                   op0=ALU.mult, op1=ALU.mult) if weight else
                               tt(hpre[:, k, :], xT[:, k, :], src, ALU.mult))
                        ins.then_inc(*signal("xn" + tag, k))
                    if k == KD - 1:
                        dve.wait_ge(*done("xn" + tag, KD - 1))
                        v.engine_nop().then_inc(*read("spread" + tag))
                    if k >= AHEAD:
                        h_rest(tag, [k - AHEAD])

            dve.wait_ge(*done("cs"))
            ada_sum(0)
            ada_sum(1)
            dve.wait_ge(*arrived("const"))
            spread("1", diag)
            dve.wait_ge(*done("rootmeta"))
            link(v.reciprocal(msum[0:META, 1:2], msum[0:META, 0:1]))
            ts(rbc[0:META, 0:META], ident[0:META, 0:META], msum[0:META, 1:2], None, ALU.mult)\
                .then_inc(*signal("diagmeta"))
            ada_sum(2)
            for k in range(KD):
                dve.wait_ge(*copied("x", k))
            normed("1", "xn1")
            dve.wait_ge(*done("v1"))
            ada_mod(0)
            ada_mod(1)
            split_lo()
            ada_mod(2)
            ada_mod(3)
            dve.wait_ge(*copied("ada", 3))
            stt(out=modA1, in0=modT[:, 8:16], scalar=1.0, in1=col("norm1", 0, 8), op0=ALU.add, op1=ALU.mult)\
                .then_inc(*signal("modA1"))
            h_rest("1")
            split_lo()
            dve.wait_ge(*copied("meta"))
            hm = hmeta.rearrange("p (k t) -> p k t", k=KD)
            dve.wait_ge(*filled("spreadmeta"))
            dve.wait_ge(*done("v1"))
            for k in range(KD):
                last = stt(out=hm[:, k, :], in0=hm[:, k, :], scalar=col("pre", k), in1=bank("spreadmeta")[:, 0:META],
                           op0=ALU.mult, op1=ALU.mult)
                last.then_inc(*(read("spreadmeta") if k == KD - 1 else signal("hmeta", k)))
            dve.wait_ge(*done("h1", KD - 1))
            for i in range(2):
                v.memset(raw[i][:, 0:3], 0.0)
            v.memset(raw[2][:, 0:3], 0.0).then_inc(*signal("rawpad"))

            def conv4(m):
                dve.wait_ge(*copied("pj", m))
                tap = lambda k: V2[:, 12 * k + m:12 * k + m + 1]
                ts(qkv[:, m, :], raw[m % 3][:, 0:T], tap(0), None, ALU.mult).then_inc(*signal("conv", m, 0))
                for k in range(1, 4):
                    dve.wait_ge(*done("conv", m, k - 1))
                    stt(out=qkv[:, m, :], in0=raw[m % 3][:, k:k + T], scalar=tap(k), in1=qkv[:, m, :],
                        op0=ALU.mult, op1=ALU.add).then_inc(*signal("conv", m, k))

            for m in range(12):
                conv4(m)
                if m % 2:
                    split_lo()
                    if m >= 5:
                        ada_mod(4 + (m - 5) // 2)
                    if m <= 7:
                        ada_sum(4 + (m - 1) // 2)
            ada_sum(8)
            dve.wait_ge(*copied("ab"))
            dve.wait_ge(*arrived("gate", 3))
            link(ts(gate_tmp[1][0:8, :], gate_tmp[3][0:8, :], dtb[0:8, :], None, ALU.add))
            stt(out=gate_tmp[2][0:8, :], in0=gate_tmp[1][0:8, :], scalar=-1.0, in1=gate_tmp[1][0:8, :], op0=ALU.mult, op1=ALU.min)\
                .then_inc(*signal("nabs"))
            dve.wait_ge(*copied("hsum"))
            link(v.reciprocal(grow[0:40, :], row_buf[0][0:40, :]))
            link(ts(grow[0:8, :], grow[0:8, :], float(HD) ** -0.5, None, ALU.mult))
            split_lo()
            split_lo()
            ada_sum(9)
            dve.wait_ge(*copied("sksum"))
            link(v.reciprocal(row_buf[1], row_buf[1]))
            link(tt(wqk, col("qn"), col("kn"), ALU.mult))
            dve.wait_ge(*copied("sk"))
            stt(out=sk, in0=sk, scalar=wqk, in1=row_buf[1], op0=ALU.mult, op1=ALU.mult).then_inc(*signal("skn"))
            dve.wait_ge(*done("egb"))
            link(ts(gate_tmp[0][32:40, :], gate_tmp[0][32:40, :], 1.0, None, ALU.add))
            link(v.reciprocal(gate_tmp[0][32:40, :], gate_tmp[0][32:40, :]))
            link(v.tensor_copy(grow[64:72, :], gate_tmp[0][32:40, :]))
            link(tt(glog[32:40, :], gate_tmp[0][32:40, :], grow[32:40, :], ALU.mult))
            dve.wait_ge(*done("lnabs"))
            dve.wait_ge(*done("ealog"))
            link(ts(gate_tmp[1][0:8, :], gate_tmp[1][0:8, :], 0.0, None, ALU.max))
            link(tt(gate_tmp[1][0:8, :], gate_tmp[1][0:8, :], gate_tmp[2][0:8, :], ALU.add))
            link(ts(gate_tmp[1][0:8, :], gate_tmp[1][0:8, :], nega[0:8, :], -1.0, ALU.mult, ALU.mult))
            v.tensor_tensor_scan(glog[0:8, :], cst("reset", 8), gate_tmp[1][0:8, :], 0.0, ALU.mult, ALU.add)\
                .then_inc(*signal("grows"))
            split_lo()
            split_lo()
            ada_mod(8)
            dve.wait_ge(*copied("sqsum"))
            link(v.reciprocal(rq, rq))
            ada_mod(9)
            dve.wait_ge(*copied("ada", 9))
            stt(out=modA2, in0=modT[:, 32:40], scalar=1.0, in1=col("norm2", 0, 8), op0=ALU.add, op1=ALU.mult)\
                .then_inc(*signal("modA2"))

            def sw_bias(u):
                b, hp = SWU[u]
                wk = WIN if b == 0 else 2 * WIN
                dve.wait_ge(*filled("ss", u))
                if u >= 2:
                    dve.wait_ge(*done("sexp", u - 2, 1))
                for p in range(2):
                    h = 2 * hp + p
                    al = alibi[:, h * 2 * WIN + (2 * WIN - wk):(h + 1) * 2 * WIN]
                    ins = stt(out=sc[u % 2][:, p * wk:(p + 1) * wk], in0=bank("ss", u)[:, p * wk:(p + 1) * wk],
                              scalar=rq[:, b * 8 + h:b * 8 + h + 1], in1=al, op0=ALU.mult, op1=ALU.add)
                    ins.then_inc(*(read("ss", u) if p else signal("sbias", u)))
                dve.wait_ge(*copied("ss", u))
                s2 = 2 * (u % 8)
                link(v.reduce_max(smax[:, s2:s2 + 2], sc[u % 2][:, 0:2 * wk].rearrange("p (h k) -> p h k", h=2), AX.X))
                link(tt(smax[:, s2:s2 + 2], smax[:, s2:s2 + 2], sinks[:, 2 * hp:2 * hp + 2], ALU.max))
                link(ts(snmax[:, s2:s2 + 2], smax[:, s2:s2 + 2], -1.0, None, ALU.mult))
                tt(sesk[:, s2:s2 + 2], sinks[:, 2 * hp:2 * hp + 2], snmax[:, s2:s2 + 2], ALU.add)\
                    .then_inc(*signal("snmax", u))

            def sw_sum(u):
                s2 = 2 * (u % 8)
                dve.wait_ge(*done("sexp", u, 1))
                dve.wait_ge(*done("sesk", u))
                link(tt(sden[:, s2:s2 + 2], ssumx[:, s2:s2 + 2], sesk[:, s2:s2 + 2], ALU.add))
                v.reciprocal(sden[:, s2:s2 + 2], sden[:, s2:s2 + 2]).then_inc(*signal("srec", u))

            def window(j, point):
                u = 6 * j + point
                if u == 0:
                    dve.wait_ge(*arrived("alibi"))
                if u < len(SWU):
                    sw_bias(u)
                if 0 <= u - 2 < len(SWU):
                    sw_sum(u - 2)
                if u in (20, 21):
                    split_lo()

            v4 = lambda t: t.rearrange("p (n c) -> p n c", n=4)
            v8 = lambda t: t.rearrange("p (n c) -> p n c", n=NC)
            over_c = lambda c: c.unsqueeze(2).broadcast_to([P, NC, CH])
            colv = cols.rearrange("p (n s j) -> p n s j", n=NC, s=4)
            mask64 = lambda name: cst(name).unsqueeze(1).broadcast_to([P, NC, CH])
            mask4 = lambda name: cst(name).unsqueeze(1).broadcast_to([P, 4, P])
            link(v.memset(block_diag[0], 0.0))
            v.memset(block_diag[1], 0.0).then_inc(*signal("bdzero"))
            dve.wait_ge(*copied("cols", 1))
            def head_expand(j):
                dve.wait_ge(*copied("osum", j))
                link(v.reciprocal(frs, fss))
                v.tensor_copy(row_buf[j % 2].rearrange("p (c d) -> p c d", d=HD), frs.unsqueeze(2).broadcast_to([P, 8, HD]))\
                    .then_inc(*signal("oexp", j))

            def head_scale(j):
                dve.wait_ge(*filled("ospread", j))
                stt(out=qkv[:, j, :], in0=qkv[:, j, :], scalar=col("gdn_norm"), in1=bank("ospread", j)[:, :],
                    op0=ALU.mult, op1=ALU.mult).then_inc(*read("ospread", j))

            def head_gate(j):
                dve.wait_ge(*copied("ospread", j))
                tt(qkv[:, j, :], qkv[:, j, :], gz[:, j, :], ALU.mult).then_inc(*signal("mixg", j))

            def decays(j, part):
                gcolj, _, rkj, _ = (colv[:, :, s, j] for s in range(4))
                if part == 0:
                    dve.wait_ge(*copied("rows", j, 0))
                    link(tt(e_, g_row, over_c(gcolj), ALU.subtract))
                    ts(e_, e_, 0.0, None, ALU.min).then_inc(*signal("emin", j))
                    tt(cB, g_row[:, :, CH - 1], gcolj, ALU.subtract).then_inc(*signal("cBarg", j))
                if part == 1:
                    dve.wait_ge(*done("e", j))
                    link(tt(e_, e_, over_c(rkj), ALU.mult))
                    dve.wait_ge(*filled("rows", j, 1))
                    tt(w1, e_, v8(bank("rows", j, 1)[:, :]), ALU.mult).then_inc(*read("rows", j, 1))
                    dve.wait_ge(*copied("rows", j, 1))
                    link(tt(w1, w1, mask64("strictT"), ALU.mult))
                if part == 2:
                    dve.wait_ge(*filled("rows", j, 2))
                    link(tt(w2, e_, v8(bank("rows", j, 2)[:, :]), ALU.mult))
                    link(tt(w2, w2, mask64("inclT"), ALU.mult))
                    dve.wait_ge(*done("gx", j))
                    tt(qe[j % 2], gx, v8(bank("rows", j, 2)[:, :]), ALU.mult).then_inc(*read("rows", j, 2))
                    dve.wait_ge(*copied("rows", j, 2))
                    tt(qe[j % 2], qe[j % 2], v8(qkv[:, j, :]), ALU.mult).then_inc(*signal("qe", j))

            for j in range(NJ):
                gcolj, brkj, rkj, betaj = (colv[:, :, s, j] for s in range(4))
                if j == 0:
                    for part in range(3):
                        decays(0, part)
                for half in range(2):
                    dve.wait_ge(*filled("kk", j, half))
                    w = w1[:, 4 * half:4 * half + 4, :].unsqueeze(2).broadcast_to([P, 4, 2, CH])
                    tt(block_diag[2][:, 4 * half:4 * half + 4, :].rearrange("p n (h c) -> p n h c", h=2),
                       bank("kk", j, half)[:, :].rearrange("p (n h c) -> p n h c", n=4, h=2), w, ALU.mult)\
                        .then_inc(*read("kk", j, half))
                dve.wait_ge(*filled("kq", j))
                tt(qkw, v8(bank("kq", j)[:, :]), w2, ALU.mult).then_inc(*read("kq", j))
                for i, (dst, name) in enumerate(((block_diag[5], "m16"), (block_diag[6], "m32"), (block_diag[7], "m64"))):
                    if i == 1:
                        window(j, 0)
                    for half in range(2):
                        dve.wait_ge(*filled("tA", j, half))
                        src = v4(bank("tA", j, half)[:, :])
                        ins = tt(dst[:, 4 * half:4 * half + 4, :], src, mask4(name), ALU.mult)
                        ins.then_inc(*(read("tA", j, half) if i == 2 else signal("tA_part", j, half, i)))

                def add(name, op=ALU.add):
                    for half in range(2):
                        dve.wait_ge(*filled(name, j, half))
                        d = block_diag[4][:, 4 * half:4 * half + 4, :]
                        tt(d, d, v4(bank(name, j, half)[:, :]), op).then_inc(*read(name, j, half))

                def scaled(name, parts):
                    for half in range(2):
                        dve.wait_ge(*filled(name, j, half))
                        src = v4(bank(name, j, half)[:, :])
                        for i, (dst, c) in enumerate(parts):
                            ins = tt(dst[:, 4 * half:4 * half + 4, :], src,
                                     c[:, 4 * half:4 * half + 4].unsqueeze(2).broadcast_to([P, 4, P]), ALU.mult)
                            ins.then_inc(*(read(name, j, half) if i == len(parts) - 1 else signal(name + "_part", j, half)))

                if j:
                    head_expand(j - 1)
                window(j, 1)
                dve.wait_ge(*done("p0", j))
                add("p1")
                dve.wait_ge(*done("cBexp", j))
                link(tt(cA, cA, brkj, ALU.mult))
                link(tt(cB, cB, rkj, ALU.mult))
                scaled("kt", ((block_diag[8], cA), (block_diag[0], cB)))
                scaled("vt", ((block_diag[1], betaj),))
                add("p2")
                add("p3")
                window(j, 2)
                if j:
                    head_scale(j - 1)
                add("i32", ALU.subtract)
                window(j, 3)
                add("i64", ALU.subtract)
                dve.wait_ge(*done("eglast", j))
                for n in range(NC - 1):
                    if n in (2, 5):
                        window(j, 4 + n // 3)
                    if n == 6 and j:
                        head_gate(j - 1)
                    if n in (1, 3) and j < NJ - 1:
                        decays(j + 1, n // 2)
                    dve.wait_ge(*filled("su", j, n))
                    ps = bank("su", j, n)[:, 0:P]
                    if n == 0:
                        v.tensor_copy(state, ps).then_inc(*read("su", j, n))
                    else:
                        dve.wait_ge(*copied("su", j, n - 1))
                        stt(out=state, in0=state, scalar=eglast[j % 2][:, n:n + 1], in1=ps, op0=ALU.mult, op1=ALU.add)\
                            .then_inc(*read("su", j, n))
                if j < NJ - 1:
                    decays(j + 1, 2)
            for k in MIX_ORDER:
                if k == 5:
                    head_expand(NJ - 1)
                if k == 7:
                    head_scale(NJ - 1)
                    head_gate(NJ - 1)
                lo_part("mix", (k,), h_split[:, 1, k, real], qkv[:, k, :] if k < 4 else sq[:, k - 4, :], h_split[:, 0, k, real])

            def residual(key, m, gate):
                dve.wait_ge(*filled(*key))
                stt(out=xT[:, m, :], in0=bank(*key)[:, :], scalar=modT[:, gate + m:gate + m + 1], in1=xT[:, m, :],
                    op0=ALU.mult, op1=ALU.add).then_inc(*read(*key))

            for m in range(KD):
                residual(("mo", m), m, 16)
                if m in (1, 3, 5):
                    split_lo()
            spread("2", diag)
            normed_and_rest("2")
            split_lo()
            for part, (c0, n) in enumerate(FFN_PARTS):
                for i in range(c0 // 2, (c0 + n) // 2):
                    split_lo()
                    if i in (1, 3):
                        ada_sum(10 + i // 2)
                    for k in (2 * i, 2 * i + 1):
                        dve.wait_ge(*copied("fg", k))
                        dve.wait_ge(*filled("fu", k))
                        tt(silug[k % 2], bank("fu", k)[:, :], silug[k % 2], ALU.mult).then_inc(*read("fu", k))
                    for k in (2 * i, 2 * i + 1):
                        lo_part("a", (k,), act_split[:, 1, k - c0, :], silug[k % 2], act_split[:, 0, k - c0, :])
                    split_lo()
                    if i == 5:
                        ada_mod(10)
                        ada_mod(11)
                        dve.wait_ge(*copied("ada", 11))
                for m in range(KD):
                    residual(("fd", part, m), m, 40)
                    if not part or m < KD - 1:
                        split_lo()
            spread("3", diag)
            dve.wait_ge(*done("meta_hi"))
            tt(h_split[:, 1, :, 0:META], hm, h_split[:, 0, :, 0:META].bitcast(F32), ALU.subtract).then_inc(*signal("h3meta"))
            normed_and_rest("3", "pre")
            split_lo()
            dve.wait_ge(*done("h3", KD - 1))

            H2 = TM // 2
            v.memset(conf_in[0][:, 0:30], 0.0)
            v.memset(conf_in[1][:, 0:30], 0.0)
            v.memset(short_in[0][:, 0:2], 0.0)
            link(v.memset(short_in[1][:, 0:2], 0.0))
            lo, hi = slice(0, HD), slice(HD, P)

            def shifted(dst, src, by, first, rows=slice(0, P)):
                link(tt(dst[rows, first:TM], src[rows, first:TM], src[rows, first - by:TM - by], ALU.add))

            def pooled(m, rows, src):
                return stt(out=pool_sum[m][rows, META:TM], in0=src[rows, META:TM],
                           scalar=cst("invw")[rows, m:m + 1], in1=pv[m][rows, META:TM], op0=ALU.mult, op1=ALU.subtract)

            tap_at = [0]

            def taps(n):
                for k in range(tap_at[0], min(tap_at[0] + n, CONF_K)):
                    for m in range(2):
                        if k == 0:
                            dve.wait_ge(*copied("cu", m, 1))
                        else:
                            dve.wait_ge(*done("cconv", k - 1, m))
                        tap = V2[:, V2_ROWS["conf"] + 2 * k + m:V2_ROWS["conf"] + 2 * k + m + 1]
                        src = conf_in[m][:, META + k:META + k + T]
                        ins = (ts(conf_sum[:, m, :], src, tap, col("conf_b", m), ALU.mult, ALU.add) if k == 0 else
                               stt(out=conf_sum[:, m, :], in0=src, scalar=tap, in1=conf_sum[:, m, :], op0=ALU.mult, op1=ALU.add))
                        ins.then_inc(*(signal("cmean_in", m) if k == CONF_K - 1 else signal("cconv", k, m)))
                tap_at[0] += n

            split_lo()
            for m in range(2):
                for half in range(2):
                    dve.wait_ge(*copied("cgate", m, half))
                    dve.wait_ge(*filled("cu", m, half))
                    tt(conf_in[m][:, 30 + half * H2:30 + (half + 1) * H2], bank("cu", m, half)[:, 0:H2],
                       conf_gate[m][:, half * H2:(half + 1) * H2], ALU.mult).then_inc(*read("cu", m, half))
            split_lo()
            taps(3)
            for m in range(2):
                dve.wait_ge(*copied("pv", m, 1))
                shifted(pool_sum[m], pv[m], 1, 1)
                if m == 0:
                    shifted(pool_sum[2], pool_sum[0], 2, 3, hi)
                else:
                    shifted(pool_sum[2], pool_sum[1], 2, 3)
                    shifted(pool_sum[1], pool_sum[2], 4, 7)
                    shifted(pool_sum[2], pool_sum[1], 8, 15, hi)
                link(pooled(m, lo, pool_sum[m]))
                pooled(m, hi, pool_sum[2]).then_inc(*signal("pool", m))
                dve.wait_ge(*done("pool", m))
            split_lo()
            taps(4)
            split_lo()
            taps(4)
            split_lo()
            for m in range(2):
                dve.wait_ge(*filled("py", m))
                dve.wait_ge(*copied("pg", m))
                stt(out=ybr[:, m, :], in0=bank("py", m)[:, :], scalar=col("pool_scale", m), in1=pg[:, m, :],
                    op0=ALU.mult, op1=ALU.mult).then_inc(*read("py", m))
            taps(4)
            split_lo()
            taps(4)
            split_lo()
            for m in range(2):
                for half in range(2):
                    dve.wait_ge(*copied("cgx", m, half))
                    dve.wait_ge(*filled("xv", m, half))
                    tt(short_in[m][:, 2 + half * H2:2 + (half + 1) * H2], bank("xv", m, half)[:, 0:H2],
                       cgx[m][:, half * H2:(half + 1) * H2], ALU.mult).then_inc(*read("xv", m, half))
            split_lo()
            taps(4)
            for m in range(2):
                dve.wait_ge(*copied("xv", m, 1))
                acc = cgx[m][:, 0:T]
                for k in range(SC_K):
                    tap = V2[:, V2_ROWS["sc"] + 2 * k + m:V2_ROWS["sc"] + 2 * k + m + 1]
                    src = short_in[m][:, META + k:META + k + T]
                    link(ts(acc, src, tap, None, ALU.mult) if k == 0 else
                         stt(out=acc, in0=src, scalar=tap, in1=acc, op0=ALU.mult, op1=ALU.add))
                dve.wait_ge(*copied("bg", m))
                link(tt(acc, acc, bg[:, m, :], ALU.mult))
                dve.wait_ge(*copied("sg", m))
                tt(ybr[:, 8 + m, :], ybr[:, 8 + m, :], acc, ALU.mult).then_inc(*signal("yd", m))
            split_lo()
            taps(CONF_K)
            split_lo()
            split_lo()
            for k in range(2):
                dve.wait_ge(*done("cqsq", k))
                ts(cq[:, k, :], cq[:, k, :], col("q_norm", k), None, ALU.mult).then_inc(*signal("cqg", k))
            dve.wait_ge(*copied("cmean"))
            for m in range(2):
                tt(conf_sum[:, m, :], conf_sum[:, m, :], conf_stats_[:, 0, :], ALU.subtract).then_inc(*signal("ccen", m))
            split_lo()
            dve.wait_ge(*copied("cvar"))
            link(v.reciprocal(conf_stats_[:, 1, :], conf_stats_[:, 1, :]))
            for m in range(2):
                dve.wait_ge(*done("cvar_in", m))
                tt(conf_sum[:, m, :], conf_sum[:, m, :], conf_stats_[:, 1, :], ALU.mult).then_inc(*signal("cnorm", m))
            for m in range(2):
                dve.wait_ge(*done("csilu", m))
                tt(ybr[:, 6 + m, :], ybr[:, 6 + m, :], conf_sum[:, m, :], ALU.mult).then_inc(*signal("yc", m))
            split_lo()
            dve.wait_ge(*done("ckvsq"))
            for half in range(2):
                dve.wait_ge(*copied("kvsum", half))
            link(v.reciprocal(krb, krb))
            stt(out=ckv, in0=ckv, scalar=col("kv_norm"), in1=krb, op0=ALU.mult, op1=ALU.mult).then_inc(*signal("ckvn"))
            dve.wait_ge(*copied("cqsum"))
            v.reciprocal(rqm, rqm).then_inc(*signal("rqm"))
            for k in range(2):
                dve.wait_ge(*done("yc", k))
            v.memset(mpR[0], 0.0)
            v.memset(mpR[1], 0.0)
            v.memset(v_mla[:, 4, :], 0.0).then_inc(*signal("vpad"))
            r3 = slice(HD, QD)
            dve.wait_ge(*arrived("rope"))
            dve.wait_ge(*arrived("krs", 2))
            link(tt(kr[r3, :], kr[r3, :], rope[r3, 0, :], ALU.mult))
            link(tt(krs[r3, :], krs[r3, :], rope[r3, 1, :], ALU.mult))
            tt(k_mla[r3, :, :], kr[r3, :].unsqueeze(1).broadcast_to([QK_ROPE, 8, TM]),
               krs[r3, :].unsqueeze(1).broadcast_to([QK_ROPE, 8, TM]), ALU.add).then_inc(*signal("krope"))
            for g in range(4):
                q2 = q_mla[r3, 2 * g:2 * g + 2, :]
                dve.wait_ge(*arrived(f"qsw{g % 2}", 2 * (g // 2 + 1)))
                cs2 = [rope[r3, s, META:TM].unsqueeze(1).broadcast_to([QK_ROPE, 2, T]) for s in range(2)]
                link(tt(q2, q2, cs2[0], ALU.mult))
                qs = qsw2[g % 2][r3, :, :]
                link(tt(qs, qs, cs2[1], ALU.mult))
                tt(q2, q2, qs, ALU.add).then_inc(*signal("qrope", g))
                dve.wait_ge(*done("qrope", g))

            def ml_max(u):
                i, h = MLU[u]
                n = keys_of[i]
                dve.wait_ge(*copied("ms2" if n > 512 else "ms", u))
                s, c = msc[u % 2], u % 16
                link(tt(s[:, n - WIN:n], s[:, n - WIN:n], cst("causal"), ALU.add))
                link(v.reduce_max(smax[:, c:c + 1], s[:, 0:n], AX.X))
                ts(snmax[:, c:c + 1], smax[:, c:c + 1], -1.0, None, ALU.mult).then_inc(*signal("mmax", u))

            def ml_rec(u):
                i, h = MLU[u]
                c = u % 16
                dve.wait_ge(*done("mexp", u))
                v.reciprocal(sden[:, c:c + 1], ssumx[:, c:c + 1]).then_inc(*signal("mrec", u))

            for u in range(len(MLU) + 3):
                if u >= 3 and MLU[u - 3][1] == 7:
                    i = MLU[u - 3][0]
                    dve.wait_ge(*filled("mo2", i))
                    for pair in range(4):
                        dve.wait_ge(*copied("mg", pair))
                    y = ybr[:, 2:6, i * WIN:(i + 1) * WIN]
                    tt(y, bank("mo2", i)[:, :].rearrange("p (h t) -> p h t", h=4), y, ALU.mult)\
                        .then_inc(*read("mo2", i))
                if u < len(MLU):
                    ml_max(u)
                if 1 <= u <= len(MLU):
                    ml_rec(u - 1)
                x = u + 2
                if 4 < x <= 33 and x % 4 == 1:
                    m, b = MIX_EARLY[x // 4 - 1]
                    if b != 1:
                        gate_at, _ = early_gate(x // 4 - 1)
                        dve.wait_ge(*copied("gl", m, b))
                        dve.wait_ge(*filled("y", m, b))
                        tt(mix_sum_of(m) if b == 0 else gate_at, bank("y", m, b)[:, :], gate_at, ALU.mult).then_inc(*read("y", m, b))
                        if b:
                            dve.wait_ge(*copied("y", m, b))
                            tt(mix_sum_of(m), mix_sum_of(m), gate_at, ALU.add).then_inc(*signal("gadd", m, b))
                if x in (10, 18, 26):
                    split_lo(0)
                if x in (11, 19, 27):
                    split_lo(1)
            split_lo()
            for m in range(2):
                dve.wait_ge(*filled("y", m, 1))
                tt(prod[m], bank("y", m, 1)[:, :], mla_gate_buf[m], ALU.mult).then_inc(*read("y", m, 1))
                dve.wait_ge(*copied("y", m, 1))
                dve.wait_ge(*done("gadd", m, 3))
                tt(mix_sum_of(m), mix_sum_of(m), prod[m], ALU.add).then_inc(*signal("macc", m))
            for m in range(2):
                lo_part("m", (m,), mix_split[:, 1, m, :], mix_sum_of(m), mix_split[:, 0, m, :])
            for m in range(2, KD):
                for b in range(4):
                    x = 4 * m + b
                    dve.wait_ge(*copied("gl", m, b))
                    dve.wait_ge(*filled("y", m, b))
                    dst = mix_sum[m % 2] if b == 0 else prod[b % 2]
                    if b == 0 and m >= 4:
                        dve.wait_ge(*done("m", m - 2))
                    tt(dst, bank("y", m, b)[:, :], sg[x % 2], ALU.mult).then_inc(*read("y", m, b))
                    dve.wait_ge(*copied("y", m, b))
                    if b:
                        ins = tt(mix_sum[m % 2], mix_sum[m % 2], prod[b % 2], ALU.add)
                        if b < 3:
                            link(ins)
                        else:
                            ins.then_inc(*signal("macc", m))
                    elif m > 2:
                        lo_part("m", (m - 1,), mix_split[:, 1, m - 1, :], mix_sum[(m - 1) % 2], mix_split[:, 0, m - 1, :])
                    if b % 2:
                        split_lo()
            lo_part("m", (KD - 1,), mix_split[:, 1, KD - 1, :], mix_sum[(KD - 1) % 2], mix_split[:, 0, KD - 1, :])
            split_lo()
            split_lo()
            dve.wait_ge(*arrived("post"))
            for b in range(4):
                for half in range(2):
                    dve.wait_ge(*copied("xt", b, half))
                dve.wait_ge(*done("fss", b, 1))
                tt(fss[:, 2 * b:2 * b + 1], fss[:, 2 * b:2 * b + 1], fss[:, 2 * b + 1:2 * b + 2], ALU.add)\
                    .then_inc(*signal("ftot", b))
                dve.wait_ge(*done("froot", b))
                link(v.reciprocal(frs[:, 4 + b:5 + b], frs[:, b:b + 1]))
                for half in range(2):
                    c = slice(512 * half, 512 * half + 512)
                    f = fin[b][:, c]
                    stt(out=f, in0=bank("fo", b, half)[:, :], scalar=frs[:, 4 + b:5 + b], in1=post[:, c],
                        op0=ALU.mult, op1=ALU.mult).then_inc(*read("fo", b, half))
                    if half:
                        dve.wait_ge(*copied("fo", b, half))
                        tt(f, f, xtok[:, b, c], ALU.add).then_inc(*signal("fin_right", b))

    return counted


_INS = ["x", "c", "w_ada", "b_ada", "norm1_w", "w_in", "conv_w", "a_log", "dt_bias", "gdn_norm_w", "q_norm_w",
        "k_norm_w", "sinks", "w_out", "norm2_w", "w_gate", "w_up", "w_down", "meta_tokens_2", "pre_norm_g_2",
        "w_in_2", "gate_bias_2", "pool_w_2", "pool_scale_2", "w_out_pool_2", "q_norm_g_2", "w_uq_2", "kv_norm_g_2",
        "w_ukv_2", "w_out_mla_2", "conf_dw_w_2", "conf_dw_b_2", "conf_ln_g_2", "conf_ln_b_2", "w_out_conf_2",
        "sc_dw_w_2", "w_out_sc_2", "w_o_2", "post_norm_g_2"]


def kernel(**inputs):
    import concourse.bacc as _bacc
    from concourse.bass_utils import run_bass_kernel_spmd as _run

    consts, alibi, rope = shape_constants()
    arrays = {f"in_{name}_dram": np.ascontiguousarray(inputs[name]) for name in _INS}
    arrays |= {"in_consts_dram": consts, "in_alibi_dram": alibi, "in_rope_dram": rope}

    def build(known):
        nc = _bacc.Bacc("TRN2", target_bir_lowering=False, num_devices=1)
        aps = {n[3:-5]: nc.dram_tensor(n, v.shape, mybir.dt.from_np(v.dtype), kind="ExternalInput").ap()
               for n, v in arrays.items()}
        o = nc.dram_tensor("out_0_dram", (1, T, D), F32, kind="ExternalOutput").ap()
        return nc, program(nc, aps, o, known)

    nc, _ = build(build(None)[1])
    return _run(nc, [arrays], core_ids=[0]).results[0]["out_0_dram"]
```
